# Optimizing a Trainium2 kernel written in Bass

```python
import math
import jax, jax.numpy as jnp
from jax import lax
import numpy as np

D_MODEL = 1024
BATCH = 1
SEQ = 256
DEPTH = 4
DEC_BATCH = 8
DEC_SEQ = 4
PAST_LEN = 2048
PAGE_SIZE = 128

N_MIXERS = 3
N_RWKV = (DEPTH + 2) // 3
N_GDN = (DEPTH + 1) // 3
N_HGRN = DEPTH // 3
N_VRES = N_RWKV - 1

RWKV_N = 64
RWKV_H = D_MODEL // RWKV_N
DECAY_LORA = 64
AAA_LORA = 64
MV_LORA = 32
GATE_LORA = 128
RWKV_LNX_EPS = 64e-5

GDN_H = 8
GDN_DK = 128
GDN_DV = 128
GDN_CONV = 4
GDN_CHUNK = 64
GDN_QK = GDN_H * GDN_DK
GDN_VD = GDN_H * GDN_DV
GDN_CONV_DIM = 2 * GDN_QK + GDN_VD
GDN_IN = GDN_CONV_DIM + GDN_VD + 2 * GDN_H

HGRN_DK = 128
HGRN_H = D_MODEL // HGRN_DK
HGRN_DV = D_MODEL // HGRN_H
HGRN_CHUNK = 32
HGRN_FK = HGRN_H * HGRN_DK
HGRN_VD = HGRN_H * HGRN_DV
HGRN_IN = 2 * HGRN_FK + 2 * HGRN_VD

D_FF = 2816
FFN_CONV = 3

NORM_EPS = 1e-6
L2_EPS = 1e-6

kernel_name = 'hybrid_rwkv7_gdn_hgrn2_convffn_step'

def _rmsnorm(x, w):
    xf = x.astype(jnp.float32)
    y = xf * lax.rsqrt(jnp.mean(xf * xf, axis=-1, keepdims=True) + NORM_EPS)
    return (y * w.astype(jnp.float32)).astype(x.dtype)

def _l2norm(x):
    xf = x.astype(jnp.float32)
    return xf * lax.rsqrt(jnp.sum(xf * xf, axis=-1, keepdims=True) + L2_EPS)

def _causal_conv(x, hist, w):
    width, T = w.shape[0], x.shape[1]
    xp = jnp.concatenate([hist.astype(x.dtype), x], axis=1)
    y = sum(xp[:, j:j + T] * w[j] for j in range(width))
    return y, xp[:, xp.shape[1] - (width - 1):]

def _to_chunks(t, C):
    B, T = t.shape[0], t.shape[1]
    t = t.reshape((B, T // C, C) + t.shape[2:])
    return jnp.moveaxis(jnp.moveaxis(t, 1, 0), 2, 3)

def _from_chunks(o):
    n, B, H, C = o.shape[:4]
    o = jnp.moveaxis(jnp.moveaxis(o, 3, 2), 0, 1)
    return o.reshape((B, n * C, H) + o.shape[4:])

def _rwkv7_scan(r, w, k, v, kk, a, S0):
    def step(S, inp):
        r_t, w_t, k_t, v_t, kk_t, a_t = inp
        sa = jnp.einsum('bhvk,bhk->bhv', S, kk_t)
        S = (S * w_t[:, :, None, :] - sa[..., None] * (kk_t * a_t)[:, :, None, :]
             + v_t[..., None] * k_t[:, :, None, :])
        return S, jnp.einsum('bhvk,bhk->bhv', S, r_t)
    xs = tuple(jnp.moveaxis(t, 1, 0) for t in (r, w, k, v, kk, a))
    S, o = lax.scan(step, S0.astype(jnp.float32), xs)
    return jnp.moveaxis(o, 0, 1), S

def _gated_delta_chunked(q, k, v, g, beta, S0):
    T = q.shape[1]
    C = math.gcd(T, GDN_CHUNK)
    q, k, v, g, beta = (_to_chunks(t.astype(jnp.float32), C) for t in (q, k, v, g, beta))
    gc = jnp.cumsum(g, axis=-1)
    idx = jnp.arange(C)
    causal = idx[:, None] >= idx[None, :]
    strict = idx[:, None] > idx[None, :]
    decay = jnp.exp(jnp.where(causal, gc[..., :, None] - gc[..., None, :], -jnp.inf))
    kb = k * beta[..., None]
    L = jnp.where(strict, jnp.einsum('nbhik,nbhjk->nbhij', kb, k) * decay, 0.0)
    eye = jnp.eye(C, dtype=jnp.float32)
    Tinv = lax.linalg.triangular_solve(eye + L, jnp.broadcast_to(eye, L.shape),
                                       left_side=True, lower=True, unit_diagonal=True)
    u = Tinv @ (v * beta[..., None])
    wk = Tinv @ (kb * jnp.exp(gc)[..., None])
    qk = jnp.einsum('nbhik,nbhjk->nbhij', q, k) * decay
    qg = q * jnp.exp(gc)[..., None]
    g_last = gc[..., -1]
    kd = k * jnp.exp(g_last[..., None] - gc)[..., None]

    def step(S, inp):
        u_c, w_c, qk_c, qg_c, kd_c, gl_c = inp
        v_new = u_c - w_c @ S
        o = qg_c @ S + qk_c @ v_new
        S = S * jnp.exp(gl_c)[..., None, None] + jnp.einsum('bhck,bhcv->bhkv', kd_c, v_new)
        return S, o
    S, o = lax.scan(step, S0.astype(jnp.float32), (u, wk, qk, qg, kd, g_last))
    return _from_chunks(o), S

def _gla_chunked(q, k, v, logf, S0):
    T = q.shape[1]
    C = math.gcd(T, HGRN_CHUNK)
    q, k, v, logf = (_to_chunks(t.astype(jnp.float32), C) for t in (q, k, v, logf))
    gc = jnp.cumsum(logf, axis=3)
    idx = jnp.arange(C)
    causal = (idx[:, None] >= idx[None, :])[:, :, None]

    def step(S, inp):
        q_c, k_c, v_c, g_c = inp
        dec = jnp.exp(jnp.where(causal, g_c[..., :, None, :] - g_c[..., None, :, :], -jnp.inf))
        A = jnp.einsum('bhik,bhjk,bhijk->bhij', q_c, k_c, dec)
        o = (q_c * jnp.exp(g_c)) @ S + A @ v_c
        gl = g_c[..., -1, :]
        S = S * jnp.exp(gl)[..., None] + jnp.einsum('bhck,bhcv->bhkv', k_c * jnp.exp(gl[..., None, :] - g_c), v_c)
        return S, o
    S, o = lax.scan(step, S0.astype(jnp.float32), (q, k, v, gc))
    return _from_chunks(o), S

def _rwkv7_mixer(x, shift0, S0, v_first, P, j):
    B, T, D = x.shape
    hd = lambda t: t.reshape(B, T, RWKV_H, RWKV_N).astype(jnp.float32)
    prev = jnp.concatenate([shift0[:, None].astype(x.dtype), x[:, :-1]], axis=1)
    mixed = x[None] + (prev - x)[None] * P['rwkv_mix'][j][:, None, None, :]
    xr, xw, xk, xv, xa, xg = (mixed[s] for s in range(6))
    r, k, v = jnp.einsum('sbtd,sde->sbte', jnp.stack([xr, xk, xv]), P['rwkv_w_rkv'][j])
    w_log = -jax.nn.softplus(-(P['rwkv_w0'][j] + jnp.tanh(xw @ P['rwkv_w1'][j]) @ P['rwkv_w2'][j]).astype(jnp.float32)) - 0.5
    a = jax.nn.sigmoid(P['rwkv_a0'][j] + (xa @ P['rwkv_a1'][j]) @ P['rwkv_a2'][j])
    if v_first is None:
        v_first = v
    else:
        gate_v = jax.nn.sigmoid(P['rwkv_v0'][j - 1] + (xv @ P['rwkv_v1'][j - 1]) @ P['rwkv_v2'][j - 1])
        v = v + (v_first - v) * gate_v
    g = jax.nn.sigmoid(xg @ P['rwkv_g1'][j]) @ P['rwkv_g2'][j]
    kk = _l2norm(hd(k * P['rwkv_k_k'][j]))
    k = k * (1 + (a - 1) * P['rwkv_k_a'][j])
    decay = jnp.exp(-jnp.exp(w_log))
    o, S = _rwkv7_scan(hd(r), hd(decay), hd(k), hd(v), kk, hd(a), S0)
    mu = jnp.mean(o, -1, keepdims=True)
    var = jnp.mean(jnp.square(o - mu), -1, keepdims=True)
    o = ((o - mu) * lax.rsqrt(var + RWKV_LNX_EPS)).reshape(B, T, D) * P['rwkv_lnx_w'][j] + P['rwkv_lnx_b'][j]
    bonus = jnp.sum(hd(r) * hd(k) * P['rwkv_r_k'][j], -1, keepdims=True) * hd(v)
    out = ((o + bonus.reshape(B, T, D)) * g).astype(x.dtype) @ P['rwkv_w_o'][j]
    return out, x[:, -1], S.astype(S0.dtype), v_first

def _gdn_mixer(x, conv0, S0, P, j):
    B, T, _ = x.shape
    proj = x @ P['gdn_w_in'][j]
    qkv, conv_new = _causal_conv(proj[..., :GDN_CONV_DIM], conv0, P['gdn_conv_w'][j])
    qkv = jax.nn.silu(qkv)
    q = _l2norm(qkv[..., :GDN_QK].reshape(B, T, GDN_H, GDN_DK)) * GDN_DK ** -0.5
    k = _l2norm(qkv[..., GDN_QK:2 * GDN_QK].reshape(B, T, GDN_H, GDN_DK))
    v = qkv[..., 2 * GDN_QK:].reshape(B, T, GDN_H, GDN_DV).astype(jnp.float32)
    gate = proj[..., GDN_CONV_DIM:GDN_CONV_DIM + GDN_VD].reshape(B, T, GDN_H, GDN_DV).astype(jnp.float32)
    rest = proj[..., GDN_CONV_DIM + GDN_VD:].astype(jnp.float32)
    beta = jax.nn.sigmoid(rest[..., :GDN_H])
    g = -jnp.exp(P['gdn_a_log'][j].astype(jnp.float32)) * jax.nn.softplus(rest[..., GDN_H:] + P['gdn_dt_bias'][j])
    o, S = _gated_delta_chunked(q, k, v, g, beta, S0)
    o = _rmsnorm(o, P['gdn_norm_w'][j]) * jax.nn.silu(gate)
    out = o.reshape(B, T, GDN_VD).astype(x.dtype) @ P['gdn_w_o'][j]
    return out, conv_new, S.astype(S0.dtype)

def _hgrn2_mixer(x, S0, lb, P, j):
    B, T, _ = x.shape
    proj = (x @ P['hgrn_w_in'][j]).astype(jnp.float32)
    q = jax.nn.silu(proj[..., :HGRN_FK])
    f = lb + (1.0 - lb) * jax.nn.sigmoid(proj[..., HGRN_FK:2 * HGRN_FK])
    i_in = proj[..., 2 * HGRN_FK:2 * HGRN_FK + HGRN_VD]
    gate = proj[..., 2 * HGRN_FK + HGRN_VD:]
    hk = lambda t: t.reshape(B, T, HGRN_H, HGRN_DK)
    o, S = _gla_chunked(hk(q), hk(1.0 - f), i_in.reshape(B, T, HGRN_H, HGRN_DV), hk(jnp.log(f)), S0)
    o = _rmsnorm(o, P['hgrn_norm_w'][j]).reshape(B, T, HGRN_VD) * jax.nn.silu(gate)
    return o.astype(x.dtype) @ P['hgrn_w_o'][j], S.astype(S0.dtype)

def _conv_ffn(x, conv0, P, i):
    h, conv_new = _causal_conv(x @ P['ffn_w_up'][i], conv0, P['ffn_conv_w'][i])
    y = jax.nn.silu(h[..., D_FF:]) * h[..., :D_FF]
    return y @ P['ffn_w_down'][i], conv_new

def _trunk(x, shift0, wkv0, gconv0, gS0, hS0, fconv0, P):
    lb_soft = jax.nn.softmax(P['hgrn_lb'].astype(jnp.float32), axis=0)
    lb_layer = jnp.cumsum(lb_soft, axis=0) - lb_soft[0]
    v_first = None
    shift, wkv, gconv, gS, hS, fconv = [], [], [], [], [], []
    for i in range(DEPTH):
        kind, j = i % N_MIXERS, i // N_MIXERS
        h = _rmsnorm(x, P['norm_mix_pre'][i])
        if kind == 0:
            out, s_shift, s_wkv, v_first = _rwkv7_mixer(h, shift0[j], wkv0[j], v_first, P, j)
            shift.append(s_shift)
            wkv.append(s_wkv)
        elif kind == 1:
            out, c_new, s_new = _gdn_mixer(h, gconv0[j], gS0[j], P, j)
            gconv.append(c_new)
            gS.append(s_new)
        else:
            out, s_new = _hgrn2_mixer(h, hS0[j], lb_layer[i], P, j)
            hS.append(s_new)
        x = x + _rmsnorm(out, P['norm_mix_post'][i])
        out, c_new = _conv_ffn(_rmsnorm(x, P['norm_ffn_pre'][i]), fconv0[i], P, i)
        fconv.append(c_new)
        x = x + _rmsnorm(out, P['norm_ffn_post'][i])
    return x, (jnp.stack(shift), jnp.stack(wkv), jnp.stack(gconv), jnp.stack(gS), jnp.stack(hS), jnp.stack(fconv))

def setup_inputs(seed: int = 0) -> dict:
    keys = iter(jax.random.split(jax.random.key(seed), 64))

    def nrm(shape, scale):
        return jax.random.normal(next(keys), shape, jnp.float32) * scale

    def uni(shape, lo, hi):
        return jax.random.uniform(next(keys), shape, jnp.float32, lo, hi)

    def gain(shape):
        return 1.0 + nrm(shape, 0.05)

    D = D_MODEL
    dt = jnp.exp(uni((N_GDN, GDN_H), math.log(1e-3), math.log(1e-1)))
    return {
        'x_prompt': nrm((BATCH, SEQ, D), 1.0),
        'x_sample': nrm((DEC_BATCH, DEC_SEQ, D), 1.0),
        'state_rwkv_shift': nrm((N_RWKV, DEC_BATCH, D), 1.0),
        'state_rwkv_wkv': nrm((N_RWKV, DEC_BATCH, RWKV_H, RWKV_N, RWKV_N), 0.3),
        'state_gdn_conv': nrm((N_GDN, DEC_BATCH, GDN_CONV - 1, GDN_CONV_DIM), 1.0),
        'state_gdn_S': nrm((N_GDN, DEC_BATCH, GDN_H, GDN_DK, GDN_DV), 0.3),
        'state_hgrn_S': nrm((N_HGRN, DEC_BATCH, HGRN_H, HGRN_DK, HGRN_DV), 1.0),
        'state_ffn_conv': nrm((DEPTH, DEC_BATCH, FFN_CONV - 1, 2 * D_FF), 1.0),
        'norm_mix_pre': gain((DEPTH, D)),
        'norm_mix_post': gain((DEPTH, D)),
        'norm_ffn_pre': gain((DEPTH, D)),
        'norm_ffn_post': gain((DEPTH, D)),
        'rwkv_mix': uni((N_RWKV, 6, D), 0.0, 1.0),
        'rwkv_w_rkv': nrm((N_RWKV, 3, D, D), D ** -0.5),
        'rwkv_w0': -2.5 + nrm((N_RWKV, D), 0.5),
        'rwkv_w1': nrm((N_RWKV, D, DECAY_LORA), D ** -0.5),
        'rwkv_w2': nrm((N_RWKV, DECAY_LORA, D), 0.1 * DECAY_LORA ** -0.5),
        'rwkv_a0': nrm((N_RWKV, D), 0.1),
        'rwkv_a1': nrm((N_RWKV, D, AAA_LORA), D ** -0.5),
        'rwkv_a2': nrm((N_RWKV, AAA_LORA, D), 0.1 * AAA_LORA ** -0.5),
        'rwkv_v0': nrm((N_VRES, D), 0.1),
        'rwkv_v1': nrm((N_VRES, D, MV_LORA), D ** -0.5),
        'rwkv_v2': nrm((N_VRES, MV_LORA, D), 0.1 * MV_LORA ** -0.5),
        'rwkv_g1': nrm((N_RWKV, D, GATE_LORA), D ** -0.5),
        'rwkv_g2': nrm((N_RWKV, GATE_LORA, D), GATE_LORA ** -0.5),
        'rwkv_k_k': 0.85 + nrm((N_RWKV, D), 0.05),
        'rwkv_k_a': 1.0 + nrm((N_RWKV, D), 0.05),
        'rwkv_r_k': nrm((N_RWKV, RWKV_H, RWKV_N), 0.1),
        'rwkv_lnx_w': gain((N_RWKV, D)),
        'rwkv_lnx_b': nrm((N_RWKV, D), 0.02),
        'rwkv_w_o': nrm((N_RWKV, D, D), D ** -0.5),
        'gdn_w_in': nrm((N_GDN, D, GDN_IN), D ** -0.5),
        'gdn_conv_w': nrm((N_GDN, GDN_CONV, GDN_CONV_DIM), GDN_CONV ** -0.5),
        'gdn_a_log': jnp.log(uni((N_GDN, GDN_H), 1.0, 16.0)),
        'gdn_dt_bias': dt + jnp.log(-jnp.expm1(-dt)),
        'gdn_norm_w': gain((N_GDN, GDN_DV)),
        'gdn_w_o': nrm((N_GDN, GDN_VD, D), GDN_VD ** -0.5),
        'hgrn_w_in': nrm((N_HGRN, D, HGRN_IN), D ** -0.5),
        'hgrn_lb': nrm((DEPTH, HGRN_FK), 0.1),
        'hgrn_norm_w': gain((N_HGRN, HGRN_DV)),
        'hgrn_w_o': nrm((N_HGRN, HGRN_VD, D), HGRN_VD ** -0.5),
        'ffn_w_up': nrm((DEPTH, D, 2 * D_FF), D ** -0.5),
        'ffn_conv_w': nrm((DEPTH, FFN_CONV, 2 * D_FF), FFN_CONV ** -0.5),
        'ffn_w_down': nrm((DEPTH, D_FF, D), D_FF ** -0.5),
    }

def reference(x_prompt, x_sample, state_rwkv_shift, state_rwkv_wkv, state_gdn_conv, state_gdn_S,
              state_hgrn_S, state_ffn_conv, norm_mix_pre, norm_mix_post, norm_ffn_pre, norm_ffn_post,
              rwkv_mix, rwkv_w_rkv, rwkv_w0, rwkv_w1, rwkv_w2, rwkv_a0, rwkv_a1, rwkv_a2,
              rwkv_v0, rwkv_v1, rwkv_v2, rwkv_g1, rwkv_g2, rwkv_k_k, rwkv_k_a, rwkv_r_k,
              rwkv_lnx_w, rwkv_lnx_b, rwkv_w_o, gdn_w_in, gdn_conv_w, gdn_a_log, gdn_dt_bias,
              gdn_norm_w, gdn_w_o, hgrn_w_in, hgrn_lb, hgrn_norm_w, hgrn_w_o,
              ffn_w_up, ffn_conv_w, ffn_w_down):
    P = dict(norm_mix_pre=norm_mix_pre, norm_mix_post=norm_mix_post, norm_ffn_pre=norm_ffn_pre,
             norm_ffn_post=norm_ffn_post, rwkv_mix=rwkv_mix, rwkv_w_rkv=rwkv_w_rkv, rwkv_w0=rwkv_w0,
             rwkv_w1=rwkv_w1, rwkv_w2=rwkv_w2, rwkv_a0=rwkv_a0, rwkv_a1=rwkv_a1, rwkv_a2=rwkv_a2,
             rwkv_v0=rwkv_v0, rwkv_v1=rwkv_v1, rwkv_v2=rwkv_v2, rwkv_g1=rwkv_g1, rwkv_g2=rwkv_g2,
             rwkv_k_k=rwkv_k_k, rwkv_k_a=rwkv_k_a, rwkv_r_k=rwkv_r_k, rwkv_lnx_w=rwkv_lnx_w,
             rwkv_lnx_b=rwkv_lnx_b, rwkv_w_o=rwkv_w_o, gdn_w_in=gdn_w_in, gdn_conv_w=gdn_conv_w,
             gdn_a_log=gdn_a_log, gdn_dt_bias=gdn_dt_bias, gdn_norm_w=gdn_norm_w, gdn_w_o=gdn_w_o,
             hgrn_w_in=hgrn_w_in, hgrn_lb=hgrn_lb, hgrn_norm_w=hgrn_norm_w, hgrn_w_o=hgrn_w_o,
             ffn_w_up=ffn_w_up, ffn_conv_w=ffn_conv_w, ffn_w_down=ffn_w_down)
    Bp = x_prompt.shape[0]
    zero_like = lambda s: jnp.zeros((s.shape[0], Bp) + s.shape[2:], s.dtype)
    y_prompt, (p_shift, p_wkv, p_gconv, p_gS, p_hS, p_fconv) = _trunk(
        x_prompt, zero_like(state_rwkv_shift), zero_like(state_rwkv_wkv), zero_like(state_gdn_conv),
        zero_like(state_gdn_S), zero_like(state_hgrn_S), zero_like(state_ffn_conv), P)
    y_sample, (s_shift, s_wkv, s_gconv, s_gS, s_hS, s_fconv) = _trunk(
        x_sample, state_rwkv_shift, state_rwkv_wkv, state_gdn_conv, state_gdn_S, state_hgrn_S,
        state_ffn_conv, P)
    return (y_prompt, y_sample, p_shift, s_shift, p_wkv, s_wkv, p_gconv, s_gconv,
            p_gS, s_gS, p_hS, s_hS, p_fconv, s_fconv)


_drawn_inputs = setup_inputs


def setup_inputs(seed=0):
    import zlib

    import numpy as np

    out = dict(_drawn_inputs(seed))
    spreads = {}
    factors = {'rwkv_w1': 4.593, 'rwkv_w2': 4.679}
    for name, (base, spread) in spreads.items():
        noise = np.random.default_rng([zlib.crc32(name.encode()), seed]).standard_normal(out[name].shape)
        drawn = base * np.exp(spread * noise) if base else spread * noise
        out[name] = __import__('jax').numpy.asarray(drawn.astype(out[name].dtype))
    for name, factor in factors.items():
        out[name] = (out[name] * factor).astype(out[name].dtype)
    return out
```

```python
from contextlib import ExitStack

import concourse.bass as bass
from concourse import mybir

F32 = mybir.dt.float32
U32 = mybir.dt.uint32
ALU = mybir.AluOpType
ACT = mybir.ActivationFunctionType
AX_X = mybir.AxisListType.X

P = 128
D = 1024
KC = D // P
NPR = 256
NB = 8
NT = 4
NS = NB * NT
T = NPR + NS
SLOT = KC * T
DEPTH = 4
FF = 2816
FC = FF // P
FPAIR = FC // 2
DOWN_K = (8, 7, 7)
RING = 4
SLAB = 2048
LEVELS = 7
EPS = 1e-6
LNX_EPS = 64e-5
RW_DECAY = 0.6065306597126334
MIX_ORDER = (3, 2, 0, 1, 4, 5)
FW, GW = 3, 4
GT = 24


def weight_plan():
    plan = []

    def ffn(i):
        for p in range(FPAIR):
            plan.append(("up", i, 0, p))
            plan.append(("up", i, 1, p))
        for m in range(4):
            for s in range(3):
                plan.append(("down", i, m, s))

    def rwkv(j):
        plan.extend(("rkv", j, 2, m) for m in range(4))
        if j:
            plan.append(("v12",))
        plan.extend(("rkv", j, 1, m) for m in range(4))
        plan.extend(("rkv", j, 0, m) for m in range(4))
        plan.append(("wa1", j))
        plan.append(("wa2", j))
        plan.append(("g1", j))
        plan.append(("g2", j))
        plan.extend(("rwo", j, m) for m in range(4))

    rwkv(0)
    ffn(0)
    plan.extend(("gin", m) for m in range(16))
    plan.append(("grest",))
    plan.extend(("gwo", m) for m in range(4))
    ffn(1)
    plan.extend(("hin", m) for m in range(16))
    plan.extend(("hwo", m) for m in range(4))
    ffn(2)
    rwkv(1)
    ffn(3)
    return plan


PARAM_ROWS = (128, 96, 120, 34, 96, 88, 88, 88, 88, 88, 88, 128)
PARAM_DMAS = 24


def build(nc, A, OUT):
    ctx = ExitStack()
    with ctx:
        def sb(name, shape, dt=F32):
            return ctx.enter_context(nc.sbuf_tensor(name, shape, dt))

        sems = {}

        def sem(name):
            if name not in sems:
                sems[name] = ctx.enter_context(nc.semaphore(name))
            return sems[name]

        arena = sb("arena", [P, 12 * SLOT])
        names = ["X", "H", "SQ"] + [f"A{i}" for i in range(9)]

        def flat(name, n=1):
            k = names.index(name)
            return arena[:, k * SLOT:(k + n) * SLOT]

        def act3(name):
            return flat(name).rearrange("p (c t) -> p c t", c=KC)

        ring = sb("ring", [P, RING, SLAB])
        ident = sb("ident", [P, P])
        ones = sb("ones", [P, P])
        bones = sb("bones", [P, P])
        same = sb("same", [P, 2, P])
        low = sb("low", [P, LEVELS, P])
        upp = sb("upp", [P, LEVELS, P])
        mask4 = sb("mask4", [P, 4, P])
        samp4 = sb("samp4", [NS, 4, NS])
        lastm = sb("lastm", [NS, NS])
        seg = sb("seg", [P, T])
        bmask = sb("bmask", [P, NB, NS])
        rmask = sb("rmask", [NS, NB])
        pv = sb("pv", [P, 12, P])
        omka = sb("omka", [P, 2, KC])
        lb = sb("lb", [P, 8, KC])
        rstd = sb("rstd", [P, T])
        tm = sb("tm", [P, 2, 1024])
        ysb = sb("ysb", [P, 2, 512])
        rs = sb("rs", [P, 2, 256])
        nu = sb("nu", [P, 2, 256])
        xd = sb("xd", [P, 2, 256])
        sraw = sb("sraw", [P, 1024])
        sst = sb("sst", [P, 2, 512])
        sp = sb("sp", [P, 2, 128])
        sout = sb("sout", [P, 1024])
        spo = sb("spo", [P, 2, 128])
        tms = sb("tms", [NS, 3, P])
        ms = sb("ms", [NS, 2, 4, NS])
        ams = sb("ams", [P, 2, NB, NS])
        rms_ = sb("rms_", [P, 2, NS])
        us = sb("us", [NS, 4, P])
        vms = sb("vms", [NS, 2, 512])
        cen = sb("cen", [P, 4, KC, 2])
        els = sb("els", [P, KC, NB])
        lora = sb("lora", [P, T])
        tb = sb("tb", [P, 3, 16])
        neg = sb("neg", [P, 3, 8])
        ed = sb("ed", [P, 3, 4])
        gpar = sb("gpar", [8, 4])
        eps = sb("eps", [P, 2])
        bank = [ctx.enter_context(nc.psum_tensor(f"bank{i}", [P, 512], F32)) for i in range(2)]
        wide = [ctx.enter_context(nc.psum_tensor(f"wide{i}", [P, 1024], F32)) for i in range(3)]
        bk = [bank[0][:, :], bank[1][:, :]] + [wide[i // 2][:, (i % 2) * 512:(i % 2 + 1) * 512] for i in range(6)]

        def lvl_banks(g):
            return 2 + g, (4, 5) if g == 0 else (6, 7)

        hist = flat("A7")[:, 0:704].rearrange("p (b r) -> p b r", b=NB)
        last = flat("A7")[:, 704:704 + 792].rearrange("p (b r) -> p b r", b=NB + 1)
        g8 = sout[0:8, 0:3 * T].rearrange("p (q t) -> p q t", q=3)

        X, H, SQ = act3("X"), act3("H"), act3("SQ")
        S = [act3(f"A{i}") for i in range(9)]
        MX = flat("H", 2)[:, 0:4096].rearrange("p (g m q t) -> p g m q t", g=2, m=4, q=4)
        T2 = flat("A0")[:, 0:2048].rearrange("p (g m q t) -> p g m q t", g=2, m=4, q=2)
        ARp = flat("A6", 2)[:, 0:4096].rearrange("p (c b q t) -> p c b q t", c=KC, b=2, q=2)
        ARs = flat("A6", 2)[:, 4096:4608].rearrange("p (c q t) -> p c q t", c=KC, q=2)

        filled = {"scalar": sem("filled_for_scalar"), "vector": sem("filled_for_vector")}
        drained = {"scalar": sem("drained_by_scalar"), "vector": sem("drained_by_vector")}
        landed = [sem(f"weights_landed{i}") for i in range(RING)]
        slab_used = sem("slab_used")

        told = {}
        seen = {}

        def signal(name):
            told[name] = told.get(name, 0) + 1
            return sem(name)

        def after(eng, name, n=1):
            seen[id(eng), name] = seen.get((id(eng), name), 0) + n
            return seen[id(eng), name]

        def after_dma(eng, name, n=1):
            return after(eng, name, 16 * n)

        mark = {}
        plan = weight_plan()
        release = []
        n_filled = {"scalar": 0, "vector": 0}
        act_bank, vec_bank = [], []
        holder = {}

        def freed(b):
            if b not in holder:
                return sem("masks_ready"), 1
            e, k = holder[b]
            return drained[e], k + 1

        def result(e, *banks):
            k = n_filled[e]
            n_filled[e] += 1
            (act_bank if e == "scalar" else vec_bank).append(banks[0])
            for b in banks:
                holder[b] = (e, k)
            return k

        def cols(w, c0, n):
            return w[:, c0:c0 + n].rearrange("(k p) n -> p k n", p=P)

        def slab_parts(key, slot):
            kind = key[0]

            def v(o, k, n, rows=P):
                return slot[0:rows, o:o + k * n].rearrange("p (k n) -> p k n", k=k)

            if kind == "rkv":
                return [(v(0, 8, 256), cols(A["rwkv_w_rkv"][key[1], key[2]], key[3] * 256, 256))]
            if kind == "g1":
                return [(v(0, 8, 128), cols(A["rwkv_g1"][key[1]], 0, 128))]
            if kind == "v12":
                return [(v(0, 8, 32), cols(A["rwkv_v1"][0], 0, 32)), (slot[0:32, 256:1280], A["rwkv_v2"][0])]
            if kind == "wa1":
                return [(v(0, 8, 64), cols(A["rwkv_w1"][key[1]], 0, 64)),
                        (v(512, 8, 64), cols(A["rwkv_a1"][key[1]], 0, 64))]
            if kind == "wa2":
                return [(slot[0:64, 0:1024], A["rwkv_w2"][key[1]]),
                        (slot[0:64, 1024:2048], A["rwkv_a2"][key[1]])]
            if kind == "g2":
                return [(slot[:, 0:1024], A["rwkv_g2"][key[1]])]
            if kind == "rwo":
                return [(v(0, 8, 256), cols(A["rwkv_w_o"][key[1]], key[2] * 256, 256))]
            if kind == "gin":
                return [(v(0, 8, 256), cols(A["gdn_w_in"][0], key[1] * 256, 256))]
            if kind == "grest":
                return [(v(0, 8, 16), cols(A["gdn_w_in"][0], 4096, 16))]
            if kind == "gwo":
                return [(v(0, 8, 256), cols(A["gdn_w_o"][0], key[1] * 256, 256))]
            if kind == "hin":
                return [(v(0, 8, 256), cols(A["hgrn_w_in"][0], key[1] * 256, 256))]
            if kind == "hwo":
                return [(v(0, 8, 256), cols(A["hgrn_w_o"][0], key[1] * 256, 256))]
            if kind == "up":
                return [(v(0, 8, 256), cols(A["ffn_w_up"][key[1]], key[2] * FF + key[3] * 256, 256))]
            k0 = sum(DOWN_K[:key[3]])
            k = DOWN_K[key[3]]
            w = A["ffn_w_down"][key[1]][k0 * P:(k0 + k) * P]
            return [(v(0, k, 256), cols(w, key[2] * 256, 256))]

        landed_at = []
        per_slot = [0] * RING
        for n, key in enumerate(plan):
            per_slot[n % RING] += 16 * len(slab_parts(key, ring[:, 0, :]))
            landed_at.append(per_slot[n % RING])

        def pcol(kind, j, c):
            if kind in ("mix_pre", "mix_post", "ffn_pre", "ffn_post"):
                r = ("mix_pre", "mix_post", "ffn_pre", "ffn_post").index(kind) * 4 + j
                return pv[:, 0, r * 8 + c:r * 8 + c + 1]
            if kind == "mix":
                return pv[:, 1, j * 8 + c:j * 8 + c + 1]
            order = ("w0", "a0", "k_k", "k_a", "r_k", "lnx_w", "lnx_b", "v0")
            r = order.index(kind) * 2 + j
            return pv[:, 2, r * 8 + c:r * 8 + c + 1]

        def fconv(i, tap, c):
            r = i * 132 + tap * 44 + c
            return pv[:, 5 + r // 88, r % 88:r % 88 + 1]

        def gconv(tap, c):
            return pv[:, 4, tap * 24 + c:tap * 24 + c + 1]

        shiftT = pv[:, 11, :].rearrange("p (j b c) -> p j b c", j=2, b=NB)

        def ps3(b):
            return b[:, 0:T]

        def span(lead):
            return lead + NPR + NB * (lead + NT)

        def buf(n, lead):
            return flat("A5", 2)[:, n * span(lead):(n + 1) * span(lead)]

        def split(ap, lead):
            return ap[:, lead:lead + NPR], ap[:, lead + NPR:lead + NPR + NB * (lead + NT)].rearrange(
                "p (b t) -> p b t", b=NB)[:, :, lead:lead + NT]

        block = ctx.enter_context(nc.Block())

        @block.tensor
        def _(pe):
            state = {"slab": 0, "lin": 0}

            def slab():
                n = state["slab"]
                state["slab"] += 1
                pe.wait_ge(landed[n % RING], landed_at[n])
                return ring[:, n % RING, :]

            def free_after(s, value):
                release.append((s, value))

            def free_by(mm):
                mm.then_inc(signal("slab_used"), 1)
                release.append((slab_used, told["slab_used"]))

            def lin_bank():
                b = state["lin"] % 4
                state["lin"] += 1
                return b

            def linear_slab(w, rhs, tiles, key, ready=None, k_rows=P, nk=KC, m=P):
                for q in range(tiles):
                    b = lin_bank()
                    pe.wait_ge(*freed(b))
                    for k in range(nk):
                        if ready and q == 0:
                            pe.wait_ge(sem(ready), after(pe, ready))
                        mm = nc.tensor.matmul(bk[b][0:m, 0:T], w(k, q), rhs(k), start=(k == 0), stop=(k == nk - 1))
                    mm.then_inc(filled["scalar"], 1)
                    i = result("scalar", b)
                    mark[key, q] = i
                return i

            def square_linear(keys, rhs, name, ready=None):
                for s in range(keys):
                    sl = slab()
                    w = sl.rearrange("p (k n) -> p k n", k=8)
                    i = linear_slab(lambda k, q: w[:, k, q * P:(q + 1) * P], rhs, 2, (name, s),
                                    ready if s == 0 else None)
                    mark[name, 2 * s], mark[name, 2 * s + 1] = i - 1, i
                    free_after(filled["scalar"], i + 1)
                return i

            def norm_stat(weights, n):
                b = 4 + n % 2
                pe.wait_ge(*freed(b))
                for c in range(KC):
                    pe.wait_ge(sem("square_ready"), after(pe, "square_ready"))
                    mm = nc.tensor.matmul(bk[b][:, 0:T], weights[:, :], SQ[:, c, :], start=(c == 0), stop=(c == KC - 1))
                mm.then_inc(filled["scalar"], 1)
                result("scalar", b)

            def tile_stats(weights, ready, consumer="scalar", src=SQ):
                for c in range(KC):
                    pe.wait_ge(sem(ready), after(pe, ready))
                    b = 4 + c % 2
                    pe.wait_ge(*freed(b))
                    mm = nc.tensor.matmul(bk[b][:, 0:T], weights[:, :], src[:, c, :], start=True, stop=True)
                    mm.then_inc(filled[consumer], 1)
                    result(consumer, b)

            def turn(dst, src, n, base=0):
                return nc.tensor.transpose(dst, src, ident[base:base + n, base:base + n])

            def load_hist(rows, layer):
                pe.wait_ge(sem("hist_landed"), after_dma(pe, "hist_landed"))
                for q in range(2):
                    b = 6 + q
                    pe.wait_ge(*freed(b))
                    for i in range(4):
                        mm = turn(bk[b][:, i * 88:i * 88 + rows], sraw[0:rows, (q * 4 + i) * P:(q * 4 + i + 1) * P], rows)
                    mm.then_inc(filled["scalar"], 1)
                    mark["hist", layer] = result("scalar", b)

            def conv_state_out(rows):
                pe.wait_ge(sem("last_saved"), after(pe, "last_saved"))
                for q in range(3):
                    b = 6 + q % 2
                    pe.wait_ge(*freed(b))
                    for i in range(3):
                        mm = turn(bk[b][0:rows, i * P:(i + 1) * P], last[:, 3 * q + i, 0:rows], P)
                    mm.then_inc(filled["scalar"], 1)
                    result("scalar", b)

            def ffn(i):
                norm_stat(ones, 1)
                load_hist(88, i)
                for p in range(FPAIR):
                    for half in range(2):
                        sl = slab()
                        w = sl.rearrange("p (k n) -> p k n", k=8)
                        k = linear_slab(lambda k, q: w[:, k, q * P:(q + 1) * P], lambda k: H[:, k, :], 2,
                                        ("up", i, p, half), "h_ready" if p == 0 and half == 0 else None)
                        free_after(filled["scalar"], k + 1)
                y = flat("A0", 3)[:, 0:FC * T].rearrange("p (c t) -> p c t", c=FC)
                for m in range(4):
                    bs = [lin_bank(), lin_bank()]
                    for b_ in bs:
                        pe.wait_ge(*freed(b_))
                    kt = 0
                    for s in range(3):
                        sl = slab()
                        w = sl[:, 0:DOWN_K[s] * 256].rearrange("p (k n) -> p k n", k=DOWN_K[s])
                        for k in range(DOWN_K[s]):
                            if m == 0:
                                pe.wait_ge(sem("y_ready"), after(pe, "y_ready"))
                            for q in range(2):
                                mm = nc.tensor.matmul(bk[bs[q]][:, 0:T], w[:, k, q * P:(q + 1) * P], y[:, kt, :],
                                                      start=(kt == 0), stop=(kt == FC - 1))
                                if kt == FC - 1:
                                    mm.then_inc(filled["scalar"], 1)
                                    done = result("scalar", bs[q])
                            kt += 1
                        if s < 2:
                            free_by(mm)
                    free_after(filled["scalar"], done + 1)
                conv_state_out(88)
                norm_stat(ones, 0)

            def levels():
                ky, kp = [0, 0], [None, None]
                for l in range(LEVELS):
                    for g in range(2):
                        yb, pb = lvl_banks(g)
                        if l == 0:
                            pe.wait_ge(sem(f"t_ready{g}"), after(pe, f"t_ready{g}"))
                        else:
                            pe.wait_ge(drained["vector"], kp[g] + 1)
                        pe.wait_ge(*freed(yb))
                        for m in range(4):
                            mm = nc.tensor.matmul(bk[yb][:, m * P:(m + 1) * P], MX[:, g, m, 0, :], T2[:, g, m, 0, :],
                                                  start=True, stop=True)
                        mm.then_inc(filled["vector"], 1)
                        ky[g] = result("vector", yb)
                    for g in range(2):
                        yb, pb = lvl_banks(g)
                        pe.wait_ge(drained["vector"], ky[g] + 1)
                        for b_ in pb:
                            pe.wait_ge(*freed(b_))
                        for m in range(4):
                            ps = wide[1 + g][:, m * 256:m * 256 + 256]
                            y = ysb[:, g, m * P:(m + 1) * P]
                            nc.tensor.matmul(ps[:, 0:P], T2[:, g, m, 1, :], y, start=True, stop=True)
                            mm = nc.tensor.matmul(ps[:, P:2 * P], y, T2[:, g, m, 1, :], start=True, stop=True)
                        mm.then_inc(filled["vector"], 1)
                        kp[g] = result("vector", *pb)
                for g in range(2):
                    pe.wait_ge(drained["vector"], kp[g] + 1)

            def rwkv(j):
                norm_stat(ones, 0)
                M = [S[1], S[2]]

                def mixed(i):
                    return lambda k: M[i % 2][:, k, :]

                square_linear(4, mixed(0), ("v", j), "mix_ready")
                if j:
                    sl = slab()
                    wv1 = sl[:, 0:256].rearrange("p (k n) -> p k n", k=8)
                    kv = linear_slab(lambda k, q: wv1[:, k, :], mixed(0), 1, ("v1", j), m=32)
                    mark["mix_used", j, 0] = kv
                    pe.wait_ge(drained["scalar"], kv + 1)
                    for c in range(KC):
                        k2 = linear_slab(lambda k, q: sl[0:32, 256 + c * P:256 + (c + 1) * P], lambda k: lora[0:32, :], 1,
                                         ("v2", j, c), nk=1)
                    free_after(filled["scalar"], k2 + 1)
                else:
                    mark["mix_used", j, 0] = mark[("v", j), 7]
                square_linear(4, mixed(1), ("k", j), "mix_ready")
                mark["mix_used", j, 1] = mark[("k", j), 7]
                square_linear(4, mixed(2), ("r", j), "mix_ready")
                mark["mix_used", j, 2] = mark[("r", j), 7]
                sl1 = slab()
                w1 = sl1[:, 0:512].rearrange("p (k n) -> p k n", k=8)
                a1 = sl1[:, 512:1024].rearrange("p (k n) -> p k n", k=8)
                kw = linear_slab(lambda k, q: w1[:, k, :], mixed(3), 1, ("w1", j), "mix_ready", m=64)
                mark["mix_used", j, 3] = kw
                sl2 = slab()
                pe.wait_ge(drained["scalar"], kw + 1)
                for c in range(KC):
                    linear_slab(lambda k, q: sl2[0:64, c * P:(c + 1) * P], lambda k: lora[0:64, :], 1, ("w2", j, c), nk=1)
                ka = linear_slab(lambda k, q: a1[:, k, :], mixed(4), 1, ("a1", j), "mix_ready", m=64)
                mark["mix_used", j, 4] = ka
                free_after(filled["scalar"], ka + 1)
                pe.wait_ge(drained["scalar"], ka + 1)
                for c in range(KC):
                    k2 = linear_slab(lambda k, q: sl2[0:64, 1024 + c * P:1024 + (c + 1) * P],
                                     lambda k: lora[0:64, :], 1, ("a2", j, c), nk=1)
                free_after(filled["scalar"], k2 + 1)
                wg1 = slab()[:, 0:1024].rearrange("p (k n) -> p k n", k=8)
                kg = linear_slab(lambda k, q: wg1[:, k, :], mixed(5), 1, ("g1", j), "mix_ready")
                mark["mix_used", j, 5] = kg
                free_after(filled["scalar"], kg + 1)
                sl3 = slab()
                pe.wait_ge(drained["scalar"], kg + 1)
                for c in range(KC):
                    k2 = linear_slab(lambda k, q: sl3[:, c * P:(c + 1) * P], lambda k: lora[:, :], 1, ("g2", j, c), nk=1)
                free_after(filled["scalar"], k2 + 1)
                pe.wait_ge(sem("shift_saved"), after(pe, "shift_saved"))
                pe.wait_ge(*freed(6))
                mm = turn(bk[6][0:72, 0:P], spo_flat[:, 0:72], P)
                mm.then_inc(filled["scalar"], 1)
                result("scalar", 6)
                tile_stats(bones, "square_ready")
                tile_stats(bones, "bonus_product", "vector")

                pe.wait_ge(sem("operands_ready"), after(pe, "operands_ready"))
                K_, B_, V_ = S[4], S[1], S[3]
                for r in range(4):
                    kt = {}
                    for g in range(2):
                        c = 2 * r + g
                        for b in range(2):
                            pe.wait_ge(*freed(b))
                            for q, src in enumerate((V_, K_, B_)):
                                mm = turn(bk[b][:, q * P:(q + 1) * P], src[:, c, b * P:(b + 1) * P], P)
                            mm.then_inc(filled["scalar"], 1)
                            kt[g] = result("scalar", b)
                    for g in range(2):
                        c = 2 * r + g
                        yb, pb = lvl_banks(g)
                        for m in range(4):
                            hh, b = divmod(m, 2)
                            rows = slice(64 * hh, 64 * hh + 64)
                            bb = (yb, pb[0], pb[1], 1)[m]
                            pe.wait_ge(*freed(bb))
                            rhs = ARp[rows, c, b].rearrange("p q t -> p (q t)")
                            nc.tensor.matmul(bk[bb][:, 0:256], B_[rows, c, b * P:(b + 1) * P], rhs, start=True, stop=True)
                            mm = nc.tensor.matmul(bk[bb][:, 256:512], K_[rows, c, b * P:(b + 1) * P], rhs,
                                                  start=True, stop=True)
                            mm.then_inc(filled["vector"], 1)
                            result("vector", bb)
                    levels()
                    ks = [0, 0]
                    for b in range(2):
                        for g in range(2):
                            c = 2 * r + g
                            tg = tm[:, g, 0:768].rearrange("p (b q f) -> p b q f", b=2, q=3)
                            pe.wait_ge(drained["scalar"], kt[g] + 1)
                            bb = g
                            pe.wait_ge(*freed(bb))
                            if b:
                                pe.wait_ge(drained["vector"], ks[g] + 1)
                            if b:
                                nc.tensor.matmul(bk[bb][:, 0:P], ARp[:, c, b, 0, :], sp[:, g, :], start=True,
                                                 stop=False, skip_group_check=True)
                            for hh in range(2):
                                mm = nc.tensor.matmul(bk[bb][:, hh * 64:hh * 64 + 64], MX[:, g, 2 * hh + b, 2, :],
                                                      tg[:, b, 0, hh * 64:hh * 64 + 64], start=(b == 0),
                                                      stop=(b == 0 or hh == 1), skip_group_check=True)
                            mm.then_inc(filled["vector"], 1)
                            kr = result("vector", bb)
                            mark["r0", j, r, b, g] = kr
                        ku = [0, 0]
                        for g in range(2):
                            pe.wait_ge(drained["vector"], mark["r0", j, r, b, g] + 1)
                            pe.wait_ge(*freed(g))
                            for hh in range(2):
                                mm = nc.tensor.matmul(bk[g][:, hh * 64:hh * 64 + 64], T2[:, g, 2 * hh + b, 1, :],
                                                      rs[:, g, hh * 64:hh * 64 + 64], start=True, stop=True)
                            mm.then_inc(filled["scalar"], 1)
                            ku[g] = result("scalar", g)
                        for g in range(2):
                            c = 2 * r + g
                            tg = tm[:, g, 0:768].rearrange("p (b q f) -> p b q f", b=2, q=3)
                            pe.wait_ge(drained["scalar"], ku[g] + 1)
                            bb = 4 + g
                            pe.wait_ge(*freed(bb))
                            if b:
                                nc.tensor.matmul(bk[bb][:, 0:P], sp[:, g, :], ARp[:, c, b, 1, :],
                                                 start=True, stop=False, skip_group_check=True)
                            for hh in range(2):
                                rows = slice(64 * hh, 64 * hh + 64)
                                m = 2 * hh + b
                                o = bk[bb][rows, 0:P]
                                nc.tensor.matmul(o, tg[:, b, 0, hh * 64:hh * 64 + 64], MX[:, g, m, 3, :],
                                                 start=(b == 0), stop=False, skip_group_check=True)
                                mm = nc.tensor.matmul(o, nu[:, g, hh * 64:hh * 64 + 64], MX[:, g, m, 1, :],
                                                      start=False, stop=True, skip_group_check=True)
                            mm.then_inc(filled["scalar"], 1)
                            result("scalar", bb)
                            bb = 2 + g
                            pe.wait_ge(*freed(bb))
                            nc.tensor.matmul(bk[bb][:, 0:P], tg[:, b, 1, :], tg[:, b, 0, :], start=True, stop=False)
                            mm = nc.tensor.matmul(bk[bb][:, 0:P], tg[:, b, 2, :], nu[:, g, 0:P], start=False, stop=True)
                            mm.then_inc(filled["vector"], 1)
                            ks[g] = result("vector", bb)
                    for g in range(2):
                        pe.wait_ge(drained["vector"], ks[g] + 1)
                        pe.wait_ge(*freed(6 + g))
                        mm = turn(bk[6 + g][:, 0:P], sp[:, g, :], P)
                        mm.then_inc(filled["scalar"], 1)
                        result("scalar", 6 + g)
                    for g in range(2):
                        rwkv_sample(j, 2 * r + g)

                for c in range(KC):
                    if c == 0:
                        pe.wait_ge(drained["scalar"], n_filled["scalar"] - 1 + 1)
                    b = 4 + c % 2
                    pe.wait_ge(*freed(b))
                    mm = nc.tensor.matmul(bk[b][:, 0:T], bones[:, :], S[5][:, c, :], start=True, stop=True)
                    mm.then_inc(filled["vector"], 1)
                    mark["mean", j, c] = result("vector", b)
                tile_stats(bones, "square_ready")
                square_linear(4, lambda k: S[5][:, k, :], ("rwo", j), "mixer_out")
                norm_stat(ones, 1)

            spo_flat = spo[:, :, :].rearrange("p a b -> p (a b)")

            def rwkv_sample(j, c):
                K_, B_, V_ = S[4], S[1], S[3]
                pe.wait_ge(sem("sample_state_in"), after_dma(pe, "sample_state_in", 2))
                pe.wait_ge(*freed(0))
                for b in range(NB):
                    mm = turn(bk[0][:, b * 64:(b + 1) * 64], sraw[0:64, b * P:(b + 1) * P], 64)
                mm.then_inc(filled["scalar"], 1)
                mark["sraw", "rwkv", j, c] = result("scalar", 0)
                pe.wait_ge(*freed(1))
                for q, src in enumerate((V_, K_, B_)):
                    mm = turn(bk[1][0:NS, q * P:(q + 1) * P], src[:, c, NPR:T], P)
                mm.then_inc(filled["scalar"], 1)
                ktm = mark["tms", "rwkv", j, c] = result("scalar", 1)
                for hh in range(2):
                    rows = slice(64 * hh, 64 * hh + 64)
                    rhs = ARs[rows, c].rearrange("p q t -> p (q t)")
                    pe.wait_ge(*freed(2 + hh))
                    nc.tensor.matmul(bk[2 + hh][0:NS, 0:64], B_[rows, c, NPR:T], rhs, start=True, stop=True)
                    mm = nc.tensor.matmul(bk[2 + hh][0:NS, 64:128], K_[rows, c, NPR:T], rhs, start=True, stop=True)
                    mm.then_inc(filled["vector"], 1)
                    km = result("vector", 2 + hh)
                pe.wait_ge(drained["scalar"], ktm + 1)
                pe.wait_ge(drained["vector"], km + 1)
                pe.wait_ge(sem("spread_ready"), after(pe, "spread_ready"))
                pe.wait_ge(*freed(5))
                for hh in range(2):
                    o = bk[5][0:NS, hh * 64:hh * 64 + 64]
                    nc.tensor.matmul(o, ms[:, hh, 2, :], tms[:, 0, hh * 64:hh * 64 + 64], start=True, stop=False)
                    for b in range(NB):
                        mm = nc.tensor.matmul(o, ams[:, hh, b, :], sst[:, 0, b * 64:(b + 1) * 64],
                                              start=False, stop=(b == NB - 1))
                mm.then_inc(filled["vector"], 1)
                kx = result("vector", 5)
                for step in range(3):
                    pe.wait_ge(drained["vector"], kx + 1)
                    bb = 2 + step % 2
                    pe.wait_ge(*freed(bb))
                    for hh in range(2):
                        mm = nc.tensor.matmul(bk[bb][0:NS, hh * 64:hh * 64 + 64], ms[:, hh, 0, :],
                                              us[:, step, hh * 64:hh * 64 + 64], start=True, stop=True)
                    mm.then_inc(filled["vector"], 1)
                    kx = result("vector", bb)
                pe.wait_ge(drained["vector"], kx + 1)
                pe.wait_ge(*freed(4))
                for hh in range(2):
                    rows = slice(64 * hh, 64 * hh + 64)
                    o = bk[4][rows, 0:NS]
                    nc.tensor.matmul(o, tms[:, 0, hh * 64:hh * 64 + 64], ms[:, hh, 3, :], start=True, stop=False)
                    nc.tensor.matmul(o, us[:, 3, hh * 64:hh * 64 + 64], ms[:, hh, 1, :], start=False, stop=False)
                    for b in range(NB):
                        mm = nc.tensor.matmul(o[:, b * NT:(b + 1) * NT], sst[:, 0, b * 64:(b + 1) * 64],
                                              rms_[:, hh, b * NT:(b + 1) * NT], start=False, stop=(b == NB - 1))
                mm.then_inc(filled["scalar"], 1)
                result("scalar", 4)
                for hh in range(2):
                    pe.wait_ge(sem("values_spread"), after(pe, "values_spread"))
                    bb = 6 + hh
                    pe.wait_ge(*freed(bb))
                    nc.tensor.matmul(bk[bb][:, :], tms[:, 1, :], vms[:, 0, :], start=True, stop=False)
                    mm = nc.tensor.matmul(bk[bb][:, :], tms[:, 2, :], vms[:, 1, :], start=False, stop=True)
                    mm.then_inc(filled["vector"], 1)
                    result("vector", bb)
                pe.wait_ge(sem("sample_state_new"), after(pe, "sample_state_new"))
                for q in range(2):
                    pe.wait_ge(*freed(2 + q))
                    for i in range(4):
                        b = 4 * q + i
                        mm = turn(bk[2 + q][0:64, i * P:(i + 1) * P], sst[:, 1, b * 64:(b + 1) * 64], P)
                    mm.then_inc(filled["scalar"], 1)
                    result("scalar", 2 + q)

            def gdn():
                norm_stat(ones, 0)
                load_hist(72, "gdn")
                square_linear(16, lambda k: H[:, k, :], "gin", "h_ready")
                w = slab()[:, 0:128].rearrange("p (k n) -> p k n", k=8)
                linear_slab(lambda k, q: w[:, k, 0:8], lambda k: H[:, k, :], 1, "gbeta", m=8)
                i = linear_slab(lambda k, q: w[:, k, 8:16], lambda k: H[:, k, :], 1, "gdecay", m=8)
                free_after(filled["scalar"], i + 1)
                conv_state_out(72)
                tile_stats(ones, "square_ready")
                tile_stats(ones, "square_ready")
                pe.wait_ge(sem("decay_ready"), after(pe, "decay_ready"))
                pe.wait_ge(*freed(6))
                for blk, n in enumerate((P, P, NS)):
                    for q in range(2):
                        mm = turn(bk[6][0:n, blk * 16 + q * 8:blk * 16 + q * 8 + 8],
                                  g8[:, 2 * q, blk * P:blk * P + n], 8)
                mm.then_inc(filled["scalar"], 1)
                result("scalar", 6)
                for h in range(8):
                    b = 4 + h % 2
                    pe.wait_ge(*freed(b))
                    mm = nc.tensor.matmul(bk[b][:, 0:T], ident[0:8, h:h + 1].to_broadcast([8, P]), g8[:, 2, :], start=True, stop=True)
                    mm.then_inc(filled["scalar"], 1)
                    result("scalar", b)
                pe.wait_ge(sem("operands_ready"), after(pe, "operands_ready"))
                Q, K, V, QG = S[1], S[4], S[2], S[7]
                for r in range(2):
                    kt, ks = {}, [0, 0]
                    for g in range(2):
                        for hh in range(2):
                            h = 4 * r + 2 * g + hh
                            pe.wait_ge(*freed(hh))
                            for q, (src, b) in enumerate(((V, 0), (K, 0), (V, 1), (K, 1))):
                                mm = turn(bk[hh][:, q * P:(q + 1) * P], src[:, h, b * P:(b + 1) * P], P)
                            mm.then_inc(filled["scalar"], 1)
                            kt[g] = mark["gtm", r, g] = result("scalar", hh)
                    for g in range(2):
                        yb, pb = lvl_banks(g)
                        for m in range(4):
                            hh, b = divmod(m, 2)
                            h = 4 * r + 2 * g + hh
                            bb = (yb, pb[0], pb[1], 1)[m]
                            pe.wait_ge(*freed(bb))
                            kk = K[:, h, b * P:(b + 1) * P]
                            nc.tensor.matmul(bk[bb][:, 0:P], kk, kk, start=True, stop=True)
                            mm = nc.tensor.matmul(bk[bb][:, P:2 * P], kk, Q[:, h, b * P:(b + 1) * P], start=True, stop=True)
                            mm.then_inc(filled["vector"], 1)
                            result("vector", bb)
                    levels()
                    for b in range(2):
                        kr = [0, 0]
                        if b:
                            for g in range(2):
                                pe.wait_ge(drained["vector"], ks[g] + 1)
                                pe.wait_ge(*freed(g))
                                for hh in range(2):
                                    h = 4 * r + 2 * g + hh
                                    mm = nc.tensor.matmul(bk[g][:, hh * P:(hh + 1) * P], K[:, h, P:2 * P],
                                                          gstate(g, hh), start=True, stop=True)
                                mm.then_inc(filled["vector"], 1)
                                kr[g] = result("vector", g)
                        kz = [0, 0]
                        for g in range(2):
                            tg = tm[:, g, :].rearrange("p (h b q f) -> p h b q f", h=2, b=2, q=2)
                            pe.wait_ge(drained["scalar"], kt[g] + 1)
                            if b:
                                pe.wait_ge(drained["vector"], kr[g] + 1)
                            pe.wait_ge(*freed(g))
                            for hh in range(2):
                                rhs = rs[:, g, hh * P:(hh + 1) * P] if b else tg[:, hh, 0, 0, :]
                                mm = nc.tensor.matmul(bk[g][:, hh * P:(hh + 1) * P], T2[:, g, 2 * hh + b, 1, :], rhs,
                                                      start=True, stop=True)
                            mm.then_inc(filled["scalar"], 1)
                            kz[g] = mark["z", r, b, g] = result("scalar", g)
                        for g in range(2):
                            tg = tm[:, g, :].rearrange("p (h b q f) -> p h b q f", h=2, b=2, q=2)
                            pe.wait_ge(drained["scalar"], kz[g] + 1)
                            bb = 4 + g
                            pe.wait_ge(*freed(bb))
                            for hh in range(2):
                                h = 4 * r + 2 * g + hh
                                o = bk[bb][:, hh * P:(hh + 1) * P]
                                mm = nc.tensor.matmul(o, nu[:, g, hh * P:(hh + 1) * P], MX[:, g, 2 * hh + b, 1, :],
                                                      start=True, stop=(b == 0))
                                if b:
                                    mm = nc.tensor.matmul(o, gstate(g, hh), QG[:, h, P:2 * P], start=False, stop=True)
                            mm.then_inc(filled["scalar"], 1)
                            result("scalar", bb)
                            pe.wait_ge(sem("xd_ready"), after(pe, "xd_ready"))
                            bb = 2 + g
                            pe.wait_ge(*freed(bb))
                            for hh in range(2):
                                mm = nc.tensor.matmul(bk[bb][:, hh * P:(hh + 1) * P], tg[:, hh, b, 1, :],
                                                      xd[:, g, hh * P:(hh + 1) * P], start=True, stop=True)
                            mm.then_inc(filled["vector"], 1)
                            ks[g] = mark["gstate", r, b, g] = result("vector", bb)
                    for g in range(2):
                        for hh in range(2):
                            gdn_sample(4 * r + 2 * g + hh)
                tile_norm_out("gwo")

            def tile_norm_out(name):
                tile_stats(ones, "square_ready")
                square_linear(4, lambda k: S[5][:, k, :], name, "mixer_out")
                norm_stat(ones, 1)

            def gdn_sample(h):
                Q, K, V, QG = S[1], S[4], S[2], S[7]
                pe.wait_ge(*freed(1))
                for q, src in enumerate((V, K)):
                    mm = turn(bk[1][0:NS, q * P:(q + 1) * P], src[:, h, NPR:T], P)
                mm.then_inc(filled["scalar"], 1)
                ktm = mark["tms", "gdn", h] = result("scalar", 1)
                pe.wait_ge(*freed(2))
                nc.tensor.matmul(bk[2][0:NS, 0:NS], K[:, h, NPR:T], K[:, h, NPR:T], start=True, stop=True)
                mm = nc.tensor.matmul(bk[2][0:NS, NS:2 * NS], K[:, h, NPR:T], Q[:, h, NPR:T], start=True, stop=True)
                mm.then_inc(filled["vector"], 1)
                result("vector", 2)
                pe.wait_ge(sem("sample_state_in"), after_dma(pe, "sample_state_in"))
                pe.wait_ge(sem("spread_ready"), after(pe, "spread_ready"))
                pe.wait_ge(*freed(3))
                for b in range(NB):
                    mm = nc.tensor.matmul(bk[3][0:NS, 0:P], ams[:, 0, b, :], sraw[:, b * P:(b + 1) * P],
                                          start=(b == 0), stop=(b == NB - 1))
                mm.then_inc(filled["vector"], 1)
                kx = result("vector", 3)
                pe.wait_ge(drained["scalar"], ktm + 1)
                for step in range(3):
                    pe.wait_ge(drained["vector"], kx + 1)
                    bb = 2 + step % 2
                    pe.wait_ge(*freed(bb))
                    mm = nc.tensor.matmul(bk[bb][0:NS, 0:P], ms[:, 0, 0, :], us[:, step, :], start=True, stop=True)
                    mm.then_inc(filled["vector"], 1)
                    kx = result("vector", bb)
                pe.wait_ge(sem("x_scaled"), after(pe, "x_scaled"))
                pe.wait_ge(*freed(4))
                nc.tensor.matmul(bk[4][:, 0:NS], us[:, 3, :], ms[:, 0, 1, :], start=True, stop=False)
                for b in range(NB):
                    mm = nc.tensor.matmul(bk[4][:, b * NT:(b + 1) * NT], sraw[:, b * P:(b + 1) * P],
                                          QG[:, h, NPR + b * NT:NPR + (b + 1) * NT], start=False, stop=(b == NB - 1))
                mm.then_inc(filled["scalar"], 1)
                result("scalar", 4)
                pe.wait_ge(sem("values_spread"), after(pe, "values_spread"))
                pe.wait_ge(*freed(6))
                pe.wait_ge(*freed(7))
                for q in range(2):
                    mm = nc.tensor.matmul(bk[6 + q], tms[:, 1, :], vms[:, q, :], start=True, stop=True)
                mm.then_inc(filled["vector"], 1)
                mark["sraw", "gdn", h] = result("vector", 6, 7)

            def gstate(g, hh):
                return (sp if hh == 0 else spo)[:, g, :]

            def hgrn():
                norm_stat(ones, 0)
                square_linear(16, lambda k: H[:, k, :], "hin", "h_ready")
                Q, K, V, QG, KD, QL, KL = S[0], S[2], S[4], S[5], S[6], H, SQ
                for l in range(LEVELS + 1):
                    pe.wait_ge(sem("level_operands"), after(pe, "level_operands"))
                    q_, k_ = (Q, K) if l == 0 else (QL, KL)
                    for n in range(4):
                        bb = n
                        pe.wait_ge(*freed(bb))
                        for i in range(4):
                            h, b = divmod(4 * n + i, 2)
                            mm = nc.tensor.matmul(bk[bb][:, i * P:(i + 1) * P], k_[:, h, b * P:(b + 1) * P],
                                                  q_[:, h, b * P:(b + 1) * P], start=True, stop=True)
                        mm.then_inc(filled["vector"], 1)
                        result("vector", bb)
                    if l <= 2:
                        pe.wait_ge(*freed(4))
                        for h in range(8):
                            mm = nc.tensor.matmul(bk[4][0:NS, h * NS:(h + 1) * NS], k_[:, h, NPR:T], q_[:, h, NPR:T],
                                                  start=True, stop=True)
                        mm.then_inc(filled["vector"], 1)
                        result("vector", 4)
                pe.wait_ge(drained["vector"], n_filled["vector"] - 1 + 1)
                AT = flat("A1")[:, 0:2048].rearrange("p (h b t) -> p h b t", h=8, b=2)
                ATS = flat("A1")[0:NS, 2048:2304].rearrange("p (h t) -> p h t", h=8)
                for h in range(8):
                    g = h % 2
                    pe.wait_ge(*freed(g))
                    for q, (src, b) in enumerate(((V, 0), (KD, 0), (V, 1), (KD, 1))):
                        mm = turn(bk[g][:, q * P:(q + 1) * P], src[:, h, b * P:(b + 1) * P], P)
                    mm.then_inc(filled["scalar"], 1)
                    kt = result("scalar", g)
                    pe.wait_ge(*freed(2 + g))
                    for q, src in enumerate((V, KD)):
                        mm = turn(bk[2 + g][0:NS, q * P:(q + 1) * P], src[:, h, NPR:T], P)
                    mm.then_inc(filled["scalar"], 1)
                    ktm = mark["tms", "hgrn", h] = result("scalar", 2 + g)
                    pe.wait_ge(drained["scalar"], kt + 1)
                    tg = tm[:, g, 0:512].rearrange("p (b q f) -> p b q f", b=2, q=2)
                    for b in range(2):
                        if b:
                            pe.wait_ge(drained["vector"], ks + 1)
                        pe.wait_ge(*freed(5))
                        mm = nc.tensor.matmul(bk[5][:, 0:P], tg[:, b, 0, :], AT[:, h, b, :], start=True, stop=(b == 0))
                        if b:
                            mm = nc.tensor.matmul(bk[5][:, 0:P], sp[:, g, :], QG[:, h, P:2 * P], start=False, stop=True)
                        mm.then_inc(filled["scalar"], 1)
                        result("scalar", 5)
                        pe.wait_ge(*freed(4))
                        mm = nc.tensor.matmul(bk[4][:, 0:P], tg[:, b, 1, :], tg[:, b, 0, :], start=True, stop=True)
                        mm.then_inc(filled["vector"], 1)
                        ks = result("vector", 4)
                    mark["hstate", h] = ks
                    pe.wait_ge(drained["scalar"], ktm + 1)
                    pe.wait_ge(sem("sample_state_in"), after_dma(pe, "sample_state_in"))
                    pe.wait_ge(*freed(5))
                    nc.tensor.matmul(bk[5][:, 0:NS], tms[:, 0, :], ATS[:, h, :], start=True, stop=False)
                    for b in range(NB):
                        mm = nc.tensor.matmul(bk[5][:, b * NT:(b + 1) * NT], sraw[:, b * P:(b + 1) * P],
                                              QG[:, h, NPR + b * NT:NPR + (b + 1) * NT], start=False, stop=(b == NB - 1))
                    mm.then_inc(filled["scalar"], 1)
                    result("scalar", 5)
                    pe.wait_ge(sem("values_spread"), after(pe, "values_spread"))
                    pe.wait_ge(*freed(6))
                    pe.wait_ge(*freed(7))
                    for q in range(2):
                        mm = nc.tensor.matmul(bk[6 + q], tms[:, 1, :], vms[:, q, :], start=True, stop=True)
                    mm.then_inc(filled["vector"], 1)
                    mark["sraw", "hgrn", h] = result("vector", 6, 7)
                tile_norm_out("hwo")

            pe.wait_ge(sem("masks_ready"), after(pe, "masks_ready"))
            pe.wait_ge(sem("params_landed"), after_dma(pe, "params_landed", PARAM_DMAS))
            for n, rows in enumerate(PARAM_ROWS):
                b = 6 + n % 2
                pe.wait_ge(*freed(b))
                mm = turn(bk[b][:, 0:rows], flat("A2", 1)[0:rows, n * P:(n + 1) * P], rows)
                mm.then_inc(filled["scalar"], 1)
                result("scalar", b)
            xin = flat("A0", 2)[:, 0:3072].rearrange("p (b f) -> p b f", b=3)
            pe.wait_ge(sem("x_landed"), after_dma(pe, "x_landed", 2))
            for blk, n in enumerate((P, P, NS)):
                for q in range(2):
                    b = 2 * (blk % 2) + q
                    pe.wait_ge(*freed(b))
                    for i in range(4):
                        mm = turn(bk[b][:, i * P:i * P + n], xin[0:n, blk, (4 * q + i) * P:(4 * q + i + 1) * P], n)
                    mm.then_inc(filled["scalar"], 1)
                    result("scalar", b)
            rwkv(0)
            ffn(0)
            gdn()
            ffn(1)
            hgrn()
            ffn(2)
            rwkv(1)
            ffn(3)
            pe.wait_ge(sem("x_ready"), after(pe, "x_ready", 2 * DEPTH * KC))
            for blk, n in enumerate((P, P, NS)):
                for q in range(2):
                    b = 2 * (blk % 2) + q
                    pe.wait_ge(*freed(b))
                    for i in range(4):
                        mm = turn(bk[b][0:n, i * P:(i + 1) * P], X[:, 4 * q + i, blk * P:blk * P + n], P)
                    mm.then_inc(filled["scalar"], 1)
                    result("scalar", b)

        @block.scalar
        def _(act):
            n_taken = {"n": 0}

            def take():
                n_taken["n"] += 1
                return n_taken["n"]

            def fn(out, in_, f, bias=0.0, scale=1.0):
                if f == ACT.Copy and not isinstance(bias, float):
                    f = ACT.Identity
                return nc.scalar.activation(out, in_, f, bias=bias, scale=scale)

            def squares(src, hear_name=None):
                for c in range(KC):
                    if hear_name:
                        act.wait_ge(sem(hear_name), after(act, hear_name))
                    fn(SQ[:, c, :], src[:, c, :], ACT.Square).then_inc(signal("square_ready"), 1)

            def rms():
                act.wait_ge(filled["scalar"], take())
                fn(rstd[:, :], bk4(n_taken["n"]), ACT.Ln, bias=eps[:, 0:1], scale=1.0 / D).then_inc(drained["scalar"], 1)
                act.wait_ge(drained["scalar"], n_taken["n"])
                fn(rstd[:, :], rstd[:, :], ACT.Exp, scale=-0.5).then_inc(signal("rstd_ready"), 1)
                act.wait_ge(sem("rstd_ready"), told["rstd_ready"])

            def bk4(n):
                return bk[act_bank[n - 1]][:, 0:T]

            def ps(m=P):
                return bk[act_bank[n_taken["n"] - 1]][0:m, 0:T]

            def psb():
                return bk[act_bank[n_taken["n"] - 1]]

            def evac(dst, f=ACT.Copy, bias=0.0, m=P):
                act.wait_ge(filled["scalar"], take())
                fn(dst, ps(m), f, bias=bias).then_inc(drained["scalar"], 1)
                act.wait_ge(drained["scalar"], n_taken["n"])

            def pre_norm():
                squares(X, "x_ready")
                rms()

            def out_projection():
                for c in range(KC):
                    evac(S[3][:, c, :])
                    fn(SQ[:, c, :], S[3][:, c, :], ACT.Square).then_inc(signal("square_ready"), 1)

            def head_rstd(dst, scale, e):
                for c in range(KC):
                    act.wait_ge(filled["scalar"], take())
                    fn(dst[:, c, :], ps(), ACT.Ln, bias=eps[:, e:e + 1], scale=scale).then_inc(drained["scalar"], 1)
                    act.wait_ge(drained["scalar"], n_taken["n"])
                fn(dst, dst, ACT.Exp, scale=-0.5).then_inc(signal("rk_ready"), 1)
                act.wait_ge(sem("rk_ready"), told["rk_ready"])

            def take_hist(rows):
                for q in range(2):
                    act.wait_ge(filled["scalar"], take())
                    fn(hist[:, q * 4:q * 4 + 4, 0:rows],
                             psb()[:, 0:352].rearrange("p (i r) -> p i r", i=4)[:, :, 0:rows], ACT.Copy).then_inc(drained["scalar"], 1)
                    act.wait_ge(drained["scalar"], n_taken["n"])

            def conv_state_out(prompt_out, sample_out, rows, width):
                stage = tm[:, :, :].rearrange("p a b -> p (a b)")[0:rows, 0:9 * P].rearrange("r (b f) -> r b f", b=9)
                hear_conv_out()
                state["conv"] += 32
                for q in range(3):
                    act.wait_ge(filled["scalar"], take())
                    fn(stage[:, 3 * q:3 * q + 3, :],
                             psb()[0:rows, 0:3 * P].rearrange("r (b f) -> r b f", b=3), ACT.Copy).then_inc(drained["scalar"], 1)
                    act.wait_ge(drained["scalar"], n_taken["n"])
                act.dma_start(prompt_out.rearrange("b w (c f) -> (w c) b f", f=P), stage[:, 0:1, :]).then_inc(sem("conv_state_out"), 16)
                act.dma_start(sample_out.rearrange("b w (c f) -> (w c) b f", f=P), stage[:, 1:9, :]).then_inc(sem("conv_state_out"), 16)

            def two_part(dst_p, dst_s, src_p, src_s, f):
                fn(dst_p, src_p, f)
                return fn(dst_s, src_s, f)

            def ffn(i):
                pre_norm()
                take_hist(88)
                lead = FW - 1

                def gate(p):
                    for q in range(2):
                        act.wait_ge(sem("gate_conv"), after(act, "gate_conv"))
                        cv = buf(4 + (p % 2) * 4 + 2 + q, lead)[:, 0:NPR + NB * (lead + NT)]
                        fn(cv, cv, ACT.Silu).then_inc(signal("silu_ready"), 1)

                for p in range(FPAIR):
                    for half in range(2):
                        if half and p:
                            gate(p - 1)
                        for q in range(2):
                            act.wait_ge(filled["scalar"], take())
                            if p:
                                act.wait_ge(sem("saved"), after(act, "saved"))
                                if not half:
                                    act.wait_ge(sem("value_conv"), after(act, "value_conv"))
                            dp, ds = split(buf(half * 2 + q, lead), lead)
                            two_part(dp, ds, psb()[:, 0:NPR], psb()[:, NPR:T].rearrange("p (b t) -> p b t", b=NB), ACT.Copy).then_inc(drained["scalar"], 1)
                            act.wait_ge(drained["scalar"], n_taken["n"])
                gate(FPAIR - 1)
                act.wait_ge(sem("saved"), after(act, "saved", 4))
                act.wait_ge(sem("value_conv"), after(act, "value_conv", 2))
                out_projection()
                conv_state_out(OUT["prompt_ffn_conv"][i], OUT["sample_ffn_conv"][i], 88, 2)
                rms()

            def shift_out(j):
                act.wait_ge(filled["scalar"], take())
                hear_state_out()
                fn(sout[0:72, 0:P], psb()[0:72, 0:P], ACT.Copy).then_inc(drained["scalar"], 1)
                act.wait_ge(drained["scalar"], n_taken["n"])
                o = sem("sample_state_out")
                act.dma_start(OUT["prompt_shift"][j].rearrange("b (c f) -> (b c) f", f=P), sout[0:8, 0:P]).then_inc(o, 16)
                act.dma_start(OUT["sample_shift"][j].rearrange("b (c f) -> (b c) f", f=P), sout[8:72, 0:P]).then_inc(o, 16)
                state["out"] += 32

            state = {"out": 0, "pout": 0, "conv": 0}

            def hear_conv_out():
                if state["conv"]:
                    act.wait_ge(sem("conv_state_out"), state["conv"])

            def hear_state_out():
                if state["out"]:
                    act.wait_ge(sem("sample_state_out"), state["out"])

            def hear_prompt_out():
                if state["pout"]:
                    act.wait_ge(sem("prompt_state_out"), state["pout"])

            def rwkv(j):
                pre_norm()
                for c in range(KC):
                    evac(S[3][:, c, :])
                if j:
                    act.wait_ge(sem("v_first_kept"), 16)
                    act.dma_start(S[8], A["v_first"].rearrange("(c p) t -> p c t", p=P)).then_inc(sem("v_first_back"), 16)
                    evac(lora[0:32, :], m=32)
                    for c in range(KC):
                        evac(SQ[:, c, :], ACT.Sigmoid, pcol("v0", 0, c))
                else:
                    act.dma_start(A["v_first"].rearrange("(c p) t -> p c t", p=P), S[3]).then_inc(sem("v_first_kept"), 16)
                for c in range(KC):
                    evac(S[4][:, c, :])
                for c in range(KC):
                    evac(S[5][:, c, :])
                evac(lora[0:64, :], ACT.Tanh, m=64)
                for c in range(KC):
                    evac(S[6][:, c, :], ACT.Sigmoid, pcol("w0", j, c))
                evac(lora[0:64, :], m=64)
                for c in range(KC):
                    evac(S[7][:, c, :], ACT.Sigmoid, pcol("a0", j, c))
                evac(lora[:, :], ACT.Sigmoid)
                if j:
                    act.wait_ge(sem("v_mixed"), after(act, "v_mixed"))
                for c in range(KC):
                    evac(S[8][:, c, :])
                shift_out(j)
                squares(S[0], "kk_raw")
                head_rstd(S[1], 1.0, 0)
                act.wait_ge(sem("ge_ready"), after(act, "ge_ready"))
                fn(cen[:, 1], cen[:, 0], ACT.Exp).then_inc(signal("scalar_chain"), 1)
                act.wait_ge(sem("scalar_chain"), told["scalar_chain"])
                fn(SQ, SQ, ACT.Exp).then_inc(signal("e_excl"), 1)
                act.wait_ge(sem("e_excl"), told["e_excl"])
                act.wait_ge(sem("a_done"), after(act, "a_done"))
                fn(SQ, H, ACT.Exp).then_inc(signal("e_incl"), 1)
                act.wait_ge(sem("e_incl"), told["e_incl"])
                fn(H, H, ACT.Exp, scale=-1.0).then_inc(signal("e_neg"), 1)
                act.wait_ge(sem("e_neg"), told["e_neg"])
                for r in range(4):
                    for g in range(2):
                        for b in range(2):
                            act.wait_ge(filled["scalar"], take())
                            if r == 0 and g == 0 and b == 0:
                                hear_conv_out()
                            fn(tm[:, g, b * 384:(b + 1) * 384], psb()[:, 0:384], ACT.Copy).then_inc(drained["scalar"], 1)
                            act.wait_ge(drained["scalar"], n_taken["n"])
                    for b in range(2):
                        for g in range(2):
                            act.wait_ge(filled["scalar"], take())
                            fn(nu[:, g, 0:P], psb()[:, 0:P], ACT.Copy, scale=-1.0).then_inc(drained["scalar"], 1)
                            act.wait_ge(drained["scalar"], n_taken["n"])
                        for g in range(2):
                            act.wait_ge(filled["scalar"], take())
                            fn(S[5][:, 2 * r + g, b * P:(b + 1) * P], psb()[:, 0:P], ACT.Copy).then_inc(drained["scalar"], 1)
                            act.wait_ge(drained["scalar"], n_taken["n"])
                    hear_prompt_out()
                    for g in range(2):
                        act.wait_ge(filled["scalar"], take())
                        fn(spo[:, g, :], psb()[:, 0:P], ACT.Copy).then_inc(drained["scalar"], 1)
                        act.wait_ge(drained["scalar"], n_taken["n"])
                        c = 2 * r + g
                        for hh in range(2):
                            rows = slice(64 * hh, 64 * hh + 64)
                            act.dma_start(OUT["prompt_wkv"][j, 0, 2 * c + hh], spo[rows, g, rows]).then_inc(
                                sem("prompt_state_out"), 16)
                            state["pout"] += 16
                    for g in range(2):
                        c = 2 * r + g
                        act.wait_ge(filled["scalar"], take())
                        fn(sst[:, 0, :], psb(), ACT.Copy).then_inc(drained["scalar"], 1)
                        act.wait_ge(drained["scalar"], n_taken["n"])
                        act.wait_ge(filled["scalar"], take())
                        fn(tms[:, :, :], psb()[0:NS, 0:384].rearrange("s (q f) -> s q f", q=3), ACT.Copy).then_inc(drained["scalar"], 1)
                        act.wait_ge(drained["scalar"], n_taken["n"])
                        act.wait_ge(filled["scalar"], take())
                        fn(S[5][:, c, NPR:T], psb()[:, 0:NS], ACT.Copy).then_inc(drained["scalar"], 1)
                        act.wait_ge(drained["scalar"], n_taken["n"])
                        hear_state_out()
                        for q in range(2):
                            act.wait_ge(filled["scalar"], take())
                            fn(sout[0:64, q * 512:(q + 1) * 512], psb()[0:64, :], ACT.Copy).then_inc(drained["scalar"], 1)
                            act.wait_ge(drained["scalar"], n_taken["n"])
                        so = sout[0:64, :].rearrange("v (b h k) -> v b h k", b=NB, h=2)
                        for hh in range(2):
                            act.dma_start(OUT["sample_wkv"][j, :, 2 * c + hh].rearrange("b v k -> v b k"),
                                          so[:, :, hh, :]).then_inc(sem("sample_state_out"), 16)
                        state["out"] += 32
                for c in range(KC):
                    act.wait_ge(drained["vector"], mark["mean", j, c] + 1)
                    fn(SQ[:, c, :], S[5][:, c, :], ACT.Square).then_inc(signal("square_ready"), 1)
                head_rstd(H, 1.0 / 64, 1)
                out_projection()
                rms()

            def gdn():
                pre_norm()
                take_hist(72)
                lead = GW - 1
                dst = (S[1], S[4], S[2])

                def qkv(n):
                    act.wait_ge(sem("gconv"), after(act, "gconv"))
                    cv = buf(4 + n % 4, lead)
                    d = dst[n // KC][:, n % KC, :]
                    ins = two_part(d[:, 0:NPR], d[:, NPR:T].rearrange("p (b t) -> p b t", b=NB), cv[:, 0:NPR],
                                   cv[:, lead + NPR:span(lead)].rearrange("p (b t) -> p b t", b=NB)[:, :, 0:NT], ACT.Silu)
                    ins.then_inc(signal("qkv_ready"), 1)
                    act.wait_ge(sem("qkv_ready"), told["qkv_ready"])

                for n in range(GT):
                    act.wait_ge(filled["scalar"], take())
                    if n >= 4:
                        act.wait_ge(sem("saved"), after(act, "saved"))
                    dp, ds = split(buf(n % 4, lead), lead)
                    two_part(dp, ds, psb()[:, 0:NPR], psb()[:, NPR:T].rearrange("p (b t) -> p b t", b=NB), ACT.Copy).then_inc(drained["scalar"], 1)
                    act.wait_ge(drained["scalar"], n_taken["n"])
                    if n >= 2:
                        qkv(n - 2)
                qkv(GT - 2)
                qkv(GT - 1)
                act.wait_ge(sem("saved"), after(act, "saved", 4))
                for c in range(KC):
                    evac(S[8][:, c, :], ACT.Silu)
                hear_state_out()
                evac(g8[:, 0, :], ACT.Sigmoid, m=8)
                evac(g8[:, 1, :], ACT.Identity, gpar[:, 1:2], m=8)
                fn(g8[:, 2, :], g8[:, 1, :], ACT.Abs).then_inc(signal("scalar_chain"), 1)
                act.wait_ge(sem("scalar_chain"), told["scalar_chain"])
                fn(g8[:, 2, :], g8[:, 2, :], ACT.Exp, scale=-1.0).then_inc(signal("scalar_chain"), 1)
                act.wait_ge(sem("scalar_chain"), told["scalar_chain"])
                fn(g8[:, 2, :], g8[:, 2, :], ACT.Ln, bias=1.0).then_inc(signal("softplus_ready"), 1)
                act.wait_ge(sem("softplus_ready"), told["softplus_ready"])
                conv_state_out(OUT["prompt_gdn_conv"][0], OUT["sample_gdn_conv"][0], 72, 3)
                squares(S[1])
                head_rstd(S[3], 1.0, 0)
                squares(S[4])
                head_rstd(SQ, 1.0, 0)
                act.wait_ge(filled["scalar"], take())
                fn(tb[:, 0:2, :], psb()[:, 0:32].rearrange("p (b q) -> p b q", b=2), ACT.Copy)
                fn(tb[0:NS, 2, :], psb()[0:NS, 32:48], ACT.Copy).then_inc(drained["scalar"], 1)
                act.wait_ge(drained["scalar"], n_taken["n"])
                fn(neg[:, 0:2, :], tb[:, 0:2, 8:16], ACT.Exp)
                fn(neg[0:NS, 2, :], tb[0:NS, 2, 8:16], ACT.Exp).then_inc(signal("scalar_chain"), 1)
                act.wait_ge(sem("scalar_chain"), told["scalar_chain"])
                fn(neg[:, 0:2, :], neg[:, 0:2, :], ACT.Copy, scale=-1.0)
                fn(neg[0:NS, 2, :], neg[0:NS, 2, :], ACT.Copy, scale=-1.0).then_inc(signal("scalar_chain"), 1)
                act.wait_ge(sem("scalar_chain"), told["scalar_chain"])
                for h in range(8):
                    evac(S[6][:, h, :])
                act.wait_ge(sem("qk_done"), after(act, "qk_done"))
                fn(S[3], S[6], ACT.Exp).then_inc(signal("eg_ready"), 1)
                act.wait_ge(sem("eg_ready"), told["eg_ready"])
                hear_conv_out()
                for r in range(2):
                    for g in range(2):
                        for hh in range(2):
                            act.wait_ge(filled["scalar"], take())
                            fn(tm[:, g, hh * 512:(hh + 1) * 512], psb(), ACT.Copy).then_inc(drained["scalar"], 1)
                            act.wait_ge(drained["scalar"], n_taken["n"])
                    for g in range(2):
                        act.wait_ge(sem("exponents_ready"), after(act, "exponents_ready"))
                        fn(ysb[:, g, :], ysb[:, g, :], ACT.Exp).then_inc(signal("decays_exp"), 1)
                        act.wait_ge(sem("decays_exp"), told["decays_exp"])
                    for b in range(2):
                        for g in range(2):
                            act.wait_ge(filled["scalar"], take())
                            for hh in range(2):
                                h = 4 * r + 2 * g + hh
                                ins = fn(nu[:, g, hh * P:(hh + 1) * P], psb()[:, hh * P:(hh + 1) * P], ACT.Copy,
                                         scale=tb[:, b, h:h + 1])
                            ins.then_inc(drained["scalar"], 1)
                            act.wait_ge(drained["scalar"], n_taken["n"])
                        for g in range(2):
                            act.wait_ge(filled["scalar"], take())
                            fn(S[5][:, 4 * r + 2 * g:4 * r + 2 * g + 2, b * P:(b + 1) * P],
                                     psb()[:, 0:256].rearrange("p (h t) -> p h t", h=2), ACT.Copy).then_inc(drained["scalar"], 1)
                            act.wait_ge(drained["scalar"], n_taken["n"])
                    for g in range(2):
                        act.wait_ge(drained["vector"], mark["gstate", r, 1, g] + 1)
                        for hh in range(2):
                            act.dma_start(OUT["prompt_gdn_S"][0, 0, 4 * r + 2 * g + hh],
                                          (sp, spo)[hh][:, g, :]).then_inc(sem("prompt_state_out"), 16)
                            state["pout"] += 16
                    for g in range(2):
                        for hh in range(2):
                            h = 4 * r + 2 * g + hh
                            act.wait_ge(sem("sample_exponents"), after(act, "sample_exponents"))
                            fn(ms[:, 1, 0, :], ms[:, 1, 0, :], ACT.Exp).then_inc(signal("sample_decays"), 1)
                            act.wait_ge(sem("sample_decays"), told["sample_decays"])
                            act.wait_ge(filled["scalar"], take())
                            fn(tms[:, 0:2, :], psb()[0:NS, 0:256].rearrange("s (q f) -> s q f", q=2), ACT.Copy).then_inc(drained["scalar"], 1)
                            act.wait_ge(drained["scalar"], n_taken["n"])
                            act.wait_ge(filled["scalar"], take())
                            fn(S[5][:, h, NPR:T], psb()[:, 0:NS], ACT.Copy).then_inc(drained["scalar"], 1)
                            act.wait_ge(drained["scalar"], n_taken["n"])
                            sample_out(OUT["sample_gdn_S"], "gdn", h)
                finish_heads()

            def sample_out(out, kind, h):
                act.wait_ge(drained["vector"], mark["sraw", kind, h] + 1)
                act.dma_start(out[0, :, h].rearrange("b k v -> k b v"),
                              sout[:, :].rearrange("p (b v) -> p b v", b=NB)).then_inc(sem("sample_state_out"), 16)
                state["out"] += 16

            def finish_heads():
                squares(S[5])
                head_rstd(H, 1.0 / P, 0)
                out_projection()
                rms()

            def hgrn():
                pre_norm()
                for c in range(KC):
                    evac(S[0][:, c, :], ACT.Silu)
                for c in range(KC):
                    evac(S[1][:, c, :], ACT.Sigmoid)
                for c in range(KC):
                    evac(S[4][:, c, :])
                for c in range(KC):
                    evac(S[8][:, c, :], ACT.Silu)
                act.wait_ge(sem("f_ready"), after(act, "f_ready"))
                fn(S[1], S[1], ACT.Ln).then_inc(signal("log_f_ready"), 1)
                act.wait_ge(sem("log_f_ready"), told["log_f_ready"])
                act.wait_ge(sem("cumulated"), after(act, "cumulated"))
                fn(S[5], S[3], ACT.Exp).then_inc(signal("exp_cumulated"), 1)
                act.wait_ge(sem("exp_cumulated"), told["exp_cumulated"])
                act.wait_ge(sem("to_end_ready"), after(act, "to_end_ready"))
                fn(S[6], S[6], ACT.Exp).then_inc(signal("exp_to_end"), 1)
                act.wait_ge(sem("exp_to_end"), told["exp_to_end"])
                for l in range(1, LEVELS + 1):
                    act.wait_ge(sem("distance_ready"), after(act, "distance_ready"))
                    e = S[7] if l <= 2 else S[7][:, :, 0:NPR]
                    fn(e, e, ACT.Abs).then_inc(signal("scalar_chain"), 1)
                    act.wait_ge(sem("scalar_chain"), told["scalar_chain"])
                    fn(e, e, ACT.Exp, scale=-1.0).then_inc(signal("distance_exp"), 1)
                    act.wait_ge(sem("distance_exp"), told["distance_exp"])
                hear_conv_out()
                for h in range(8):
                    g = h % 2
                    act.wait_ge(filled["scalar"], take())
                    fn(tm[:, g, 0:512], psb(), ACT.Copy).then_inc(drained["scalar"], 1)
                    act.wait_ge(drained["scalar"], n_taken["n"])
                    act.wait_ge(filled["scalar"], take())
                    fn(tms[:, 0:2, :], psb()[0:NS, 0:256].rearrange("s (q f) -> s q f", q=2), ACT.Copy).then_inc(drained["scalar"], 1)
                    act.wait_ge(drained["scalar"], n_taken["n"])
                    for b in range(2):
                        act.wait_ge(filled["scalar"], take())
                        fn(S[2][:, h, b * P:(b + 1) * P], psb()[:, 0:P], ACT.Copy).then_inc(drained["scalar"], 1)
                        act.wait_ge(drained["scalar"], n_taken["n"])
                    act.wait_ge(filled["scalar"], take())
                    fn(S[2][:, h, NPR:T], psb()[:, 0:NS], ACT.Copy).then_inc(drained["scalar"], 1)
                    act.wait_ge(drained["scalar"], n_taken["n"])
                    act.wait_ge(drained["vector"], mark["hstate", h] + 1)
                    act.dma_start(OUT["prompt_hgrn_S"][0, 0, h], sp[:, g, :]).then_inc(sem("prompt_state_out"), 16)
                    state["pout"] += 16
                    sample_out(OUT["sample_hgrn_S"], "hgrn", h)
                squares(S[2])
                head_rstd(H, 1.0 / P, 0)
                out_projection()
                rms()

            act.wait_ge(sem("constants_ready"), after(act, "constants_ready"))
            for n, rows in enumerate(PARAM_ROWS):
                act.wait_ge(filled["scalar"], take())
                fn(pv[:, n, 0:rows], psb()[:, 0:rows], ACT.Copy).then_inc(drained["scalar"], 1)
                act.wait_ge(drained["scalar"], n_taken["n"])
            act.wait_ge(sem("gate_params_landed"), after_dma(act, "gate_params_landed", 2))
            fn(gpar[:, 2:3], gpar[:, 0:1], ACT.Exp).then_inc(signal("scalar_chain"), 1)
            act.wait_ge(sem("scalar_chain"), told["scalar_chain"])
            fn(gpar[:, 2:3], gpar[:, 2:3], ACT.Copy, scale=-1.0).then_inc(signal("scalar_chain"), 1)
            act.wait_ge(sem("scalar_chain"), told["scalar_chain"])
            act.wait_ge(sem("lb_shifted"), after(act, "lb_shifted"))
            fn(lb[:, 0:4, :], lb[:, 0:4, :], ACT.Exp).then_inc(signal("lb_exp"), 1)
            act.wait_ge(sem("lb_exp"), told["lb_exp"])
            for blk, n in enumerate((P, P, NS)):
                for q in range(2):
                    act.wait_ge(filled["scalar"], take())
                    fn(X[:, 4 * q:4 * q + 4, blk * P:blk * P + n],
                             psb().rearrange("p (i t) -> p i t", i=4)[:, :, 0:n], ACT.Copy).then_inc(drained["scalar"], 1)
                    act.wait_ge(drained["scalar"], n_taken["n"])
            squares(X)
            first = [True]
            real_pre = pre_norm

            def pre_norm():
                if first[0]:
                    first[0] = False
                    rms()
                else:
                    real_pre()

            rwkv(0)
            ffn(0)
            gdn()
            ffn(1)
            hgrn()
            ffn(2)
            rwkv(1)
            ffn(3)
            y = tm[:, :, :]
            hear_conv_out()
            for blk, n in enumerate((P, P, NS)):
                g = blk % 2
                if blk == 2:
                    act.wait_ge(sem("y_out"), 32)
                for q in range(2):
                    act.wait_ge(filled["scalar"], take())
                    fn(tm[0:n, g, q * 512:(q + 1) * 512], psb()[0:n, :], ACT.Copy).then_inc(drained["scalar"], 1)
                    act.wait_ge(drained["scalar"], n_taken["n"])
                dst = OUT["y_prompt"][0, blk * P:blk * P + n] if blk < 2 else OUT["y_sample"].rearrange("b t f -> (b t) f")
                act.dma_start(dst, tm[0:n, g, :]).then_inc(sem("y_out"), 16)
            act.wait_ge(sem("y_out"), 48)
            hear_state_out()
            hear_prompt_out()

        @block.vector
        def _(dve):
            V = nc.vector
            n_taken = {"n": 0}
            state = {"out": 0}

            def take():
                n_taken["n"] += 1
                return n_taken["n"]

            def psb():
                return bk[vec_bank[n_taken["n"] - 1]]

            def stt(out, a, s, b, o0=ALU.mult, o1=ALU.mult):
                return V.scalar_tensor_tensor(out=out, in0=a, scalar=s, in1=b, op0=o0, op1=o1)

            def tt(out, a, b, op=ALU.mult):
                return V.tensor_tensor(out, a, b, op)

            def ts(out, a, s1, s2=None, o0=ALU.mult, o1=None):
                if s2 is None:
                    return V.tensor_scalar(out, a, s1, None, o0)
                return V.tensor_scalar(out, a, s1, s2, o0, o1)

            def bc(ap, shape):
                return ap.to_broadcast(list(shape))

            def pre_norm(kind, i, name):
                dve.wait_ge(sem("rstd_ready"), after(dve, "rstd_ready"))
                for c in range(KC):
                    ins = stt(H[:, c, :], X[:, c, :], pcol(kind, i, c), rstd[:, :])
                    if name:
                        ins.then_inc(signal(name), 1)
                if not name:
                    name = "h_whole"
                    ins.then_inc(signal(name), 1)
                dve.wait_ge(sem(name), told[name])

            def post_norm(kind, i):
                dve.wait_ge(sem("rstd_ready"), after(dve, "rstd_ready"))
                for c in range(KC):
                    stt(SQ[:, c, :], S[3][:, c, :], pcol(kind, i, c), rstd[:, :]).then_inc(signal("vector_chain"), 1)
                    dve.wait_ge(sem("vector_chain"), told["vector_chain"])
                    tt(X[:, c, :], X[:, c, :], SQ[:, c, :], ALU.add).then_inc(signal("x_ready"), 1)
                dve.wait_ge(sem("x_ready"), told["x_ready"])

            def conv(n_in, n_out, width, coef, name):
                lead = width - 1
                n = span(lead) - lead
                e, o = buf(n_in, lead), buf(n_out, lead)
                ts(o[:, 0:n], e[:, 0:n], coef(0)).then_inc(signal("vector_chain"), 1)
                dve.wait_ge(sem("vector_chain"), told["vector_chain"])
                for j in range(1, width):
                    ins = stt(o[:, 0:n], e[:, j:j + n], coef(j), o[:, 0:n], ALU.mult, ALU.add)
                    if j < width - 1:
                        ins.then_inc(signal("vector_chain"), 1)
                        dve.wait_ge(sem("vector_chain"), told["vector_chain"])
                ins.then_inc(signal(name), 1)
                dve.wait_ge(sem(name), told[name])

            def ffn(i):
                pre_norm("ffn_pre", i, "h_ready")
                lead = FW - 1
                y = flat("A0", 3)[:, 0:FC * T].rearrange("p (c t) -> p c t", c=FC)

                def product(p):
                    for q in range(2):
                        dve.wait_ge(sem("silu_ready"), after(dve, "silu_ready"))
                        a, g = buf(4 + (p % 2) * 4 + q, lead), buf(4 + (p % 2) * 4 + 2 + q, lead)
                        d = y[:, 2 * p + q, :]
                        tt(d[:, 0:NPR], a[:, 0:NPR], g[:, 0:NPR])

                        def seqs(ap):
                            return ap[:, lead + NPR:span(lead)].rearrange("p (b t) -> p b t", b=NB)[:, :, 0:NT]

                        tt(d[:, NPR:T].rearrange("p (b t) -> p b t", b=NB), seqs(a), seqs(g)).then_inc(signal("y_ready"), 1)
                        dve.wait_ge(sem("y_ready"), told["y_ready"])

                for p in range(FPAIR):
                    for half in range(2):
                        if half and p:
                            product(p - 1)
                        for q in range(2):
                            dve.wait_ge(drained["scalar"], mark[("up", i, p, half), q] + 1)
                            dve.wait_ge(sem("hist_in"), after(dve, "hist_in"))
                            conv(half * 2 + q, 4 + (p % 2) * 4 + half * 2 + q, FW,
                                 lambda t: fconv(i, t, half * FC + 2 * p + q), ("value_conv", "gate_conv")[half])
                product(FPAIR - 1)
                post_norm("ffn_post", i)

            def blocks(ap):
                return ap[:, :, 0:NPR].rearrange("p c (b t) -> p c b t", b=2)

            def seqs(ap):
                return ap[:, :, NPR:T].rearrange("p c (b t) -> p c b t", b=NB)

            def invert():
                for l in range(LEVELS):
                    for g in range(2):
                        dve.wait_ge(filled["vector"], take())
                        tt(ysb[:, g, :].rearrange("p (m t) -> p m t", m=4), psb().rearrange("p (m t) -> p m t", m=4),
                                 low[:, l:l + 1, :].to_broadcast([P, 4, P])).then_inc(drained["vector"], 1)
                        dve.wait_ge(drained["vector"], n_taken["n"])
                    for g in range(2):
                        dve.wait_ge(filled["vector"], take())
                        t = T2[:, g].rearrange("p m q t -> p (m q t)")
                        tt(t, t, wide[1 + g][:, :], ALU.subtract).then_inc(drained["vector"], 1)
                        dve.wait_ge(drained["vector"], n_taken["n"])

            def start_inverse(g):
                V.tensor_copy(T2[:, g].rearrange("p m q t -> p (m q) t"),
                                        ident[:, None, :].to_broadcast([P, 8, P])).then_inc(signal(f"t_ready{g}"), 1)
                dve.wait_ge(sem(f"t_ready{g}"), told[f"t_ready{g}"])

            def rwkv(j):
                pre_norm("mix_pre", 3 * j, None)
                M = [S[1], S[2]]
                Dx = S[0]
                tt(Dx[:, :, 1:NPR], H[:, :, 0:NPR - 1], H[:, :, 1:NPR], ALU.subtract)
                ts(Dx[:, :, 0:1], H[:, :, 0:1], -1.0)
                tt(seqs(Dx)[:, :, :, 1:NT], seqs(H)[:, :, :, 0:NT - 1], seqs(H)[:, :, :, 1:NT], ALU.subtract)
                tt(seqs(Dx)[:, :, :, 0], shiftT[:, j].rearrange("p b c -> p c b"), seqs(H)[:, :, :, 0], ALU.subtract).then_inc(signal("vector_chain"), 1)
                dve.wait_ge(sem("vector_chain"), told["vector_chain"])
                for i, s in enumerate(MIX_ORDER):
                    if i >= 2:
                        dve.wait_ge(filled["scalar"], mark["mix_used", j, i - 2] + 1)
                    for c in range(KC):
                        ins = stt(M[i % 2][:, c, :], Dx[:, c, :], pcol("mix", j * 6 + s, c), H[:, c, :], ALU.mult, ALU.add)
                        ins.then_inc(signal("mix_ready"), 1)
                    if j and i == 1:
                        dve.wait_ge(drained["scalar"], mark[("v2", j, KC - 1), 0] + 1)
                        dve.wait_ge(sem("v_first_back"), 16)
                        tt(S[7], S[8], S[3], ALU.subtract).then_inc(signal("vector_chain"), 1)
                        dve.wait_ge(sem("vector_chain"), told["vector_chain"])
                        tt(S[7], S[7], SQ).then_inc(signal("vector_chain"), 1)
                        dve.wait_ge(sem("vector_chain"), told["vector_chain"])
                        tt(S[3], S[3], S[7], ALU.add).then_inc(signal("v_mixed"), 1)
                        dve.wait_ge(sem("v_mixed"), told["v_mixed"])
                dve.wait_ge(sem("mix_ready"), told["mix_ready"])
                K, B, KK, Vv, R = S[4], S[1], S[0], S[3], S[5]
                for c in range(KC):
                    dve.wait_ge(drained["scalar"], mark[("k", j), KC - 1] + 1)
                    ins = ts(KK[:, c, :], K[:, c, :], pcol("k_k", j, c))
                    ins.then_inc(signal("kk_raw"), 1)
                dve.wait_ge(drained["scalar"], mark[("a2", j, KC - 1), 0] + 1)
                dve.wait_ge(filled["scalar"], mark["mix_used", j, 5] + 1)
                for c in range(KC):
                    ins = ts(S[2][:, c, :], S[7][:, c, :], pcol("k_a", j, c), omka[:, j, c:c + 1], ALU.mult, ALU.add)
                ins.then_inc(signal("vector_chain"), 1)
                dve.wait_ge(sem("vector_chain"), told["vector_chain"])
                tt(K, K, S[2]).then_inc(signal("vector_chain"), 1)
                dve.wait_ge(sem("vector_chain"), told["vector_chain"])
                dve.wait_ge(sem("rk_ready"), after(dve, "rk_ready"))
                tt(KK, KK, S[1]).then_inc(signal("vector_chain"), 1)
                dve.wait_ge(sem("vector_chain"), told["vector_chain"])
                tt(B, KK, S[7]).then_inc(signal("vector_chain"), 1)
                dve.wait_ge(sem("vector_chain"), told["vector_chain"])
                for c in range(KC):
                    stt(SQ[:, c, :], R[:, c, :], pcol("r_k", j, c), K[:, c, :]).then_inc(signal("bonus_product"), 1)
                ts(S[6], S[6], -RW_DECAY).then_inc(signal("vector_chain"), 1)
                dve.wait_ge(sem("vector_chain"), told["vector_chain"])
                for c in range(KC):
                    ins = V.tensor_tensor_scan(H[:, c, :], seg[:, :], S[6][:, c, :], 0.0, ALU.mult, ALU.add)
                ins.then_inc(signal("vector_chain"), 1)
                dve.wait_ge(sem("vector_chain"), told["vector_chain"])
                for c in range(KC):
                    dve.wait_ge(filled["vector"], take())
                    tt(S[2][:, c, :], psb()[:, 0:T], Vv[:, c, :]).then_inc(drained["vector"], 1)
                    dve.wait_ge(drained["vector"], n_taken["n"])
                V.tensor_copy(cen[:, 0], H[:, :, 63:NPR:128]).then_inc(signal("vector_chain"), 1)
                dve.wait_ge(sem("vector_chain"), told["vector_chain"])
                tt(blocks(H), blocks(H), cen[:, 0][:, :, :, None].to_broadcast([P, KC, 2, P]), ALU.subtract).then_inc(signal("vector_chain"), 1)
                dve.wait_ge(sem("vector_chain"), told["vector_chain"])
                tt(SQ, H, S[6], ALU.subtract).then_inc(signal("ge_ready"), 1)
                dve.wait_ge(sem("ge_ready"), told["ge_ready"])
                dve.wait_ge(sem("e_excl"), after(dve, "e_excl"))
                tt(ARp[:, :, :, 0, :], blocks(KK), blocks(SQ))
                tt(ARs[:, :, 0, :], KK[:, :, NPR:T], SQ[:, :, NPR:T]).then_inc(signal("a_done"), 1)
                dve.wait_ge(sem("a_done"), told["a_done"])
                dve.wait_ge(sem("e_incl"), after(dve, "e_incl"))
                tt(ARp[:, :, :, 1, :], blocks(R), blocks(SQ))
                tt(ARs[:, :, 1, :], R[:, :, NPR:T], SQ[:, :, NPR:T])
                V.tensor_copy(cen[:, 2], SQ[:, :, 127:NPR:128])
                V.tensor_copy(els[:, :, :], seqs(SQ)[:, :, :, NT - 1]).then_inc(signal("vector_chain"), 1)
                dve.wait_ge(sem("vector_chain"), told["vector_chain"])
                dve.wait_ge(sem("e_neg"), after(dve, "e_neg"))
                tt(K, K, H)
                if j:
                    dve.wait_ge(sem("prompt_state_out"), 16 * 32)
                V.memset(sp[:, :, :], 0.0)
                V.memset(ams[:, :, :, :], 0.0)
                V.memset(rms_[:, :, :], 0.0)
                tt(B, B, H).then_inc(signal("operands_ready"), 1)
                dve.wait_ge(sem("operands_ready"), told["operands_ready"])
                for r in range(4):
                    for g in range(2):
                        for m in range(4):
                            dve.wait_ge(filled["vector"], take())
                            tt(MX[:, g, m].rearrange("p q t -> p (q t)"), psb(),
                                     mask4[:, :, :].rearrange("p q t -> p (q t)")).then_inc(drained["vector"], 1)
                            dve.wait_ge(drained["vector"], n_taken["n"])
                        start_inverse(g)
                    invert()
                    for b in range(2):
                        for g in range(2):
                            dve.wait_ge(filled["vector"], take())
                            V.tensor_copy(rs[:, g, 0:P], psb()[:, 0:P]).then_inc(drained["vector"], 1)
                            dve.wait_ge(drained["vector"], n_taken["n"])
                        for g in range(2):
                            c = 2 * r + g
                            dve.wait_ge(filled["vector"], take())
                            if b:
                                ts(sp[:, g, :], sp[:, g, :], cen[:, 2, c, 1:2]).then_inc(signal("vector_chain"), 1)
                                dve.wait_ge(sem("vector_chain"), told["vector_chain"])
                            for hh in range(2):
                                rows = slice(64 * hh, 64 * hh + 64)
                                src = psb()[rows, hh * 64:hh * 64 + 64]
                                if b:
                                    ins = stt(sp[rows, g, rows], src, cen[rows, 2, c, 1:2], sp[rows, g, rows],
                                              ALU.mult, ALU.add)
                                else:
                                    ins = ts(sp[rows, g, rows], src, cen[rows, 2, c, 0:1], cen[rows, 1, c, 1:2],
                                             ALU.mult, ALU.mult)
                            ins.then_inc(drained["vector"], 1)
                            dve.wait_ge(drained["vector"], n_taken["n"])
                    for g in range(2):
                        rwkv_sample(j, 2 * r + g)
                for c in range(KC):
                    dve.wait_ge(filled["vector"], take())
                    stt(S[5][:, c, :], psb()[:, 0:T], -1.0 / 64, S[5][:, c, :], ALU.mult, ALU.add).then_inc(drained["vector"], 1)
                    dve.wait_ge(drained["vector"], n_taken["n"])
                dve.wait_ge(sem("rk_ready"), after(dve, "rk_ready"))
                tt(S[5], S[5], H).then_inc(signal("vector_chain"), 1)
                dve.wait_ge(sem("vector_chain"), told["vector_chain"])
                for c in range(KC):
                    ins = ts(S[5][:, c, :], S[5][:, c, :], pcol("lnx_w", j, c), pcol("lnx_b", j, c), ALU.mult, ALU.add)
                ins.then_inc(signal("vector_chain"), 1)
                dve.wait_ge(sem("vector_chain"), told["vector_chain"])
                tt(S[5], S[5], S[2], ALU.add).then_inc(signal("vector_chain"), 1)
                dve.wait_ge(sem("vector_chain"), told["vector_chain"])
                for c in range(KC):
                    tt(S[5][:, c, :], S[5][:, c, :], S[8][:, c, :]).then_inc(signal("mixer_out"), 1)
                post_norm("mix_post", 3 * j)

            def spread_rows(dst, src, n):
                return tt(dst.rearrange("s (b v) -> s b v", b=NB), src[:, None, :].to_broadcast([NS, NB, n]),
                          rmask[:, :, None].to_broadcast([NS, NB, n]))

            def rwkv_sample(j, c):
                for hh in range(2):
                    rows = slice(64 * hh, 64 * hh + 64)
                    V.tensor_copy(rms_[rows, hh, :], ARs[rows, c, 1, :])
                    ins = tt(ams[rows, hh], ARs[rows, c, 0, None, :].to_broadcast([64, NB, NS]), bmask[rows])
                ins.then_inc(signal("spread_ready"), 1)
                dve.wait_ge(sem("spread_ready"), told["spread_ready"])
                for hh in range(2):
                    dve.wait_ge(filled["vector"], take())
                    tt(ms[:, hh].rearrange("s q t -> s (q t)"), psb()[0:NS, 0:128],
                             samp4[:, :, :].rearrange("s q t -> s (q t)")).then_inc(drained["vector"], 1)
                    dve.wait_ge(drained["vector"], n_taken["n"])
                dve.wait_ge(filled["vector"], take())
                V.tensor_copy(us[:, 0, :], psb()[0:NS, 0:P]).then_inc(drained["vector"], 1)
                dve.wait_ge(drained["vector"], n_taken["n"])
                nilpotent()
                dve.wait_ge(drained["scalar"], mark["tms", "rwkv", j, c] + 1)
                for hh in range(2):
                    rows = slice(64 * hh, 64 * hh + 64)
                    spread_rows(vms[:, 0, :], tms[:, 0, hh * 64:hh * 64 + 64], 64)
                    spread_rows(vms[:, 1, :], us[:, 3, hh * 64:hh * 64 + 64], 64).then_inc(signal("values_spread"), 1)
                    dve.wait_ge(sem("values_spread"), told["values_spread"])
                    dve.wait_ge(filled["vector"], take())
                    tt(sst[rows, 1, :], psb()[rows, :], sst[rows, 0, :], ALU.add).then_inc(drained["vector"], 1)
                    dve.wait_ge(drained["vector"], n_taken["n"])
                    s3 = sst[rows, 1, :].rearrange("p (b v) -> p b v", b=NB)
                    ins = tt(s3, s3, els[rows, c, :, None].to_broadcast([64, NB, 64]))
                    if hh:
                        ins.then_inc(signal("sample_state_new"), 1)
                        dve.wait_ge(sem("sample_state_new"), told["sample_state_new"])
                    else:
                        ins.then_inc(signal("vector_chain"), 1)
                        dve.wait_ge(sem("vector_chain"), told["vector_chain"])

            def nilpotent():
                dve.wait_ge(filled["vector"], take())
                V.tensor_copy(us[:, 1, :], psb()[0:NS, 0:P]).then_inc(drained["vector"], 1)
                dve.wait_ge(drained["vector"], n_taken["n"])
                dve.wait_ge(filled["vector"], take())
                tt(us[:, 2, :], psb()[0:NS, 0:P], us[:, 0, :], ALU.add).then_inc(drained["vector"], 1)
                dve.wait_ge(drained["vector"], n_taken["n"])
                dve.wait_ge(filled["vector"], take())
                tt(us[:, 3, :], psb()[0:NS, 0:P], us[:, 2, :], ALU.subtract).then_inc(drained["vector"], 1)
                dve.wait_ge(drained["vector"], n_taken["n"])

            def gdn():
                pre_norm("mix_pre", 1, "h_ready")
                for n in range(GT):
                    dve.wait_ge(drained["scalar"], mark["gin", n] + 1)
                    dve.wait_ge(sem("hist_in"), after(dve, "hist_in"))
                    if n >= 4:
                        dve.wait_ge(sem("qkv_ready"), after(dve, "qkv_ready"))
                    conv(n % 4, 4 + n % 4, GW, lambda t: gconv(t, n), "gconv")
                dve.wait_ge(sem("qkv_ready"), after(dve, "qkv_ready", 4))
                dve.wait_ge(sem("softplus_ready"), after(dve, "softplus_ready"))
                stt(g8[:, 1, :], g8[:, 1, :], 0.0, g8[:, 2, :], ALU.max, ALU.add).then_inc(signal("vector_chain"), 1)
                dve.wait_ge(sem("vector_chain"), told["vector_chain"])
                ts(g8[:, 1, :], g8[:, 1, :], gpar[:, 2:3]).then_inc(signal("vector_chain"), 1)
                dve.wait_ge(sem("vector_chain"), told["vector_chain"])
                V.tensor_tensor_scan(g8[:, 2, :], seg[0:8, :], g8[:, 1, :], 0.0, ALU.mult, ALU.add).then_inc(signal("decay_ready"), 1)
                dve.wait_ge(sem("decay_ready"), told["decay_ready"])
                Q, K, Vv, QG, EG, GR = S[1], S[4], S[2], S[7], S[3], S[6]
                dve.wait_ge(sem("rk_ready"), after(dve, "rk_ready"))
                stt(Q, Q, float(P) ** -0.5, S[3]).then_inc(signal("vector_chain"), 1)
                dve.wait_ge(sem("vector_chain"), told["vector_chain"])
                dve.wait_ge(sem("rk_ready"), after(dve, "rk_ready"))
                tt(K, K, SQ).then_inc(signal("qk_done"), 1)
                dve.wait_ge(sem("qk_done"), told["qk_done"])
                dve.wait_ge(sem("eg_ready"), after(dve, "eg_ready"))
                tt(QG, Q, EG).then_inc(signal("operands_ready"), 1)
                dve.wait_ge(sem("operands_ready"), told["operands_ready"])
                for r in range(2):
                    for g in range(2):
                        for m in range(4):
                            hh, b = divmod(m, 2)
                            h = 4 * r + 2 * g + hh
                            ins = ts(ysb[:, g, m * P:(m + 1) * P], GR[:, h, b * P:(b + 1) * P], tb[:, b, 8 + h:9 + h], 0.0,
                                     ALU.subtract, ALU.min)
                        ins.then_inc(signal("exponents_ready"), 1)
                        dve.wait_ge(sem("exponents_ready"), told["exponents_ready"])
                    for g in range(2):
                        dve.wait_ge(sem("decays_exp"), after(dve, "decays_exp"))
                        e = ysb[:, g, :].rearrange("p (m t) -> p m t", m=4)
                        V.tensor_copy(ed[:, g, :], e[:, :, P - 1])
                        for q in range(2):
                            ins = tt(MX[:, g, :, 2 + q, :], e, mask4[:, q:q + 1, :].to_broadcast([P, 4, P]))
                        ins.then_inc(signal("vector_chain"), 1)
                        dve.wait_ge(sem("vector_chain"), told["vector_chain"])
                        for m in range(4):
                            hh, b = divmod(m, 2)
                            h = 4 * r + 2 * g + hh
                            dve.wait_ge(filled["vector"], take())
                            stt(MX[:, g, m, 0, :], psb()[:, 0:P], tb[:, b, h:h + 1], MX[:, g, m, 2, :])
                            tt(MX[:, g, m, 1, :], psb()[:, P:2 * P], MX[:, g, m, 3, :]).then_inc(drained["vector"], 1)
                            dve.wait_ge(drained["vector"], n_taken["n"])
                        start_inverse(g)
                    invert()
                    for b in range(2):
                        if b:
                            for g in range(2):
                                tg = tm[:, g, :].rearrange("p (h b q f) -> p h b q f", h=2, b=2, q=2)
                                dve.wait_ge(drained["scalar"], mark["gtm", r, g] + 1)
                                dve.wait_ge(filled["vector"], take())
                                for hh in range(2):
                                    h = 4 * r + 2 * g + hh
                                    ins = stt(rs[:, g, hh * P:(hh + 1) * P], psb()[:, hh * P:(hh + 1) * P],
                                              neg[:, 1, h:h + 1], tg[:, hh, 1, 0, :], ALU.mult, ALU.add)
                                ins.then_inc(drained["vector"], 1)
                                dve.wait_ge(drained["vector"], n_taken["n"])
                        for g in range(2):
                            dve.wait_ge(drained["scalar"], mark["z", r, b, g] + 1)
                            for hh in range(2):
                                ins = ts(xd[:, g, hh * P:(hh + 1) * P], nu[:, g, hh * P:(hh + 1) * P],
                                         ed[:, g, 2 * hh + b:2 * hh + b + 1])
                            ins.then_inc(signal("xd_ready"), 1)
                            dve.wait_ge(sem("xd_ready"), told["xd_ready"])
                        for g in range(2):
                            dve.wait_ge(filled["vector"], take())
                            if b == 0 and r:
                                dve.wait_ge(sem("prompt_state_out"), 16 * 16 + 64)
                            if b == 0 and not r:
                                dve.wait_ge(sem("prompt_state_out"), 16 * 16)
                            for hh in range(2):
                                h = 4 * r + 2 * g + hh
                                src, st = psb()[:, hh * P:(hh + 1) * P], (sp, spo)[hh][:, g, :]
                                if b:
                                    ins = stt(st, st, EG[:, h, NPR - 1:NPR], src, ALU.mult, ALU.add)
                                else:
                                    ins = V.tensor_copy(st, src)
                            ins.then_inc(drained["vector"], 1)
                            dve.wait_ge(drained["vector"], n_taken["n"])
                    for g in range(2):
                        for hh in range(2):
                            gdn_sample(4 * r + 2 * g + hh)
                finish_heads(S[5], pv[:, 3, 33:34], 1)

            def finish_heads(o, w, i):
                dve.wait_ge(sem("rk_ready"), after(dve, "rk_ready"))
                for c in range(KC):
                    ins = stt(o[:, c, :], o[:, c, :], w, H[:, c, :])
                ins.then_inc(signal("vector_chain"), 1)
                dve.wait_ge(sem("vector_chain"), told["vector_chain"])
                for c in range(KC):
                    tt(S[5][:, c, :], o[:, c, :], S[8][:, c, :]).then_inc(signal("mixer_out"), 1)
                post_norm("mix_post", i)

            def state_stored():
                dve.wait_ge(sem("sample_state_out"), state["out"])

            def sample_update(decay):
                s3 = sraw[:, :].rearrange("p (b v) -> p b v", b=NB)
                o3 = sout[:, :].rearrange("p (b v) -> p b v", b=NB)
                dve.wait_ge(filled["vector"], take())
                state_stored()
                tt(o3, s3, decay.to_broadcast([P, NB, P])).then_inc(signal("vector_chain"), 1)
                dve.wait_ge(sem("vector_chain"), told["vector_chain"])
                tt(sout[:, :], sout[:, :], wide[2][:, :], ALU.add).then_inc(drained["vector"], 1)
                dve.wait_ge(drained["vector"], n_taken["n"])
                state["out"] += 16

            def gdn_sample(h):
                Q, K, Vv, QG, EG, GR = S[1], S[4], S[2], S[7], S[3], S[6]
                ts(ms[:, 1, 0, :], GR[0:NS, h, NPR:T], tb[0:NS, 2, 8 + h:9 + h], 0.0, ALU.subtract, ALU.min).then_inc(signal("sample_exponents"), 1)
                dve.wait_ge(sem("sample_exponents"), told["sample_exponents"])
                tt(ams[:, 0], K[:, h, None, NPR:T].to_broadcast([P, NB, NS]), bmask[:, :, :]).then_inc(signal("spread_ready"), 1)
                dve.wait_ge(sem("spread_ready"), told["spread_ready"])
                dve.wait_ge(sem("sample_decays"), after(dve, "sample_decays"))
                tt(ms[:, 1, 2:4, :], ms[:, 1, 0:1, :].to_broadcast([NS, 2, NS]), samp4[:, 0:2, :])
                tt(ms[:, 1, 1, :], ms[:, 1, 0, :], lastm[:, :]).then_inc(signal("vector_chain"), 1)
                dve.wait_ge(sem("vector_chain"), told["vector_chain"])
                V.reduce_sum(ed[0:NS, 2, 0:1], ms[:, 1, 1, :], AX_X).then_inc(signal("vector_chain"), 1)
                dve.wait_ge(sem("vector_chain"), told["vector_chain"])
                dve.wait_ge(filled["vector"], take())
                stt(ms[:, 0, 0, :], psb()[0:NS, 0:NS], tb[0:NS, 2, h:h + 1], ms[:, 1, 2, :])
                tt(ms[:, 0, 1, :], psb()[0:NS, NS:2 * NS], ms[:, 1, 3, :]).then_inc(drained["vector"], 1)
                dve.wait_ge(drained["vector"], n_taken["n"])
                dve.wait_ge(filled["vector"], take())
                dve.wait_ge(drained["scalar"], mark["tms", "gdn", h] + 1)
                stt(us[:, 0, :], psb()[0:NS, 0:P], neg[0:NS, 2, h:h + 1], tms[:, 0, :], ALU.mult, ALU.add).then_inc(drained["vector"], 1)
                dve.wait_ge(drained["vector"], n_taken["n"])
                nilpotent()
                ts(us[:, 3, :], us[:, 3, :], tb[0:NS, 2, h:h + 1], -1.0, ALU.mult, ALU.mult).then_inc(signal("x_scaled"), 1)
                dve.wait_ge(sem("x_scaled"), told["x_scaled"])
                ts(us[:, 1, :], us[:, 3, :], ed[0:NS, 2, 0:1]).then_inc(signal("vector_chain"), 1)
                dve.wait_ge(sem("vector_chain"), told["vector_chain"])
                spread_rows(vms[:, :, :].rearrange("s a b -> s (a b)"), us[:, 1, :], P).then_inc(signal("values_spread"), 1)
                dve.wait_ge(sem("values_spread"), told["values_spread"])
                sample_update(EG[:, h, NPR + NT - 1:T:NT][:, :, None])

            def hgrn():
                pre_norm("mix_pre", 2, "h_ready")
                Q, F, K, G, Vv, QG, KD, E = S[0], S[1], S[2], S[3], S[4], S[5], S[6], S[7]
                dve.wait_ge(drained["scalar"], mark["hin", 2 * KC - 1] + 1)
                for c in range(KC):
                    ins = ts(F[:, c, :], F[:, c, :], lb[:, 5, c:c + 1], lb[:, 4, c:c + 1], ALU.mult, ALU.add)
                ins.then_inc(signal("vector_chain"), 1)
                dve.wait_ge(sem("vector_chain"), told["vector_chain"])
                ts(K, F, -1.0, 1.0, ALU.mult, ALU.add).then_inc(signal("f_ready"), 1)
                dve.wait_ge(sem("f_ready"), told["f_ready"])
                dve.wait_ge(sem("log_f_ready"), after(dve, "log_f_ready"))
                for c in range(KC):
                    ins = V.tensor_tensor_scan(G[:, c, :], seg[:, :], F[:, c, :], 0.0, ALU.mult, ALU.add)
                ins.then_inc(signal("cumulated"), 1)
                dve.wait_ge(sem("cumulated"), told["cumulated"])
                V.memset(flat("A1"), 0.0)
                tt(blocks(KD), blocks(G)[:, :, :, P - 1:P].to_broadcast([P, KC, 2, P]), blocks(G), ALU.subtract)
                tt(seqs(KD), seqs(G)[:, :, :, NT - 1:NT].to_broadcast([P, KC, NB, NT]), seqs(G), ALU.subtract).then_inc(signal("to_end_ready"), 1)
                dve.wait_ge(sem("to_end_ready"), told["to_end_ready"])
                dve.wait_ge(sem("exp_cumulated"), after(dve, "exp_cumulated"))
                V.tensor_copy(cen[:, 2], QG[:, :, 127:NPR:128])
                V.tensor_copy(els[:, :, :], seqs(QG)[:, :, :, NT - 1]).then_inc(signal("vector_chain"), 1)
                dve.wait_ge(sem("vector_chain"), told["vector_chain"])
                tt(QG, QG, Q).then_inc(signal("vector_chain"), 1)
                dve.wait_ge(sem("vector_chain"), told["vector_chain"])
                dve.wait_ge(sem("exp_to_end"), after(dve, "exp_to_end"))
                dve.wait_ge(drained["scalar"], mark["hin", 4 * KC - 1] + 1)
                tt(KD, KD, K).then_inc(signal("level_operands"), 1)
                dve.wait_ge(sem("level_operands"), told["level_operands"])
                AT = flat("A1")[:, 0:2048].rearrange("p (n i t) -> p n i t", n=4, i=4)
                ATS = flat("A1")[0:NS, 2048:2304].rearrange("p (h t) -> p h t", h=8)

                def distances(l):
                    n = 1 << l
                    if l <= 2:
                        g = G.rearrange("p c t -> p (c t)").rearrange("p (b t) -> p b t", t=n)
                        e = E.rearrange("p c t -> p (c t)").rearrange("p (b t) -> p b t", t=n)
                        ins = tt(e, g, g[:, :, n // 2 - 1:n // 2].to_broadcast([P, KC * T // n, n]), ALU.subtract)
                    else:
                        g = G[:, :, 0:NPR].rearrange("p c (b t) -> p c b t", t=n)
                        e = E[:, :, 0:NPR].rearrange("p c (b t) -> p c b t", t=n)
                        ins = tt(e, g, g[:, :, :, n // 2 - 1:n // 2].to_broadcast([P, KC, NPR // n, n]), ALU.subtract)
                    ins.then_inc(signal("distance_ready"), 1)
                    dve.wait_ge(sem("distance_ready"), told["distance_ready"])

                for l in range(LEVELS + 1):
                    if l < LEVELS:
                        distances(l + 1)
                    m = ident[:, :] if l == 0 else upp[:, l - 1, :]
                    for n in range(4):
                        dve.wait_ge(filled["vector"], take())
                        V.copy_predicated(AT[:, n], m.bitcast(U32)[:, None, :].to_broadcast([P, 4, P]),
                                                psb().rearrange("p (i t) -> p i t", i=4)).then_inc(drained["vector"], 1)
                        dve.wait_ge(drained["vector"], n_taken["n"])
                    if l <= 2:
                        dve.wait_ge(filled["vector"], take())
                        V.copy_predicated(ATS, m[0:NS, 0:NS].bitcast(U32)[:, None, :].to_broadcast([NS, 8, NS]),
                                                psb()[0:NS, 0:256].rearrange("p (i t) -> p i t", i=8)).then_inc(drained["vector"], 1)
                        dve.wait_ge(drained["vector"], n_taken["n"])
                    if l < LEVELS:
                        dve.wait_ge(sem("distance_exp"), after(dve, "distance_exp"))
                        w = T if l + 1 <= 2 else NPR
                        tt(H[:, :, 0:w], Q[:, :, 0:w], E[:, :, 0:w])
                        tt(SQ[:, :, 0:w], K[:, :, 0:w], E[:, :, 0:w]).then_inc(signal("level_operands"), 1)
                        dve.wait_ge(sem("level_operands"), told["level_operands"])
                for h in range(8):
                    g = h % 2
                    for b in range(2):
                        dve.wait_ge(filled["vector"], take())
                        if b:
                            ins = stt(sp[:, g, :], sp[:, g, :], cen[:, 2, h, 1:2], psb()[:, 0:P], ALU.mult, ALU.add)
                        else:
                            dve.wait_ge(sem("prompt_state_out"), 16 * 16 + 16 * 8 + 16 * max(h - 1, 0))
                            ins = V.tensor_copy(sp[:, g, :], psb()[:, 0:P])
                        ins.then_inc(drained["vector"], 1)
                        dve.wait_ge(drained["vector"], n_taken["n"])
                    dve.wait_ge(drained["scalar"], mark["tms", "hgrn", h] + 1)
                    spread_rows(vms[:, :, :].rearrange("s a b -> s (a b)"), tms[:, 0, :], P).then_inc(signal("values_spread"), 1)
                    dve.wait_ge(sem("values_spread"), told["values_spread"])
                    sample_update(els[:, h, :, None])
                finish_heads(S[2], pv[:, 3, 32:33], 2)

            dve.wait_ge(sem("masks_ready"), after(dve, "masks_ready"))
            dve.wait_ge(drained["scalar"], 3 + 1)
            logits = pv[:, 3, 0:32].rearrange("p (l c) -> p l c", l=4)
            tt(lb[:, 6, :], logits[:, 0, :], logits[:, 1, :], ALU.max).then_inc(signal("vector_chain"), 1)
            dve.wait_ge(sem("vector_chain"), told["vector_chain"])
            tt(lb[:, 7, :], logits[:, 2, :], logits[:, 3, :], ALU.max).then_inc(signal("vector_chain"), 1)
            dve.wait_ge(sem("vector_chain"), told["vector_chain"])
            tt(lb[:, 6, :], lb[:, 6, :], lb[:, 7, :], ALU.max).then_inc(signal("vector_chain"), 1)
            dve.wait_ge(sem("vector_chain"), told["vector_chain"])
            tt(lb[:, 0:4, :], logits, lb[:, 6:7, :].to_broadcast([P, 4, KC]), ALU.subtract).then_inc(signal("lb_shifted"), 1)
            dve.wait_ge(sem("lb_shifted"), told["lb_shifted"])
            dve.wait_ge(sem("lb_exp"), after(dve, "lb_exp"))
            tt(lb[:, 4, :], lb[:, 1, :], lb[:, 2, :], ALU.add).then_inc(signal("vector_chain"), 1)
            dve.wait_ge(sem("vector_chain"), told["vector_chain"])
            tt(lb[:, 6, :], lb[:, 0, :], lb[:, 3, :], ALU.add).then_inc(signal("vector_chain"), 1)
            dve.wait_ge(sem("vector_chain"), told["vector_chain"])
            tt(lb[:, 6, :], lb[:, 6, :], lb[:, 4, :], ALU.add).then_inc(signal("vector_chain"), 1)
            dve.wait_ge(sem("vector_chain"), told["vector_chain"])
            V.reciprocal(lb[:, 7, :], lb[:, 6, :]).then_inc(signal("vector_chain"), 1)
            dve.wait_ge(sem("vector_chain"), told["vector_chain"])
            tt(lb[:, 4, :], lb[:, 4, :], lb[:, 7, :]).then_inc(signal("vector_chain"), 1)
            dve.wait_ge(sem("vector_chain"), told["vector_chain"])
            ts(lb[:, 5, :], lb[:, 4, :], -1.0, 1.0, ALU.mult, ALU.add).then_inc(signal("vector_chain"), 1)
            dve.wait_ge(sem("vector_chain"), told["vector_chain"])
            for j in range(2):
                ins = ts(omka[:, j, :], pv[:, 2, (3 * 2 + j) * 8:(3 * 2 + j) * 8 + 8], -1.0, 1.0, ALU.mult, ALU.add)
            ins.then_inc(signal("vector_chain"), 1)
            dve.wait_ge(sem("vector_chain"), told["vector_chain"])
            state["out"] = 32 * 9
            rwkv(0)
            ffn(0)
            gdn()
            ffn(1)
            hgrn()
            ffn(2)
            rwkv(1)
            ffn(3)

        @block.gpsimd
        def _(pool):
            G = nc.gpsimd

            def select(dst, pattern, base, mult, op=ALU.is_ge, fill=0.0):
                G.affine_select(out=dst, in_=dst, compare_op=op, fill=fill, base=base, pattern=pattern,
                                     channel_multiplier=mult).then_inc(signal("gpsimd_chain"), 1)
                pool.wait_ge(sem("gpsimd_chain"), told["gpsimd_chain"])

            stage = flat("A2")

            def rows_in(n, r0, src):
                pool.dma_start(stage[r0:r0 + src.shape[0], n * P:(n + 1) * P], src).then_inc(sem("params_landed"), 16)

            def vec(name):
                return A[name].rearrange("j (c f) -> (j c) f", f=P)

            for q, name in enumerate(("norm_mix_pre", "norm_mix_post", "norm_ffn_pre", "norm_ffn_post")):
                rows_in(0, 32 * q, vec(name))
            rows_in(1, 0, A["rwkv_mix"].rearrange("j s (c f) -> (j s c) f", f=P))
            for q, name in enumerate(("rwkv_w0", "rwkv_a0", "rwkv_k_k", "rwkv_k_a")):
                rows_in(2, 16 * q, vec(name))
            rows_in(2, 64, A["rwkv_r_k"].rearrange("j (c h) f -> (j c) (h f)", h=2))
            rows_in(2, 80, vec("rwkv_lnx_w"))
            rows_in(2, 96, vec("rwkv_lnx_b"))
            rows_in(2, 112, vec("rwkv_v0"))
            rows_in(3, 0, vec("hgrn_lb"))
            rows_in(3, 32, A["hgrn_norm_w"])
            rows_in(3, 33, A["gdn_norm_w"])
            rows_in(4, 0, A["gdn_conv_w"].rearrange("j w (c f) -> (j w c) f", f=P))
            taps = A["ffn_conv_w"].rearrange("i w (c f) -> (i w c) f", f=P)
            for q in range(6):
                rows_in(5 + q, 0, taps[q * 88:(q + 1) * 88])
            rows_in(11, 0, A["state_rwkv_shift"].rearrange("j b (c f) -> (j b c) f", f=P))
            for q, name in enumerate(("gdn_a_log", "gdn_dt_bias")):
                pool.dma_start(gpar[:, q:q + 1], A[name].rearrange("j (h o) -> (j h) o", o=1)).then_inc(
                    sem("gate_params_landed"), 16)

            G.memset(eps[:, 0:1], EPS).then_inc(signal("gpsimd_chain"), 1)
            pool.wait_ge(sem("gpsimd_chain"), told["gpsimd_chain"])
            G.memset(eps[:, 1:2], LNX_EPS).then_inc(signal("constants_ready"), 1)
            pool.wait_ge(sem("constants_ready"), told["constants_ready"])
            G.memset(ident[:, :], 0.0).then_inc(signal("gpsimd_chain"), 1)
            pool.wait_ge(sem("gpsimd_chain"), told["gpsimd_chain"])
            select(ident[:, :], [[-1, P]], 0, 1, ALU.not_equal, 1.0)
            G.memset(ones[:, :], 1.0)
            G.memset(bones[:, :], 0.0).then_inc(signal("gpsimd_chain"), 1)
            pool.wait_ge(sem("gpsimd_chain"), told["gpsimd_chain"])
            G.memset(bones[0:64, 0:64], 1.0)
            G.memset(bones[64:128, 64:128], 1.0).then_inc(signal("gpsimd_chain"), 1)
            pool.wait_ge(sem("gpsimd_chain"), told["gpsimd_chain"])
            G.memset(mask4[:, :, :], 1.0).then_inc(signal("gpsimd_chain"), 1)
            pool.wait_ge(sem("gpsimd_chain"), told["gpsimd_chain"])
            for q in range(4):
                select(mask4[:, q, :], [[1, P]], -1 if q % 2 == 0 else 0, -1)
            G.tensor_copy(same[:, 0, :], ident[:, :]).then_inc(signal("gpsimd_chain"), 1)
            pool.wait_ge(sem("gpsimd_chain"), told["gpsimd_chain"])
            for l in range(1, LEVELS + 1):
                n = 1 << l
                cur, old = same[:, l % 2, :], same[:, (l - 1) % 2, :]
                G.memset(cur, 1.0).then_inc(signal("gpsimd_chain"), 1)
                pool.wait_ge(sem("gpsimd_chain"), told["gpsimd_chain"])
                if l < LEVELS:
                    v = cur.rearrange("p (b r) -> p b r", r=n)
                    select(v, [[-n, P // n], [0, n]], 0, 1)
                    select(v, [[n, P // n], [0, n]], n - 1, -1)
                if l == 2:
                    for q in range(4):
                        G.tensor_tensor(samp4[:, q, :], mask4[0:NS, q, 0:NS], cur[0:NS, 0:NS], ALU.mult).then_inc(signal("gpsimd_chain"), 1)
                        pool.wait_ge(sem("gpsimd_chain"), told["gpsimd_chain"])
                    G.memset(lastm[:, :], 0.0).then_inc(signal("gpsimd_chain"), 1)
                    pool.wait_ge(sem("gpsimd_chain"), told["gpsimd_chain"])
                    G.tensor_copy(lastm[:, NT - 1:NS:NT], cur[0:NS, NT - 1:NS:NT]).then_inc(signal("gpsimd_chain"), 1)
                    pool.wait_ge(sem("gpsimd_chain"), told["gpsimd_chain"])
                G.tensor_tensor(upp[:, l - 1, :], cur, old, ALU.subtract).then_inc(signal("gpsimd_chain"), 1)
                pool.wait_ge(sem("gpsimd_chain"), told["gpsimd_chain"])
                G.tensor_copy(low[:, l - 1, :], upp[:, l - 1, :]).then_inc(signal("gpsimd_chain"), 1)
                pool.wait_ge(sem("gpsimd_chain"), told["gpsimd_chain"])
                G.tensor_tensor(upp[:, l - 1, :], upp[:, l - 1, :], mask4[:, 0, :], ALU.mult).then_inc(signal("gpsimd_chain"), 1)
                pool.wait_ge(sem("gpsimd_chain"), told["gpsimd_chain"])
                G.tensor_tensor(low[:, l - 1, :], low[:, l - 1, :], upp[:, l - 1, :], ALU.subtract).then_inc(signal("gpsimd_chain"), 1)
                pool.wait_ge(sem("gpsimd_chain"), told["gpsimd_chain"])
            G.memset(seg[:, :], 1.0).then_inc(signal("gpsimd_chain"), 1)
            pool.wait_ge(sem("gpsimd_chain"), told["gpsimd_chain"])
            G.memset(seg[:, 0:NPR:P], 0.0).then_inc(signal("gpsimd_chain"), 1)
            pool.wait_ge(sem("gpsimd_chain"), told["gpsimd_chain"])
            G.memset(seg[:, NPR:T:NT], 0.0).then_inc(signal("gpsimd_chain"), 1)
            pool.wait_ge(sem("gpsimd_chain"), told["gpsimd_chain"])
            G.memset(bmask[:, :, :], 1.0).then_inc(signal("gpsimd_chain"), 1)
            pool.wait_ge(sem("gpsimd_chain"), told["gpsimd_chain"])
            select(bmask[:, :, :], [[-NT, NB], [1, NS]], 0, 0)
            select(bmask[:, :, :], [[NT, NB], [-1, NS]], NT - 1, 0)
            G.memset(rmask[:, :], 1.0).then_inc(signal("gpsimd_chain"), 1)
            pool.wait_ge(sem("gpsimd_chain"), told["gpsimd_chain"])
            select(rmask[:, :], [[-NT, NB]], 0, 1)
            select(rmask[:, :], [[NT, NB]], NT - 1, -1)
            G.memset(ones[:, 0:1], 1.0).then_inc(signal("masks_ready"), 1)
            pool.wait_ge(sem("masks_ready"), told["masks_ready"])

            def ffn(i):
                lead = FW - 1
                load_hist(A["state_ffn_conv"][i])
                history(lead, 88, i, [(("up", i, p, half), q, half * 2 + q, half * FC + 2 * p + q,
                                       ("value_conv", "gate_conv")[half])
                                      for p in range(FPAIR) for half in range(2) for q in range(2)])

            sraw_free = []

            def load_hist(src):
                sample_free()
                pool.dma_start(sraw[0:src.shape[1] * src.shape[2] // P, :].rearrange("r (b f) -> r b f", b=NB),
                               src.rearrange("b w (c f) -> (w c) b f", f=P)).then_inc(sem("hist_landed"), 16)

            last_use = [None]

            def sample_free():
                if last_use[0]:
                    e, k = last_use[0]
                    pool.wait_ge(filled["scalar"] if e == "turned" else drained["vector"], k + 1)

            def history(lead, rows, layer, tiles):
                pool.wait_ge(drained["scalar"], mark["hist", layer] + 1)
                last_use[0] = ("turned", mark["hist", layer])
                for n in range(4):
                    ins = G.memset(buf(n, lead)[:, 0:lead], 0.0)
                ins.then_inc(signal("gpsimd_chain"), 1)
                pool.wait_ge(sem("gpsimd_chain"), told["gpsimd_chain"])
                hv = hist[:, :, 0:rows].rearrange("p b (w c) -> p b w c", w=lead)
                lv = last[:, :, 0:rows].rearrange("p b (w c) -> p b w c", w=lead)

                def put(i):
                    _, _, e, c, used = tiles[i]
                    if i >= 4:
                        pool.wait_ge(sem(used), after(pool, used))
                    s = buf(e, lead)[:, lead + NPR:span(lead)].rearrange("p (b t) -> p b t", b=NB)
                    G.tensor_copy(s[:, :, 0:lead], hv[:, :, :, c]).then_inc(signal("hist_in"), 1)
                    pool.wait_ge(sem("hist_in"), told["hist_in"])

                def save(i):
                    key, q, e, c, used = tiles[i]
                    k = mark[key, q] if q is not None else mark[key]
                    pool.wait_ge(drained["scalar"], k + 1)
                    ext = buf(e, lead)
                    s = ext[:, lead + NPR:span(lead)].rearrange("p (b t) -> p b t", b=NB)
                    G.tensor_copy(lv[:, 0, :, c], ext[:, NPR:NPR + lead])
                    G.tensor_copy(lv[:, 1:NB + 1, :, c], s[:, :, NT:NT + lead]).then_inc(signal("saved"), 1)
                    pool.wait_ge(sem("saved"), told["saved"])

                for i in range(4):
                    put(i)
                for i in range(len(tiles)):
                    save(i)
                    if i + 4 < len(tiles):
                        put(i + 4)
                for i in range(len(tiles) - 4, len(tiles)):
                    pool.wait_ge(sem(tiles[i][4]), after(pool, tiles[i][4]))
                G.memset(same[:, 0, 0:1], 0.0).then_inc(signal("last_saved"), 1)
                pool.wait_ge(sem("last_saved"), told["last_saved"])

            def rwkv(j):
                pool.wait_ge(sem("h_whole"), after(pool, "h_whole"))
                G.tensor_copy(spo_flat[:, 0:8], H[:, :, NPR - 1])
                G.tensor_copy(spo_flat[:, 8:72].rearrange("p (b c) -> p c b", b=NB),
                                         H[:, :, NPR + NT - 1:T:NT]).then_inc(signal("shift_saved"), 1)
                pool.wait_ge(sem("shift_saved"), told["shift_saved"])
                for c in range(KC):
                    sample_free()
                    dst = sraw[0:64, :].rearrange("v (b h k) -> v b h k", b=NB, h=2)
                    for hh in range(2):
                        pool.dma_start(dst[:, :, hh, :], A["state_rwkv_wkv"][j, :, 2 * c + hh].rearrange(
                            "b v k -> v b k")).then_inc(sem("sample_state_in"), 16)
                    last_use[0] = ("turned", mark["sraw", "rwkv", j, c])

            spo_flat = spo[:, :, :].rearrange("p a b -> p (a b)")

            def heads(src, kind):
                for h in range(8):
                    sample_free()
                    pool.dma_start(sraw[:, :].rearrange("p (b v) -> p b v", b=NB),
                                   src[0, :, h].rearrange("b k v -> k b v")).then_inc(sem("sample_state_in"), 16)
                    last_use[0] = ("updated", mark["sraw", kind, h])

            rwkv(0)
            ffn(0)
            load_hist(A["state_gdn_conv"][0])
            history(GW - 1, 72, "gdn", [(("gin", n), None, n % 4, n, "gconv") for n in range(GT)])
            heads(A["state_gdn_S"], "gdn")
            ffn(1)
            heads(A["state_hgrn_S"], "hgrn")
            ffn(2)
            rwkv(1)
            ffn(3)

        @block.sync
        def _(sync):
            sync.dma_start(flat("A0", 2)[:, 0:2048].rearrange("p (b f) -> p b f", b=2),
                           A["x_prompt"][0].rearrange("(b p) f -> p b f", p=P)).then_inc(sem("x_landed"), 16)
            sync.dma_start(flat("A0", 2)[0:NS, 2048:3072],
                           A["x_sample"].rearrange("b t f -> (b t) f")).then_inc(sem("x_landed"), 16)
            for n, key in enumerate(plan):
                if n >= RING:
                    s, v = release[n - RING]
                    sync.wait_ge(s, v)
                for dst, src in slab_parts(key, ring[:, n % RING, :]):
                    sync.dma_start(dst, src).then_inc(landed[n % RING], 16)


_INS = ['x_prompt', 'x_sample', 'state_rwkv_shift', 'state_rwkv_wkv', 'state_gdn_conv', 'state_gdn_S',
        'state_hgrn_S', 'state_ffn_conv', 'norm_mix_pre', 'norm_mix_post', 'norm_ffn_pre', 'norm_ffn_post',
        'rwkv_mix', 'rwkv_w_rkv', 'rwkv_w0', 'rwkv_w1', 'rwkv_w2', 'rwkv_a0', 'rwkv_a1', 'rwkv_a2',
        'rwkv_v0', 'rwkv_v1', 'rwkv_v2', 'rwkv_g1', 'rwkv_g2', 'rwkv_k_k', 'rwkv_k_a', 'rwkv_r_k',
        'rwkv_lnx_w', 'rwkv_lnx_b', 'rwkv_w_o', 'gdn_w_in', 'gdn_conv_w', 'gdn_a_log', 'gdn_dt_bias',
        'gdn_norm_w', 'gdn_w_o', 'hgrn_w_in', 'hgrn_lb', 'hgrn_norm_w', 'hgrn_w_o',
        'ffn_w_up', 'ffn_conv_w', 'ffn_w_down']
_OUTS = [('y_prompt', (1, 256, 1024)), ('y_sample', (8, 4, 1024)),
         ('prompt_shift', (2, 1, 1024)), ('sample_shift', (2, 8, 1024)),
         ('prompt_wkv', (2, 1, 16, 64, 64)), ('sample_wkv', (2, 8, 16, 64, 64)),
         ('prompt_gdn_conv', (1, 1, 3, 3072)), ('sample_gdn_conv', (1, 8, 3, 3072)),
         ('prompt_gdn_S', (1, 1, 8, 128, 128)), ('sample_gdn_S', (1, 8, 8, 128, 128)),
         ('prompt_hgrn_S', (1, 1, 8, 128, 128)), ('sample_hgrn_S', (1, 8, 8, 128, 128)),
         ('prompt_ffn_conv', (4, 1, 2, 5632)), ('sample_ffn_conv', (4, 8, 2, 5632))]


def kernel(**inputs):
    import numpy as _np
    import concourse.bacc as _bacc
    from concourse.bass_utils import run_bass_kernel_spmd as _run

    nc = _bacc.Bacc("TRN2", target_bir_lowering=False, num_devices=1)
    arrays, ins, outs = {}, {}, {}
    for name in _INS:
        a = _np.ascontiguousarray(inputs[name])
        arrays[f"in_{name}"] = a
        ins[name] = nc.dram_tensor(f"in_{name}", a.shape, mybir.dt.from_np(a.dtype), kind="ExternalInput").ap()
    for name, shape in _OUTS:
        outs[name] = nc.dram_tensor(f"out_{name}", shape, F32, kind="ExternalOutput").ap()
    ins["v_first"] = nc.dram_tensor("v_first", (D, T), F32, kind="Internal").ap()
    build(nc, ins, outs)
    r = _run(nc, [arrays], core_ids=[0])
    return tuple(r.results[0][f"out_{name}"] for name, _ in _OUTS)
```

```python
from contextlib import ExitStack

import concourse.bass as bass
from concourse import mybir

F32 = mybir.dt.float32
F32R = mybir.dt.float32r
U32 = mybir.dt.uint32
ALU = mybir.AluOpType
ACT = mybir.ActivationFunctionType
AX_X = mybir.AxisListType.X

P = 128
D = 1024
KC = D // P
NPR = 256
NB = 8
NT = 4
NS = NB * NT
T = NPR + NS
SLOT = KC * T
DEPTH = 4
FF = 2816
FC = FF // P
FPAIR = FC // 2
DOWN_K = (8, 7, 7)
RING = 4
SLAB = 2048
LEVELS = 7
EPS = 1e-6
LNX_EPS = 64e-5
RW_DECAY = 0.6065306597126334
MIX_ORDER = (3, 2, 0, 1, 4, 5)
FW, GW = 3, 4
GT = 24


def weight_plan():
    plan = []

    def ffn(i):
        for p in range(FPAIR):
            plan.append(("up", i, 0, p))
            plan.append(("up", i, 1, p))
        for m in range(4):
            for s in range(3):
                plan.append(("down", i, m, s))

    def rwkv(j):
        plan.extend(("rkv", j, 2, m) for m in range(4))
        if j:
            plan.append(("v12",))
        plan.extend(("rkv", j, 1, m) for m in range(4))
        plan.extend(("rkv", j, 0, m) for m in range(4))
        plan.append(("wa1", j))
        plan.append(("wa2", j))
        plan.append(("g1", j))
        plan.append(("g2", j))
        plan.extend(("rwo", j, m) for m in range(4))

    rwkv(0)
    ffn(0)
    plan.extend(("gin", m) for m in range(16))
    plan.append(("grest",))
    plan.extend(("gwo", m) for m in range(4))
    ffn(1)
    plan.extend(("hin", m) for m in range(16))
    plan.extend(("hwo", m) for m in range(4))
    ffn(2)
    rwkv(1)
    ffn(3)
    return plan


PARAM_ROWS = (128, 96, 120, 34, 96, 88, 88, 88, 88, 88, 88, 128)
PARAM_DMAS = 24


def build(nc, A, OUT):
    ctx = ExitStack()
    with ctx:
        def sb(name, shape, dt=F32):
            return ctx.enter_context(nc.sbuf_tensor(name, shape, dt))

        sems = {}

        def sem(name):
            if name not in sems:
                sems[name] = ctx.enter_context(nc.semaphore(name))
            return sems[name]

        def sb_rounded(name, shape):
            with ExitStack() as scope:
                return scope.enter_context(nc.sbuf_tensor(name, shape, F32R))

        arena_r = sb_rounded("arena_rounded", [P, 12 * SLOT])
        arena = sb("arena", [P, 12 * SLOT])
        names = ["X", "H", "SQ"] + [f"A{i}" for i in range(9)]

        def flat(name, n=1):
            k = names.index(name)
            return arena[:, k * SLOT:(k + n) * SLOT]

        def act3(name):
            return flat(name).rearrange("p (c t) -> p c t", c=KC)

        def act3r(name):
            k = names.index(name)
            return arena_r[:, k * SLOT:(k + 1) * SLOT].rearrange("p (c t) -> p c t", c=KC)

        w_lo = sb_rounded("w_lo", [P, RING, SLAB])
        ring = sb("ring", [P, RING, SLAB])
        w_hi = sb_rounded("w_hi", [P, 2, SLAB])
        ysb = sb("ysb", [P, 2, 512])
        sst = sb("sst", [P, 2, 512])
        sout = sb("sout", [P, 1024])
        vms = sb("vms", [NS, 2, 512])
        ident = sb("ident", [P, P])
        ones = sb("ones", [P, P])
        bones = sb("bones", [P, P])
        same = sb("same", [P, 2, P])
        low = sb("low", [P, LEVELS, P])
        upp = sb("upp", [P, LEVELS, P])
        mask4 = sb("mask4", [P, 4, P])
        samp4 = sb("samp4", [NS, 4, NS])
        lastm = sb("lastm", [NS, NS])
        seg = sb("seg", [P, T])
        bmask = sb("bmask", [P, NB, NS])
        rmask = sb("rmask", [NS, NB])
        pv = sb("pv", [P, 12, P])
        omka = sb("omka", [P, 2, KC])
        lb = sb("lb", [P, 8, KC])
        rstd = sb("rstd", [P, T])
        tm = sb("tm", [P, 2, 1024])
        rs = sb("rs", [P, 2, 256])
        nu = sb("nu", [P, 2, 256])
        xd = sb("xd", [P, 2, 256])
        sraw = sb("sraw", [P, 1024])
        sp = sb("sp", [P, 2, 128])
        spo = sb("spo", [P, 2, 128])
        tms = sb("tms", [NS, 3, P])
        ms = sb("ms", [NS, 2, 4, NS])
        ams = sb("ams", [P, 2, NB, NS])
        rms_ = sb("rms_", [P, 2, NS])
        us = sb("us", [NS, 4, P])
        cen = sb("cen", [P, 4, KC, 2])
        els = sb("els", [P, KC, NB])
        lora = sb("lora", [P, T])
        tb = sb("tb", [P, 3, 16])
        neg = sb("neg", [P, 3, 8])
        ed = sb("ed", [P, 3, 4])
        gpar = sb("gpar", [8, 4])
        eps = sb("eps", [P, 2])
        bank = [ctx.enter_context(nc.psum_tensor(f"bank{i}", [P, 512], F32)) for i in range(2)]
        wide = [ctx.enter_context(nc.psum_tensor(f"wide{i}", [P, 1024], F32)) for i in range(3)]
        bk = [bank[0][:, :], bank[1][:, :]] + [wide[i // 2][:, (i % 2) * 512:(i % 2 + 1) * 512] for i in range(6)]

        def lvl_banks(g):
            return 2 + g, (4, 5) if g == 0 else (6, 7)

        hist = flat("A7")[:, 0:704].rearrange("p (b r) -> p b r", b=NB)
        last = flat("A7")[:, 704:704 + 792].rearrange("p (b r) -> p b r", b=NB + 1)
        g8 = sout[0:8, 0:3 * T].rearrange("p (q t) -> p q t", q=3)

        X, H, SQ = act3("X"), act3("H"), act3("SQ")
        S = [act3(f"A{i}") for i in range(9)]
        MX = flat("H", 2)[:, 0:4096].rearrange("p (g m q t) -> p g m q t", g=2, m=4, q=4)
        T2 = flat("A0")[:, 0:2048].rearrange("p (g m q t) -> p g m q t", g=2, m=4, q=2)
        ARp = flat("A6", 2)[:, 0:4096].rearrange("p (c b q t) -> p c b q t", c=KC, b=2, q=2)
        ARs = flat("A6", 2)[:, 4096:4608].rearrange("p (c q t) -> p c q t", c=KC, q=2)

        def head_state(h):
            return (sraw[:, :], sst[:, :, :].rearrange("p a b -> p (a b)"))[h % 2]

        filled = {"scalar": sem("filled_for_scalar"), "vector": sem("filled_for_vector")}
        drained = {"scalar": sem("drained_by_scalar"), "vector": sem("drained_by_vector")}
        landed = [sem(f"weights_landed{i}") for i in range(RING)]
        slab_used = sem("slab_used")

        told = {}
        seen = {}

        def signal(name):
            told[name] = told.get(name, 0) + 1
            return sem(name)

        def after(eng, name, n=1):
            seen[id(eng), name] = seen.get((id(eng), name), 0) + n
            return seen[id(eng), name]

        def after_dma(eng, name, n=1):
            return after(eng, name, 16 * n)

        mark = {}
        plan = weight_plan()
        release = []
        n_filled = {"scalar": 0, "vector": 0}
        act_bank, vec_bank = [], []
        holder = {}

        def freed(b):
            if b not in holder:
                return sem("basics_ready"), 1
            e, k = holder[b]
            return drained[e], k + 1

        def result(e, *banks):
            k = n_filled[e]
            n_filled[e] += 1
            (act_bank if e == "scalar" else vec_bank).append(banks[0])
            for b in banks:
                holder[b] = (e, k)
            return k

        def cols(w, c0, n):
            return w[:, c0:c0 + n].rearrange("(k p) n -> p k n", p=P)

        def slab_parts(key, slot):
            kind = key[0]

            def v(o, k, n, rows=P):
                return slot[0:rows, o:o + k * n].rearrange("p (k n) -> p k n", k=k)

            if kind == "rkv":
                return [(v(0, 8, 256), cols(A["rwkv_w_rkv"][key[1], key[2]], key[3] * 256, 256))]
            if kind == "g1":
                return [(v(0, 8, 128), cols(A["rwkv_g1"][key[1]], 0, 128))]
            if kind == "v12":
                return [(v(0, 8, 32), cols(A["rwkv_v1"][0], 0, 32)), (slot[0:32, 256:1280], A["rwkv_v2"][0])]
            if kind == "wa1":
                return [(v(0, 8, 64), cols(A["rwkv_w1"][key[1]], 0, 64)),
                        (v(512, 8, 64), cols(A["rwkv_a1"][key[1]], 0, 64))]
            if kind == "wa2":
                return [(slot[0:64, 0:1024], A["rwkv_w2"][key[1]]),
                        (slot[0:64, 1024:2048], A["rwkv_a2"][key[1]])]
            if kind == "g2":
                return [(slot[:, 0:1024], A["rwkv_g2"][key[1]])]
            if kind == "rwo":
                return [(v(0, 8, 256), cols(A["rwkv_w_o"][key[1]], key[2] * 256, 256))]
            if kind == "gin":
                return [(v(0, 8, 256), cols(A["gdn_w_in"][0], key[1] * 256, 256))]
            if kind == "grest":
                return [(v(0, 8, 16), cols(A["gdn_w_in"][0], 4096, 16))]
            if kind == "gwo":
                return [(v(0, 8, 256), cols(A["gdn_w_o"][0], key[1] * 256, 256))]
            if kind == "hin":
                return [(v(0, 8, 256), cols(A["hgrn_w_in"][0], key[1] * 256, 256))]
            if kind == "hwo":
                return [(v(0, 8, 256), cols(A["hgrn_w_o"][0], key[1] * 256, 256))]
            if kind == "up":
                return [(v(0, 8, 256), cols(A["ffn_w_up"][key[1]], key[2] * FF + key[3] * 256, 256))]
            k0 = sum(DOWN_K[:key[3]])
            k = DOWN_K[key[3]]
            w = A["ffn_w_down"][key[1]][k0 * P:(k0 + k) * P]
            return [(v(0, k, 256), cols(w, key[2] * 256, 256))]

        landed_at = []
        per_slot = [0] * RING
        for n, key in enumerate(plan):
            per_slot[n % RING] += 16 * len(slab_parts(key, ring[:, 0, :]))
            landed_at.append(per_slot[n % RING])

        split_kinds = ("rkv", "rwo", "gin", "gwo", "hin", "hwo", "up", "down")
        split_order = [n for n, key in enumerate(plan) if key[0] in split_kinds]

        def hi_slot(n):
            return split_order.index(n) % 2

        def slab_size(n):
            return DOWN_K[plan[n][3]] * 256 if plan[n][0] == "down" else SLAB

        def y_hi(kt):
            return act3r(("A3", "A8", "SQ")[kt // KC])[:, kt % KC, :]

        def y_lo(kt):
            return arena_r[:, (names.index("A0") * KC + kt) * T:(names.index("A0") * KC + kt + 1) * T]

        def pcol(kind, j, c):
            if kind in ("mix_pre", "mix_post", "ffn_pre", "ffn_post"):
                r = ("mix_pre", "mix_post", "ffn_pre", "ffn_post").index(kind) * 4 + j
                return pv[:, 0, r * 8 + c:r * 8 + c + 1]
            if kind == "mix":
                return pv[:, 1, j * 8 + c:j * 8 + c + 1]
            order = ("w0", "a0", "k_k", "k_a", "r_k", "lnx_w", "lnx_b", "v0")
            r = order.index(kind) * 2 + j
            return pv[:, 2, r * 8 + c:r * 8 + c + 1]

        def fconv(i, tap, c):
            r = i * 132 + tap * 44 + c
            return pv[:, 5 + r // 88, r % 88:r % 88 + 1]

        def gconv(tap, c):
            return pv[:, 4, tap * 24 + c:tap * 24 + c + 1]

        shiftT = pv[:, 11, :].rearrange("p (j b c) -> p j b c", j=2, b=NB)

        def ps3(b):
            return b[:, 0:T]

        def span(lead):
            return lead + NPR + NB * (lead + NT)

        def buf(n, lead):
            return flat("A5", 2)[:, n * span(lead):(n + 1) * span(lead)]

        def split(ap, lead):
            return ap[:, lead:lead + NPR], ap[:, lead + NPR:lead + NPR + NB * (lead + NT)].rearrange(
                "p (b t) -> p b t", b=NB)[:, :, lead:lead + NT]

        def samples(one, which):
            for args in which:
                yield from one(*args)
                yield

        block = ctx.enter_context(nc.Block())

        @block.tensor
        def _(pe):
            state = {"slab": 0, "lin": 0}

            def slab():
                n = state["slab"]
                state["slab"] += 1
                pe.wait_ge(landed[n % RING], landed_at[n])
                return ring[:, n % RING, :]

            def free_after(s, value):
                release.append((s, value))

            def free_by(mm):
                mm.then_inc(signal("slab_used"), 1)
                release.append((slab_used, told["slab_used"]))

            def lin_bank():
                b = state["lin"] % 4
                state["lin"] += 1
                return b

            def linear_slab(w, rhs, tiles, key, ready=None, k_rows=P, nk=KC, m=P):
                for q in range(tiles):
                    b = lin_bank()
                    pe.wait_ge(*freed(b))
                    for k in range(nk):
                        if ready and q == 0:
                            pe.wait_ge(sem(ready), after(pe, ready))
                        mm = nc.tensor.matmul(bk[b][0:m, 0:T], w(k, q), rhs(k), start=(k == 0), stop=(k == nk - 1))
                    mm.then_inc(filled["scalar"], 1)
                    i = result("scalar", b)
                    mark[key, q] = i
                return i

            def split_slab_tiles(x_hi, x_lo, ready=None):
                wh, wl = split_slab()
                bs = [lin_bank(), lin_bank()]
                order = [(k, q) for k in range(KC) for q in range(2)] if ready else [(k, q) for q in range(2) for k in range(KC)]
                for k, q in order:
                    if k == 0:
                        pe.wait_ge(*freed(bs[q]))
                    if ready and q == 0:
                        pe.wait_ge(sem(ready), after(pe, ready))
                    cols_ = slice(q * P, (q + 1) * P)
                    mm = three(bk[bs[q]][:, 0:T], wh[:, k, cols_], wl[:, k, cols_],
                               act3r(x_hi)[:, k, :], act3r(x_lo)[:, k, :], k == 0, k == KC - 1)
                    if k == KC - 1:
                        mm.then_inc(filled["scalar"], 1)
                        i = result("scalar", bs[q])
                free_after(filled["scalar"], i + 1)
                return i

            def square_linear(keys, x_hi, x_lo, name, ready, stat=None):
                for s in range(keys):
                    i = split_slab_tiles(x_hi, x_lo, ready if s == 0 else None)
                    mark[name, 2 * s], mark[name, 2 * s + 1] = i - 1, i
                    if stat is not None and s:
                        norm_stat(stat, (2 * s - 2, 2 * s - 1))
                if stat is not None:
                    norm_stat(stat, (KC - 2, KC - 1))
                return i

            def split_slab():
                n = state["slab"]
                state["slab"] += 1
                pe.wait_ge(sem("hi_ready"), after(pe, "hi_ready"))
                pe.wait_ge(sem("lo_ready"), after(pe, "lo_ready"))
                k = slab_size(n) // 256
                return [w[:, 0:k * 256].rearrange("p (k n) -> p k n", k=k)
                        for w in (w_hi[:, hi_slot(n), :], w_lo[:, n % RING, :])]

            def three(out, wh, wl, xh, xl, first, last):
                nc.tensor.matmul(out, wh, xh, start=first, stop=False)
                nc.tensor.matmul(out, wh, xl, start=False, stop=False)
                return nc.tensor.matmul(out, wl, xh, start=False, stop=last)

            def norm_stat(n, tiles=range(KC), src=SQ):
                b = 4 + n % 2
                if 0 in tiles:
                    pe.wait_ge(*freed(b))
                for c in tiles:
                    pe.wait_ge(sem("square_ready"), after(pe, "square_ready"))
                    mm = nc.tensor.matmul(bk[b][:, 0:T], ones[:, :], src[:, c, :], start=(c == 0), stop=(c == KC - 1))
                if KC - 1 in tiles:
                    mm.then_inc(filled["scalar"], 1)
                    result("scalar", b)

            def tile_stats(weights, ready, consumer="scalar", src=SQ):
                for c in range(KC):
                    pe.wait_ge(sem(ready), after(pe, ready))
                    b = 4 + c % 2
                    pe.wait_ge(*freed(b))
                    mm = nc.tensor.matmul(bk[b][:, 0:T], weights[:, :], src[:, c, :], start=True, stop=True)
                    mm.then_inc(filled[consumer], 1)
                    result(consumer, b)

            def turn(dst, src, n, base=0):
                return nc.tensor.transpose(dst, src, ident[base:base + n, base:base + n])

            def load_hist(rows, layer):
                pe.wait_ge(sem("hist_landed"), after_dma(pe, "hist_landed"))
                for q in range(2):
                    b = 6 + q
                    pe.wait_ge(*freed(b))
                    for i in range(4):
                        mm = turn(bk[b][:, i * 88:i * 88 + rows], sraw[0:rows, (q * 4 + i) * P:(q * 4 + i + 1) * P], rows)
                    mm.then_inc(filled["scalar"], 1)
                    mark["hist", layer] = result("scalar", b)

            def conv_state_out(rows):
                pe.wait_ge(sem("last_saved"), after(pe, "last_saved"))
                for q in range(3):
                    b = 6 + q % 2
                    pe.wait_ge(*freed(b))
                    for i in range(3):
                        mm = turn(bk[b][0:rows, i * P:(i + 1) * P], last[:, 3 * q + i, 0:rows], P)
                    mm.then_inc(filled["scalar"], 1)
                    result("scalar", b)

            def ffn(i):
                norm_stat(1)
                load_hist(88, i)
                for p in range(FPAIR):
                    for half in range(2):
                        k = split_slab_tiles("A4", "H", "x_split" if p == 0 and half == 0 else None)
                        mark[("up", i, p, half), 0], mark[("up", i, p, half), 1] = k - 1, k
                for m in range(4):
                    bs = [lin_bank(), lin_bank()]
                    for b_ in bs:
                        pe.wait_ge(*freed(b_))
                    kt = 0
                    for s in range(3):
                        wh, wl = split_slab()
                        for k in range(DOWN_K[s]):
                            if m == 0:
                                pe.wait_ge(sem("y_ready"), after(pe, "y_ready"))
                            for q in range(2):
                                cols_ = slice(q * P, (q + 1) * P)
                                mm = three(bk[bs[q]][:, 0:T], wh[:, k, cols_], wl[:, k, cols_], y_hi(kt), y_lo(kt),
                                           kt == 0, kt == FC - 1)
                                if kt == FC - 1:
                                    mm.then_inc(filled["scalar"], 1)
                                    done = result("scalar", bs[q])
                            kt += 1
                        if s < 2:
                            free_by(mm)
                    free_after(filled["scalar"], done + 1)
                    if m:
                        norm_stat(0, (2 * m - 2, 2 * m - 1), H)
                norm_stat(0, (KC - 2, KC - 1), H)
                conv_state_out(88)

            def levels(masked, between):
                ky, kp = [0, 0], list(masked)
                for l in range(LEVELS):
                    for g in range(2):
                        yb, pb = lvl_banks(g)
                        pe.wait_ge(drained["vector"], kp[g] + 1)
                        pe.wait_ge(*freed(yb))
                        for m in range(4):
                            y = bk[yb][:, m * P:(m + 1) * P]
                            if l == 0:
                                mm = turn(y, MX[:, g, m, 0, :], P)
                            else:
                                mm = nc.tensor.matmul(y, MX[:, g, m, 0, :], T2[:, g, m, 0, :], start=True, stop=True)
                        mm.then_inc(filled["vector"], 1)
                        ky[g] = result("vector", yb)
                        next(between, None)
                    if l == 0:
                        kp = list(ky)
                        continue
                    for g in range(2):
                        yb, pb = lvl_banks(g)
                        pe.wait_ge(drained["vector"], ky[g] + 1)
                        for b_ in pb:
                            pe.wait_ge(*freed(b_))
                        for m in range(4):
                            ps = wide[1 + g][:, m * 256:m * 256 + 256]
                            y = ysb[:, g, m * P:(m + 1) * P]
                            if l < LEVELS - 1:
                                nc.tensor.matmul(ps[:, 0:P], T2[:, g, m, 1, :], y, start=True, stop=True)
                            mm = nc.tensor.matmul(ps[:, P:2 * P], y, T2[:, g, m, 1, :], start=True, stop=True)
                        mm.then_inc(filled["vector"], 1)
                        kp[g] = result("vector", *pb)
                        next(between, None)
                for _ in between:
                    pass
                for g in range(2):
                    pe.wait_ge(drained["vector"], kp[g] + 1)

            def rwkv(j):
                norm_stat(0)
                M = [S[1], S[2]]

                def mixed(i):
                    return lambda k: M[i % 2][:, k, :]

                square_linear(4, "A6", "A4", ("v", j), "mix_split")
                if j:
                    sl = slab()
                    wv1 = sl[:, 0:256].rearrange("p (k n) -> p k n", k=8)
                    kv = linear_slab(lambda k, q: wv1[:, k, :], mixed(0), 1, ("v1", j), m=32)
                    mark["mix_used", j, 0] = kv
                    pe.wait_ge(drained["scalar"], kv + 1)
                    for c in range(KC):
                        k2 = linear_slab(lambda k, q: sl[0:32, 256 + c * P:256 + (c + 1) * P], lambda k: lora[0:32, :], 1,
                                         ("v2", j, c), nk=1)
                    free_after(filled["scalar"], k2 + 1)
                else:
                    mark["mix_used", j, 0] = mark[("v", j), 7]
                square_linear(4, "A5", "A2", ("k", j), "mix_split")
                mark["mix_used", j, 1] = mark[("k", j), 7]
                square_linear(4, "A6", "A1", ("r", j), "mix_split")
                mark["mix_used", j, 2] = mark[("r", j), 7]
                sl1 = slab()
                w1 = sl1[:, 0:512].rearrange("p (k n) -> p k n", k=8)
                a1 = sl1[:, 512:1024].rearrange("p (k n) -> p k n", k=8)
                kw = linear_slab(lambda k, q: w1[:, k, :], mixed(3), 1, ("w1", j), "mix_ready", m=64)
                mark["mix_used", j, 3] = kw
                sl2 = slab()
                pe.wait_ge(drained["scalar"], kw + 1)
                for c in range(KC):
                    linear_slab(lambda k, q: sl2[0:64, c * P:(c + 1) * P], lambda k: lora[0:64, :], 1, ("w2", j, c), nk=1)
                ka = linear_slab(lambda k, q: a1[:, k, :], mixed(4), 1, ("a1", j), "mix_ready", m=64)
                mark["mix_used", j, 4] = ka
                free_after(filled["scalar"], ka + 1)
                pe.wait_ge(drained["scalar"], ka + 1)
                for c in range(KC):
                    k2 = linear_slab(lambda k, q: sl2[0:64, 1024 + c * P:1024 + (c + 1) * P],
                                     lambda k: lora[0:64, :], 1, ("a2", j, c), nk=1)
                free_after(filled["scalar"], k2 + 1)
                wg1 = slab()[:, 0:1024].rearrange("p (k n) -> p k n", k=8)
                kg = linear_slab(lambda k, q: wg1[:, k, :], mixed(5), 1, ("g1", j), "mix_ready")
                mark["mix_used", j, 5] = kg
                free_after(filled["scalar"], kg + 1)
                sl3 = slab()
                pe.wait_ge(drained["scalar"], kg + 1)
                for c in range(KC):
                    k2 = linear_slab(lambda k, q: sl3[:, c * P:(c + 1) * P], lambda k: lora[:, :], 1, ("g2", j, c), nk=1)
                free_after(filled["scalar"], k2 + 1)
                pe.wait_ge(sem("shift_saved"), after(pe, "shift_saved"))
                pe.wait_ge(*freed(6))
                mm = turn(bk[6][0:72, 0:P], spo_flat[:, 0:72], P)
                mm.then_inc(filled["scalar"], 1)
                result("scalar", 6)
                tile_stats(bones, "square_ready")
                tile_stats(bones, "bonus_product", "vector")

                pe.wait_ge(sem("operands_ready"), after(pe, "operands_ready"))
                K_, B_, V_ = S[4], S[1], S[3]
                for r in range(4):
                    kt = {}
                    for g in range(2):
                        c = 2 * r + g
                        for b in range(2):
                            pe.wait_ge(*freed(b))
                            for q, src in enumerate((V_, K_, B_)):
                                mm = turn(bk[b][:, q * P:(q + 1) * P], src[:, c, b * P:(b + 1) * P], P)
                            mm.then_inc(filled["scalar"], 1)
                            kt[g] = result("scalar", b)
                    masked = [0, 0]
                    for g in range(2):
                        c = 2 * r + g
                        yb, pb = lvl_banks(g)
                        for m in range(4):
                            hh, b = divmod(m, 2)
                            rows = slice(64 * hh, 64 * hh + 64)
                            bb = (yb, pb[0], pb[1], 1)[m]
                            pe.wait_ge(*freed(bb))
                            rhs = ARp[rows, c, b].rearrange("p q t -> p (q t)")
                            nc.tensor.matmul(bk[bb][:, 0:256], B_[rows, c, b * P:(b + 1) * P], rhs, start=True, stop=True)
                            mm = nc.tensor.matmul(bk[bb][:, 256:512], K_[rows, c, b * P:(b + 1) * P], rhs,
                                                  start=True, stop=True)
                            mm.then_inc(filled["vector"], 1)
                            masked[g] = result("vector", bb)
                    levels(masked, samples(rwkv_sample, [(j, 2 * r), (j, 2 * r + 1)]))
                    ks = [0, 0]
                    for b in range(2):
                        for g in range(2):
                            c = 2 * r + g
                            tg = tm[:, g, 0:768].rearrange("p (b q f) -> p b q f", b=2, q=3)
                            pe.wait_ge(drained["scalar"], kt[g] + 1)
                            bb = g
                            pe.wait_ge(*freed(bb))
                            if b:
                                pe.wait_ge(drained["vector"], ks[g] + 1)
                            if b:
                                nc.tensor.matmul(bk[bb][:, 0:P], ARp[:, c, b, 0, :], sp[:, g, :], start=True,
                                                 stop=False, skip_group_check=True)
                            for hh in range(2):
                                mm = nc.tensor.matmul(bk[bb][:, hh * 64:hh * 64 + 64], MX[:, g, 2 * hh + b, 2, :],
                                                      tg[:, b, 0, hh * 64:hh * 64 + 64], start=(b == 0),
                                                      stop=(b == 0 or hh == 1), skip_group_check=True)
                            mm.then_inc(filled["vector"], 1)
                            kr = result("vector", bb)
                            mark["r0", j, r, b, g] = kr
                        ku = [0, 0]
                        for g in range(2):
                            pe.wait_ge(drained["vector"], mark["r0", j, r, b, g] + 1)
                            pe.wait_ge(*freed(g))
                            for hh in range(2):
                                mm = nc.tensor.matmul(bk[g][:, hh * 64:hh * 64 + 64], T2[:, g, 2 * hh + b, 1, :],
                                                      rs[:, g, hh * 64:hh * 64 + 64], start=True, stop=True)
                            mm.then_inc(filled["scalar"], 1)
                            ku[g] = result("scalar", g)
                        for g in range(2):
                            c = 2 * r + g
                            tg = tm[:, g, 0:768].rearrange("p (b q f) -> p b q f", b=2, q=3)
                            pe.wait_ge(drained["scalar"], ku[g] + 1)
                            bb = 4 + g
                            pe.wait_ge(*freed(bb))
                            if b:
                                nc.tensor.matmul(bk[bb][:, 0:P], sp[:, g, :], ARp[:, c, b, 1, :],
                                                 start=True, stop=False, skip_group_check=True)
                            for hh in range(2):
                                rows = slice(64 * hh, 64 * hh + 64)
                                m = 2 * hh + b
                                o = bk[bb][rows, 0:P]
                                nc.tensor.matmul(o, tg[:, b, 0, hh * 64:hh * 64 + 64], MX[:, g, m, 3, :],
                                                 start=(b == 0), stop=False, skip_group_check=True)
                                mm = nc.tensor.matmul(o, nu[:, g, hh * 64:hh * 64 + 64], MX[:, g, m, 1, :],
                                                      start=False, stop=True, skip_group_check=True)
                            mm.then_inc(filled["scalar"], 1)
                            result("scalar", bb)
                            bb = 2 + g
                            pe.wait_ge(*freed(bb))
                            nc.tensor.matmul(bk[bb][:, 0:P], tg[:, b, 1, :], tg[:, b, 0, :], start=True, stop=False)
                            mm = nc.tensor.matmul(bk[bb][:, 0:P], tg[:, b, 2, :], nu[:, g, 0:P], start=False, stop=True)
                            mm.then_inc(filled["vector"], 1)
                            ks[g] = result("vector", bb)
                    for g in range(2):
                        pe.wait_ge(drained["vector"], ks[g] + 1)
                        pe.wait_ge(*freed(6 + g))
                        mm = turn(bk[6 + g][:, 0:P], sp[:, g, :], P)
                        mm.then_inc(filled["scalar"], 1)
                        result("scalar", 6 + g)

                for c in range(KC):
                    if c == 0:
                        pe.wait_ge(drained["scalar"], n_filled["scalar"] - 1 + 1)
                    b = 4 + c % 2
                    pe.wait_ge(*freed(b))
                    mm = nc.tensor.matmul(bk[b][:, 0:T], bones[:, :], S[5][:, c, :], start=True, stop=True)
                    mm.then_inc(filled["vector"], 1)
                    mark["mean", j, c] = result("vector", b)
                tile_stats(bones, "square_ready")
                square_linear(4, "A1", "A5", ("rwo", j), "mixer_out", stat=1)

            spo_flat = spo[:, :, :].rearrange("p a b -> p (a b)")

            def rwkv_sample(j, c):
                K_, B_, V_ = S[4], S[1], S[3]
                pe.wait_ge(sem("sample_state_in"), after_dma(pe, "sample_state_in", 2))
                pe.wait_ge(*freed(0))
                for b in range(NB):
                    mm = turn(bk[0][:, b * 64:(b + 1) * 64], sraw[0:64, b * P:(b + 1) * P], 64)
                mm.then_inc(filled["scalar"], 1)
                mark["sraw", "rwkv", j, c] = result("scalar", 0)
                pe.wait_ge(*freed(1))
                for q, src in enumerate((V_, K_, B_)):
                    mm = turn(bk[1][0:NS, q * P:(q + 1) * P], src[:, c, NPR:T], P)
                mm.then_inc(filled["scalar"], 1)
                ktm = mark["tms", "rwkv", j, c] = result("scalar", 1)
                yield
                for hh in range(2):
                    rows = slice(64 * hh, 64 * hh + 64)
                    rhs = ARs[rows, c].rearrange("p q t -> p (q t)")
                    pe.wait_ge(*freed(hh))
                    nc.tensor.matmul(bk[hh][0:NS, 0:64], B_[rows, c, NPR:T], rhs, start=True, stop=True)
                    mm = nc.tensor.matmul(bk[hh][0:NS, 64:128], K_[rows, c, NPR:T], rhs, start=True, stop=True)
                    mm.then_inc(filled["vector"], 1)
                    km = result("vector", hh)
                yield
                pe.wait_ge(drained["scalar"], ktm + 1)
                pe.wait_ge(drained["vector"], km + 1)
                pe.wait_ge(sem("spread_ready"), after(pe, "spread_ready"))
                pe.wait_ge(*freed(0))
                for hh in range(2):
                    o = bk[0][0:NS, hh * 64:hh * 64 + 64]
                    nc.tensor.matmul(o, ms[:, hh, 2, :], tms[:, 0, hh * 64:hh * 64 + 64], start=True, stop=False)
                    for b in range(NB):
                        mm = nc.tensor.matmul(o, ams[:, hh, b, :], sst[:, 0, b * 64:(b + 1) * 64],
                                              start=False, stop=(b == NB - 1))
                mm.then_inc(filled["vector"], 1)
                kx = result("vector", 0)
                for step in range(3):
                    yield
                    pe.wait_ge(drained["vector"], kx + 1)
                    bb = 1 - step % 2
                    pe.wait_ge(*freed(bb))
                    for hh in range(2):
                        mm = nc.tensor.matmul(bk[bb][0:NS, hh * 64:hh * 64 + 64], ms[:, hh, 0, :],
                                              us[:, step, hh * 64:hh * 64 + 64], start=True, stop=True)
                    mm.then_inc(filled["vector"], 1)
                    kx = result("vector", bb)
                yield
                pe.wait_ge(drained["vector"], kx + 1)
                pe.wait_ge(*freed(0))
                for hh in range(2):
                    rows = slice(64 * hh, 64 * hh + 64)
                    o = bk[0][rows, 0:NS]
                    nc.tensor.matmul(o, tms[:, 0, hh * 64:hh * 64 + 64], ms[:, hh, 3, :], start=True, stop=False)
                    nc.tensor.matmul(o, us[:, 3, hh * 64:hh * 64 + 64], ms[:, hh, 1, :], start=False, stop=False)
                    for b in range(NB):
                        mm = nc.tensor.matmul(o[:, b * NT:(b + 1) * NT], sst[:, 0, b * 64:(b + 1) * 64],
                                              rms_[:, hh, b * NT:(b + 1) * NT], start=False, stop=(b == NB - 1))
                mm.then_inc(filled["scalar"], 1)
                result("scalar", 0)
                for hh in range(2):
                    yield
                    pe.wait_ge(sem("values_spread"), after(pe, "values_spread"))
                    bb = 1 - hh
                    pe.wait_ge(*freed(bb))
                    nc.tensor.matmul(bk[bb][:, :], tms[:, 1, :], vms[:, 0, :], start=True, stop=False)
                    mm = nc.tensor.matmul(bk[bb][:, :], tms[:, 2, :], vms[:, 1, :], start=False, stop=True)
                    mm.then_inc(filled["vector"], 1)
                    result("vector", bb)
                yield
                pe.wait_ge(sem("sample_state_new"), after(pe, "sample_state_new"))
                for q in range(2):
                    pe.wait_ge(*freed(1 - q))
                    for i in range(4):
                        b = 4 * q + i
                        mm = turn(bk[1 - q][0:64, i * P:(i + 1) * P], sst[:, 1, b * 64:(b + 1) * 64], P)
                    mm.then_inc(filled["scalar"], 1)
                    result("scalar", 1 - q)

            def gdn():
                norm_stat(0)
                load_hist(72, "gdn")
                square_linear(16, "A3", "A0", "gin", "h_split")
                w = slab()[:, 0:128].rearrange("p (k n) -> p k n", k=8)
                linear_slab(lambda k, q: w[:, k, 0:8], lambda k: H[:, k, :], 1, "gbeta", m=8)
                i = linear_slab(lambda k, q: w[:, k, 8:16], lambda k: H[:, k, :], 1, "gdecay", m=8)
                free_after(filled["scalar"], i + 1)
                conv_state_out(72)
                tile_stats(ones, "square_ready")
                tile_stats(ones, "square_ready")
                pe.wait_ge(sem("decay_ready"), after(pe, "decay_ready"))
                pe.wait_ge(*freed(6))
                for blk, n in enumerate((P, P, NS)):
                    for q in range(2):
                        mm = turn(bk[6][0:n, blk * 16 + q * 8:blk * 16 + q * 8 + 8],
                                  g8[:, 2 * q, blk * P:blk * P + n], 8)
                mm.then_inc(filled["scalar"], 1)
                result("scalar", 6)
                for h in range(8):
                    b = 4 + h % 2
                    pe.wait_ge(*freed(b))
                    mm = nc.tensor.matmul(bk[b][:, 0:T], ident[0:8, h:h + 1].to_broadcast([8, P]), g8[:, 2, :], start=True, stop=True)
                    mm.then_inc(filled["scalar"], 1)
                    result("scalar", b)
                pe.wait_ge(sem("operands_ready"), after(pe, "operands_ready"))
                Q, K, V, QG = S[1], S[4], S[2], S[7]
                for r in range(2):
                    kt, ks, masked = {}, [0, 0], [0, 0]
                    for g in range(2):
                        for hh in range(2):
                            h = 4 * r + 2 * g + hh
                            pe.wait_ge(*freed(hh))
                            for q, (src, b) in enumerate(((V, 0), (K, 0), (V, 1), (K, 1))):
                                mm = turn(bk[hh][:, q * P:(q + 1) * P], src[:, h, b * P:(b + 1) * P], P)
                            mm.then_inc(filled["scalar"], 1)
                            kt[g] = mark["gtm", r, g] = result("scalar", hh)
                    for g in range(2):
                        yb, pb = lvl_banks(g)
                        for m in range(4):
                            hh, b = divmod(m, 2)
                            h = 4 * r + 2 * g + hh
                            bb = (yb, pb[0], pb[1], 1)[m]
                            pe.wait_ge(*freed(bb))
                            kk = K[:, h, b * P:(b + 1) * P]
                            nc.tensor.matmul(bk[bb][:, 0:P], kk, kk, start=True, stop=True)
                            mm = nc.tensor.matmul(bk[bb][:, P:2 * P], kk, Q[:, h, b * P:(b + 1) * P], start=True, stop=True)
                            mm.then_inc(filled["vector"], 1)
                            masked[g] = result("vector", bb)
                    levels(masked, samples(gdn_sample, [(4 * r + i,) for i in range(4)]))
                    for b in range(2):
                        kr = [0, 0]
                        if b:
                            for g in range(2):
                                pe.wait_ge(drained["vector"], ks[g] + 1)
                                pe.wait_ge(*freed(g))
                                for hh in range(2):
                                    h = 4 * r + 2 * g + hh
                                    mm = nc.tensor.matmul(bk[g][:, hh * P:(hh + 1) * P], K[:, h, P:2 * P],
                                                          gstate(g, hh), start=True, stop=True)
                                mm.then_inc(filled["vector"], 1)
                                kr[g] = result("vector", g)
                        kz = [0, 0]
                        for g in range(2):
                            tg = tm[:, g, :].rearrange("p (h b q f) -> p h b q f", h=2, b=2, q=2)
                            pe.wait_ge(drained["scalar"], kt[g] + 1)
                            if b:
                                pe.wait_ge(drained["vector"], kr[g] + 1)
                            pe.wait_ge(*freed(g))
                            for hh in range(2):
                                rhs = rs[:, g, hh * P:(hh + 1) * P] if b else tg[:, hh, 0, 0, :]
                                mm = nc.tensor.matmul(bk[g][:, hh * P:(hh + 1) * P], T2[:, g, 2 * hh + b, 1, :], rhs,
                                                      start=True, stop=True)
                            mm.then_inc(filled["scalar"], 1)
                            kz[g] = mark["z", r, b, g] = result("scalar", g)
                        for g in range(2):
                            tg = tm[:, g, :].rearrange("p (h b q f) -> p h b q f", h=2, b=2, q=2)
                            pe.wait_ge(drained["scalar"], kz[g] + 1)
                            bb = 4 + g
                            pe.wait_ge(*freed(bb))
                            for hh in range(2):
                                h = 4 * r + 2 * g + hh
                                o = bk[bb][:, hh * P:(hh + 1) * P]
                                mm = nc.tensor.matmul(o, nu[:, g, hh * P:(hh + 1) * P], MX[:, g, 2 * hh + b, 1, :],
                                                      start=True, stop=(b == 0))
                                if b:
                                    mm = nc.tensor.matmul(o, gstate(g, hh), QG[:, h, P:2 * P], start=False, stop=True)
                            mm.then_inc(filled["scalar"], 1)
                            result("scalar", bb)
                            pe.wait_ge(sem("xd_ready"), after(pe, "xd_ready"))
                            bb = 2 + g
                            pe.wait_ge(*freed(bb))
                            for hh in range(2):
                                mm = nc.tensor.matmul(bk[bb][:, hh * P:(hh + 1) * P], tg[:, hh, b, 1, :],
                                                      xd[:, g, hh * P:(hh + 1) * P], start=True, stop=True)
                            mm.then_inc(filled["vector"], 1)
                            ks[g] = mark["gstate", r, b, g] = result("vector", bb)
                tile_norm_out("gwo")

            def tile_norm_out(name):
                tile_stats(ones, "square_ready")
                square_linear(4, "A1", "A5", name, "mixer_out", stat=1)

            def gdn_sample(h):
                Q, K, V, QG = S[1], S[4], S[2], S[7]
                pe.wait_ge(*freed(0))
                for q, src in enumerate((V, K)):
                    mm = turn(bk[0][0:NS, q * P:(q + 1) * P], src[:, h, NPR:T], P)
                mm.then_inc(filled["scalar"], 1)
                ktm = mark["tms", "gdn", h] = result("scalar", 0)
                yield
                pe.wait_ge(*freed(1))
                nc.tensor.matmul(bk[1][0:NS, 0:NS], K[:, h, NPR:T], K[:, h, NPR:T], start=True, stop=True)
                mm = nc.tensor.matmul(bk[1][0:NS, NS:2 * NS], K[:, h, NPR:T], Q[:, h, NPR:T], start=True, stop=True)
                mm.then_inc(filled["vector"], 1)
                result("vector", 1)
                yield
                pe.wait_ge(sem(f"head_state_in{h % 2}"), after_dma(pe, f"head_state_in{h % 2}"))
                pe.wait_ge(sem("spread_ready"), after(pe, "spread_ready"))
                pe.wait_ge(*freed(0))
                for b in range(NB):
                    mm = nc.tensor.matmul(bk[0][0:NS, 0:P], ams[:, 0, b, :], head_state(h)[:, b * P:(b + 1) * P],
                                          start=(b == 0), stop=(b == NB - 1))
                mm.then_inc(filled["vector"], 1)
                kx = result("vector", 0)
                pe.wait_ge(drained["scalar"], ktm + 1)
                for step in range(3):
                    yield
                    pe.wait_ge(drained["vector"], kx + 1)
                    bb = 1 - step % 2
                    pe.wait_ge(*freed(bb))
                    mm = nc.tensor.matmul(bk[bb][0:NS, 0:P], ms[:, 0, 0, :], us[:, step, :], start=True, stop=True)
                    mm.then_inc(filled["vector"], 1)
                    kx = result("vector", bb)
                yield
                pe.wait_ge(sem("x_scaled"), after(pe, "x_scaled"))
                pe.wait_ge(*freed(0))
                nc.tensor.matmul(bk[0][:, 0:NS], us[:, 3, :], ms[:, 0, 1, :], start=True, stop=False)
                for b in range(NB):
                    mm = nc.tensor.matmul(bk[0][:, b * NT:(b + 1) * NT], head_state(h)[:, b * P:(b + 1) * P],
                                          QG[:, h, NPR + b * NT:NPR + (b + 1) * NT], start=False, stop=(b == NB - 1))
                mm.then_inc(filled["scalar"], 1)
                result("scalar", 0)
                pe.wait_ge(sem("values_spread"), after(pe, "values_spread"))
                for q in range(2):
                    pe.wait_ge(*freed(1 - q))
                    nc.tensor.matmul(bk[1 - q], tms[:, 1, :], vms[:, q, :], start=True, stop=True).then_inc(filled["vector"], 1)
                    mark["sraw", "gdn", h] = result("vector", 1 - q)

            def gstate(g, hh):
                return (sp if hh == 0 else spo)[:, g, :]

            def hgrn():
                norm_stat(0)
                square_linear(16, "A7", "H", "hin", "h_split")
                Q, K, V, QG, KD, QL, KL = S[0], S[2], S[4], S[5], S[6], H, SQ
                for l in range(LEVELS + 1):
                    pe.wait_ge(sem("level_operands"), after(pe, "level_operands"))
                    q_, k_ = (Q, K) if l == 0 else (QL, KL)
                    for n in range(4):
                        bb = n
                        pe.wait_ge(*freed(bb))
                        for i in range(4):
                            h, b = divmod(4 * n + i, 2)
                            mm = nc.tensor.matmul(bk[bb][:, i * P:(i + 1) * P], k_[:, h, b * P:(b + 1) * P],
                                                  q_[:, h, b * P:(b + 1) * P], start=True, stop=True)
                        mm.then_inc(filled["vector"], 1)
                        result("vector", bb)
                    if l <= 2:
                        pe.wait_ge(*freed(4))
                        for h in range(8):
                            mm = nc.tensor.matmul(bk[4][0:NS, h * NS:(h + 1) * NS], k_[:, h, NPR:T], q_[:, h, NPR:T],
                                                  start=True, stop=True)
                        mm.then_inc(filled["vector"], 1)
                        result("vector", 4)
                pe.wait_ge(drained["vector"], n_filled["vector"] - 1 + 1)
                AT = flat("A1")[:, 0:2048].rearrange("p (h b t) -> p h b t", h=8, b=2)
                ATS = flat("A1")[0:NS, 2048:2304].rearrange("p (h t) -> p h t", h=8)
                kt, ktm = {}, {}

                def token_major(h):
                    g = h % 2
                    pe.wait_ge(*freed(g))
                    for q, (src, b) in enumerate(((V, 0), (KD, 0), (V, 1), (KD, 1))):
                        mm = turn(bk[g][:, q * P:(q + 1) * P], src[:, h, b * P:(b + 1) * P], P)
                    mm.then_inc(filled["scalar"], 1)
                    kt[h] = result("scalar", g)
                    pe.wait_ge(*freed(2 + g))
                    for q, src in enumerate((V, KD)):
                        mm = turn(bk[2 + g][0:NS, q * P:(q + 1) * P], src[:, h, NPR:T], P)
                    mm.then_inc(filled["scalar"], 1)
                    ktm[h] = mark["tms", "hgrn", h] = result("scalar", 2 + g)

                token_major(0)
                for h in range(8):
                    g = h % 2
                    tmg = (tms, us)[g]
                    pe.wait_ge(drained["scalar"], kt[h] + 1)
                    tg = tm[:, g, 0:512].rearrange("p (b q f) -> p b q f", b=2, q=2)
                    for b in range(2):
                        if b:
                            pe.wait_ge(drained["vector"], ks + 1)
                        pe.wait_ge(*freed(5))
                        mm = nc.tensor.matmul(bk[5][:, 0:P], tg[:, b, 0, :], AT[:, h, b, :], start=True, stop=(b == 0))
                        if b:
                            mm = nc.tensor.matmul(bk[5][:, 0:P], sp[:, g, :], QG[:, h, P:2 * P], start=False, stop=True)
                        mm.then_inc(filled["scalar"], 1)
                        result("scalar", 5)
                        pe.wait_ge(*freed(4))
                        mm = nc.tensor.matmul(bk[4][:, 0:P], tg[:, b, 1, :], tg[:, b, 0, :], start=True, stop=True)
                        mm.then_inc(filled["vector"], 1)
                        ks = result("vector", 4)
                        if b == 0 and h < 7:
                            token_major(h + 1)
                    mark["hstate", h] = ks
                    pe.wait_ge(drained["scalar"], ktm[h] + 1)
                    pe.wait_ge(sem(f"head_state_in{h % 2}"), after_dma(pe, f"head_state_in{h % 2}"))
                    pe.wait_ge(*freed(5))
                    nc.tensor.matmul(bk[5][:, 0:NS], tmg[:, 0, :], ATS[:, h, :], start=True, stop=False)
                    for b in range(NB):
                        mm = nc.tensor.matmul(bk[5][:, b * NT:(b + 1) * NT], head_state(h)[:, b * P:(b + 1) * P],
                                              QG[:, h, NPR + b * NT:NPR + (b + 1) * NT], start=False, stop=(b == NB - 1))
                    mm.then_inc(filled["scalar"], 1)
                    result("scalar", 5)
                    pe.wait_ge(sem("values_spread"), after(pe, "values_spread"))
                    for q in range(2):
                        pe.wait_ge(*freed(6 + q))
                        nc.tensor.matmul(bk[6 + q], tmg[:, 1, :], vms[:, q, :], start=True, stop=True).then_inc(filled["vector"], 1)
                        mark["sraw", "hgrn", h] = result("vector", 6 + q)
                tile_norm_out("hwo")

            pe.wait_ge(sem("basics_ready"), after(pe, "basics_ready"))
            pe.wait_ge(sem("params_landed"), after_dma(pe, "params_landed", PARAM_DMAS))
            for n, rows in enumerate(PARAM_ROWS):
                b = 6 + n % 2
                pe.wait_ge(*freed(b))
                mm = turn(bk[b][:, 0:rows], flat("A2", 1)[0:rows, n * P:(n + 1) * P], rows)
                mm.then_inc(filled["scalar"], 1)
                result("scalar", b)
            xin = flat("A0", 2)[:, 0:3072].rearrange("p (b f) -> p b f", b=3)
            pe.wait_ge(sem("x_landed"), after_dma(pe, "x_landed", 2))
            for blk, n in enumerate((P, P, NS)):
                for q in range(2):
                    b = 2 * (blk % 2) + q
                    pe.wait_ge(*freed(b))
                    for i in range(4):
                        mm = turn(bk[b][:, i * P:i * P + n], xin[0:n, blk, (4 * q + i) * P:(4 * q + i + 1) * P], n)
                    mm.then_inc(filled["scalar"], 1)
                    result("scalar", b)
            rwkv(0)
            ffn(0)
            gdn()
            ffn(1)
            hgrn()
            ffn(2)
            rwkv(1)
            ffn(3)
            pe.wait_ge(sem("x_ready"), after(pe, "x_ready", 2 * DEPTH * KC))
            for blk, n in enumerate((P, P, NS)):
                for q in range(2):
                    b = 2 * (blk % 2) + q
                    pe.wait_ge(*freed(b))
                    for i in range(4):
                        mm = turn(bk[b][0:n, i * P:(i + 1) * P], X[:, 4 * q + i, blk * P:blk * P + n], P)
                    mm.then_inc(filled["scalar"], 1)
                    result("scalar", b)

        @block.scalar
        def _(act):
            n_taken = {"n": 0}

            def take():
                n_taken["n"] += 1
                return n_taken["n"]

            def fn(out, in_, f, bias=0.0, scale=1.0):
                if f == ACT.Copy and not isinstance(bias, float):
                    f = ACT.Identity
                return nc.scalar.activation(out, in_, f, bias=bias, scale=scale)

            def squares(src, hear_name=None):
                for c in range(KC):
                    if hear_name:
                        act.wait_ge(sem(hear_name), after(act, hear_name))
                    fn(SQ[:, c, :], src[:, c, :], ACT.Square).then_inc(signal("square_ready"), 1)

            def rms():
                act.wait_ge(filled["scalar"], take())
                fn(rstd[:, :], bk4(n_taken["n"]), ACT.Ln, bias=eps[:, 0:1], scale=1.0 / D).then_inc(drained["scalar"], 1)
                act.wait_ge(drained["scalar"], n_taken["n"])
                fn(rstd[:, :], rstd[:, :], ACT.Exp, scale=-0.5).then_inc(signal("rstd_ready"), 1)
                act.wait_ge(sem("rstd_ready"), told["rstd_ready"])

            def bk4(n):
                return bk[act_bank[n - 1]][:, 0:T]

            def ps(m=P):
                return bk[act_bank[n_taken["n"] - 1]][0:m, 0:T]

            def psb():
                return bk[act_bank[n_taken["n"] - 1]]

            def evac(dst, f=ACT.Copy, bias=0.0, m=P):
                act.wait_ge(filled["scalar"], take())
                fn(dst, ps(m), f, bias=bias).then_inc(drained["scalar"], 1)
                act.wait_ge(drained["scalar"], n_taken["n"])

            def split_hi(n):
                act.wait_ge(landed[n % RING], landed_at[n])
                o = split_order.index(n)
                if o >= 2:
                    act.wait_ge(*release[split_order[o - 2]])
                fn(w_hi[:, hi_slot(n), 0:slab_size(n)], ring[:, n % RING, 0:slab_size(n)], ACT.Copy).then_inc(signal("hi_ready"), 1)

            def pre_norm(first_slab):
                squares(X, "x_ready")
                hear_state_out()
                split_hi(first_slab)
                split_hi(first_slab + 1)
                rms()

            def out_projection(tiles=range(KC), out=S[3], sq=SQ):
                for c in tiles:
                    evac(out[:, c, :])
                    fn(sq[:, c, :], out[:, c, :], ACT.Square).then_inc(signal("square_ready"), 1)

            def split_out_projection(n0):
                for s in range(4):
                    out_projection((2 * s, 2 * s + 1))
                    if s < 2:
                        split_hi(n0 + s + 2)

            def first_hi(n0):
                hear_state_out()
                split_hi(n0)
                split_hi(n0 + 1)

            def head_rstd(dst, scale, e):
                for c in range(KC):
                    act.wait_ge(filled["scalar"], take())
                    fn(dst[:, c, :], ps(), ACT.Ln, bias=eps[:, e:e + 1], scale=scale).then_inc(drained["scalar"], 1)
                    act.wait_ge(drained["scalar"], n_taken["n"])
                fn(dst, dst, ACT.Exp, scale=-0.5).then_inc(signal("rk_ready"), 1)
                act.wait_ge(sem("rk_ready"), told["rk_ready"])

            def take_hist(rows):
                for q in range(2):
                    act.wait_ge(filled["scalar"], take())
                    fn(hist[:, q * 4:q * 4 + 4, 0:rows],
                             psb()[:, 0:352].rearrange("p (i r) -> p i r", i=4)[:, :, 0:rows], ACT.Copy).then_inc(drained["scalar"], 1)
                    act.wait_ge(drained["scalar"], n_taken["n"])

            def conv_state_out(prompt_out, sample_out, rows, width):
                stage = tm[:, :, :].rearrange("p a b -> p (a b)")[0:rows, 0:9 * P].rearrange("r (b f) -> r b f", b=9)
                hear_conv_out()
                state["conv"] += 32
                for q in range(3):
                    act.wait_ge(filled["scalar"], take())
                    fn(stage[:, 3 * q:3 * q + 3, :],
                             psb()[0:rows, 0:3 * P].rearrange("r (b f) -> r b f", b=3), ACT.Copy).then_inc(drained["scalar"], 1)
                    act.wait_ge(drained["scalar"], n_taken["n"])
                act.dma_start(prompt_out.rearrange("b w (c f) -> (w c) b f", f=P), stage[:, 0:1, :]).then_inc(sem("conv_state_out"), 16)
                act.dma_start(sample_out.rearrange("b w (c f) -> (w c) b f", f=P), stage[:, 1:9, :]).then_inc(sem("conv_state_out"), 16)

            def two_part(dst_p, dst_s, src_p, src_s, f):
                fn(dst_p, src_p, f)
                return fn(dst_s, src_s, f)

            def ffn(i):
                n0 = plan.index(("up", i, 0, 0))
                pre_norm(n0)
                take_hist(88)
                for c in range(KC):
                    act.wait_ge(sem("h_to_split"), after(act, "h_to_split"))
                    fn(act3r("A4")[:, c, :], H[:, c, :], ACT.Copy).then_inc(signal("x_hi"), 1)
                lead = FW - 1

                def gate(p):
                    for q in range(2):
                        act.wait_ge(sem("gate_conv"), after(act, "gate_conv"))
                        cv = buf(4 + (p % 2) * 4 + 2 + q, lead)[:, 0:NPR + NB * (lead + NT)]
                        fn(cv, cv, ACT.Silu).then_inc(signal("silu_ready"), 1)

                def hidden_hi(p):
                    for kt in (2 * p, 2 * p + 1):
                        act.wait_ge(sem("y_made"), after(act, "y_made"))
                        fn(y_hi(kt), flat("A0", 3)[:, kt * T:(kt + 1) * T], ACT.Copy).then_inc(signal("y_hi"), 1)

                for p in range(FPAIR):
                    for half in range(2):
                        if half and p:
                            gate(p - 1)
                        for q in range(2):
                            act.wait_ge(filled["scalar"], take())
                            if p:
                                act.wait_ge(sem("saved"), after(act, "saved"))
                                if not half:
                                    act.wait_ge(sem("value_conv"), after(act, "value_conv"))
                            dp, ds = split(buf(half * 2 + q, lead), lead)
                            two_part(dp, ds, psb()[:, 0:NPR], psb()[:, NPR:T].rearrange("p (b t) -> p b t", b=NB), ACT.Copy).then_inc(drained["scalar"], 1)
                            act.wait_ge(drained["scalar"], n_taken["n"])
                        split_hi(n0 + 2 * p + half + 2)
                        if not half and p >= 2:
                            hidden_hi(p - 2)
                gate(FPAIR - 1)
                hidden_hi(FPAIR - 2)
                hidden_hi(FPAIR - 1)
                act.wait_ge(sem("saved"), after(act, "saved", 4))
                act.wait_ge(sem("value_conv"), after(act, "value_conv", 2))
                for s in range(2, 12):
                    split_hi(n0 + 2 * FPAIR + s)
                    if s % 3 == 1:
                        m = (s - 4) // 3
                        out_projection((2 * m, 2 * m + 1), S[4], H)
                out_projection((6, 7), S[4], H)
                rms()
                conv_state_out(OUT["prompt_ffn_conv"][i], OUT["sample_ffn_conv"][i], 88, 2)

            def shift_out(j):
                act.wait_ge(filled["scalar"], take())
                hear_state_out()
                fn(sout[0:72, 0:P], psb()[0:72, 0:P], ACT.Copy).then_inc(drained["scalar"], 1)
                act.wait_ge(drained["scalar"], n_taken["n"])
                o = sem("sample_state_out")
                act.dma_start(OUT["prompt_shift"][j].rearrange("b (c f) -> (b c) f", f=P), sout[0:8, 0:P]).then_inc(o, 16)
                act.dma_start(OUT["sample_shift"][j].rearrange("b (c f) -> (b c) f", f=P), sout[8:72, 0:P]).then_inc(o, 16)
                state["out"] += 32

            state = {"out": 0, "pout": 0, "conv": 0}

            def hear_conv_out():
                if state["conv"]:
                    act.wait_ge(sem("conv_state_out"), state["conv"])

            def hear_state_out():
                if state["out"]:
                    act.wait_ge(sem("sample_state_out"), state["out"])

            def hear_prompt_out():
                if state["pout"]:
                    act.wait_ge(sem("prompt_state_out"), state["pout"])

            def rwkv(j):
                n0 = plan.index(("rkv", j, 2, 0))
                slabs = [plan.index(("rkv", j, q, m)) for q in (2, 1, 0) for m in range(4)]
                pre_norm(n0)

                def project(dst, first):
                    for c in range(KC):
                        evac(dst[:, c, :])
                        if c % 2 and first + c // 2 + 2 < len(slabs):
                            split_hi(slabs[first + c // 2 + 2])

                project(S[3], 0)
                if j:
                    act.wait_ge(sem("v_first_kept"), 16)
                    act.dma_start(S[8], A["v_first"].rearrange("(c p) t -> p c t", p=P)).then_inc(sem("v_first_back"), 16)
                    evac(lora[0:32, :], m=32)
                    for c in range(KC):
                        evac(SQ[:, c, :], ACT.Sigmoid, pcol("v0", 0, c))
                else:
                    act.dma_start(A["v_first"].rearrange("(c p) t -> p c t", p=P), S[3]).then_inc(sem("v_first_kept"), 16)
                project(S[4], 4)
                project(S[5], 8)
                evac(lora[0:64, :], ACT.Tanh, m=64)
                for c in range(KC):
                    evac(S[6][:, c, :], ACT.Sigmoid, pcol("w0", j, c))
                evac(lora[0:64, :], m=64)
                for c in range(KC):
                    evac(S[7][:, c, :], ACT.Sigmoid, pcol("a0", j, c))
                evac(lora[:, :], ACT.Sigmoid)
                if j:
                    act.wait_ge(sem("v_mixed"), after(act, "v_mixed"))
                for c in range(KC):
                    evac(S[8][:, c, :])
                shift_out(j)
                squares(S[0], "kk_raw")
                head_rstd(S[1], 1.0, 0)
                act.wait_ge(sem("ge_ready"), after(act, "ge_ready"))
                fn(cen[:, 1], cen[:, 0], ACT.Exp).then_inc(signal("scalar_chain"), 1)
                act.wait_ge(sem("scalar_chain"), told["scalar_chain"])
                fn(S[2], S[2], ACT.Exp).then_inc(signal("e_excl"), 1)
                act.wait_ge(sem("e_excl"), told["e_excl"])
                act.wait_ge(sem("a_done"), after(act, "a_done"))
                fn(S[0], H, ACT.Exp).then_inc(signal("e_incl"), 1)
                act.wait_ge(sem("e_incl"), told["e_incl"])
                fn(H, H, ACT.Exp, scale=-1.0).then_inc(signal("e_neg"), 1)
                act.wait_ge(sem("e_neg"), told["e_neg"])
                for r in range(4):
                    for g in range(2):
                        for b in range(2):
                            act.wait_ge(filled["scalar"], take())
                            if r == 0 and g == 0 and b == 0:
                                hear_conv_out()
                            fn(tm[:, g, b * 384:(b + 1) * 384], psb()[:, 0:384], ACT.Copy).then_inc(drained["scalar"], 1)
                            act.wait_ge(drained["scalar"], n_taken["n"])
                    for g in range(2):
                        c = 2 * r + g
                        act.wait_ge(filled["scalar"], take())
                        fn(sst[:, 0, :], psb(), ACT.Copy).then_inc(drained["scalar"], 1)
                        act.wait_ge(drained["scalar"], n_taken["n"])
                        act.wait_ge(filled["scalar"], take())
                        fn(tms[:, :, :], psb()[0:NS, 0:384].rearrange("s (q f) -> s q f", q=3), ACT.Copy).then_inc(drained["scalar"], 1)
                        act.wait_ge(drained["scalar"], n_taken["n"])
                        act.wait_ge(filled["scalar"], take())
                        fn(S[5][:, c, NPR:T], psb()[:, 0:NS], ACT.Copy).then_inc(drained["scalar"], 1)
                        act.wait_ge(drained["scalar"], n_taken["n"])
                        hear_state_out()
                        for q in range(2):
                            act.wait_ge(filled["scalar"], take())
                            fn(sout[0:64, q * 512:(q + 1) * 512], psb()[0:64, :], ACT.Copy).then_inc(drained["scalar"], 1)
                            act.wait_ge(drained["scalar"], n_taken["n"])
                        so = sout[0:64, :].rearrange("v (b h k) -> v b h k", b=NB, h=2)
                        for hh in range(2):
                            act.dma_start(OUT["sample_wkv"][j, :, 2 * c + hh].rearrange("b v k -> v b k"),
                                          so[:, :, hh, :]).then_inc(sem("sample_state_out"), 16)
                        state["out"] += 32
                    for b in range(2):
                        for g in range(2):
                            act.wait_ge(filled["scalar"], take())
                            fn(nu[:, g, 0:P], psb()[:, 0:P], ACT.Copy, scale=-1.0).then_inc(drained["scalar"], 1)
                            act.wait_ge(drained["scalar"], n_taken["n"])
                        for g in range(2):
                            act.wait_ge(filled["scalar"], take())
                            fn(S[5][:, 2 * r + g, b * P:(b + 1) * P], psb()[:, 0:P], ACT.Copy).then_inc(drained["scalar"], 1)
                            act.wait_ge(drained["scalar"], n_taken["n"])
                    hear_prompt_out()
                    for g in range(2):
                        act.wait_ge(filled["scalar"], take())
                        fn(spo[:, g, :], psb()[:, 0:P], ACT.Copy).then_inc(drained["scalar"], 1)
                        act.wait_ge(drained["scalar"], n_taken["n"])
                        c = 2 * r + g
                        for hh in range(2):
                            rows = slice(64 * hh, 64 * hh + 64)
                            act.dma_start(OUT["prompt_wkv"][j, 0, 2 * c + hh], spo[rows, g, rows]).then_inc(
                                sem("prompt_state_out"), 16)
                            state["pout"] += 16
                for c in range(KC):
                    act.wait_ge(drained["vector"], mark["mean", j, c] + 1)
                    fn(SQ[:, c, :], S[5][:, c, :], ACT.Square).then_inc(signal("square_ready"), 1)
                first_hi(plan.index(("rwo", j, 0)))
                head_rstd(H, 1.0 / 64, 1)
                split_out_projection(plan.index(("rwo", j, 0)))
                rms()

            def gdn():
                n0 = plan.index(("gin", 0))
                pre_norm(n0)
                take_hist(72)
                lead = GW - 1
                dst = (S[1], S[4], S[2])

                def qkv(n):
                    act.wait_ge(sem("gconv"), after(act, "gconv"))
                    cv = buf(4 + n % 4, lead)
                    d = dst[n // KC][:, n % KC, :]
                    ins = two_part(d[:, 0:NPR], d[:, NPR:T].rearrange("p (b t) -> p b t", b=NB), cv[:, 0:NPR],
                                   cv[:, lead + NPR:span(lead)].rearrange("p (b t) -> p b t", b=NB)[:, :, 0:NT], ACT.Silu)
                    ins.then_inc(signal("qkv_ready"), 1)
                    act.wait_ge(sem("qkv_ready"), told["qkv_ready"])

                for n in range(GT):
                    act.wait_ge(filled["scalar"], take())
                    if n >= 4:
                        act.wait_ge(sem("saved"), after(act, "saved"))
                    dp, ds = split(buf(n % 4, lead), lead)
                    two_part(dp, ds, psb()[:, 0:NPR], psb()[:, NPR:T].rearrange("p (b t) -> p b t", b=NB), ACT.Copy).then_inc(drained["scalar"], 1)
                    act.wait_ge(drained["scalar"], n_taken["n"])
                    if n % 2:
                        split_hi(n0 + n // 2 + 2)
                    if n >= 2:
                        qkv(n - 2)
                qkv(GT - 2)
                qkv(GT - 1)
                act.wait_ge(sem("saved"), after(act, "saved", 4))
                for c in range(KC):
                    evac(S[8][:, c, :], ACT.Silu)
                    if c in (1, 3):
                        split_hi(n0 + (GT + c) // 2 + 2)
                hear_state_out()
                evac(g8[:, 0, :], ACT.Sigmoid, m=8)
                evac(g8[:, 1, :], ACT.Identity, gpar[:, 1:2], m=8)
                fn(g8[:, 2, :], g8[:, 1, :], ACT.Abs).then_inc(signal("scalar_chain"), 1)
                act.wait_ge(sem("scalar_chain"), told["scalar_chain"])
                fn(g8[:, 2, :], g8[:, 2, :], ACT.Exp, scale=-1.0).then_inc(signal("scalar_chain"), 1)
                act.wait_ge(sem("scalar_chain"), told["scalar_chain"])
                fn(g8[:, 2, :], g8[:, 2, :], ACT.Ln, bias=1.0).then_inc(signal("softplus_ready"), 1)
                act.wait_ge(sem("softplus_ready"), told["softplus_ready"])
                conv_state_out(OUT["prompt_gdn_conv"][0], OUT["sample_gdn_conv"][0], 72, 3)
                squares(S[1])
                head_rstd(S[3], 1.0, 0)
                squares(S[4])
                head_rstd(SQ, 1.0, 0)
                act.wait_ge(filled["scalar"], take())
                fn(tb[:, 0:2, :], psb()[:, 0:32].rearrange("p (b q) -> p b q", b=2), ACT.Copy)
                fn(tb[0:NS, 2, :], psb()[0:NS, 32:48], ACT.Copy).then_inc(drained["scalar"], 1)
                act.wait_ge(drained["scalar"], n_taken["n"])
                fn(neg[:, 0:2, :], tb[:, 0:2, 8:16], ACT.Exp)
                fn(neg[0:NS, 2, :], tb[0:NS, 2, 8:16], ACT.Exp).then_inc(signal("scalar_chain"), 1)
                act.wait_ge(sem("scalar_chain"), told["scalar_chain"])
                fn(neg[:, 0:2, :], neg[:, 0:2, :], ACT.Copy, scale=-1.0)
                fn(neg[0:NS, 2, :], neg[0:NS, 2, :], ACT.Copy, scale=-1.0).then_inc(signal("scalar_chain"), 1)
                act.wait_ge(sem("scalar_chain"), told["scalar_chain"])
                for h in range(8):
                    evac(S[6][:, h, :])
                act.wait_ge(sem("qk_done"), after(act, "qk_done"))
                fn(S[3], S[6], ACT.Exp).then_inc(signal("eg_ready"), 1)
                act.wait_ge(sem("eg_ready"), told["eg_ready"])
                hear_conv_out()
                for r in range(2):
                    for g in range(2):
                        for hh in range(2):
                            act.wait_ge(filled["scalar"], take())
                            fn(tm[:, g, hh * 512:(hh + 1) * 512], psb(), ACT.Copy).then_inc(drained["scalar"], 1)
                            act.wait_ge(drained["scalar"], n_taken["n"])
                    for g in range(2):
                        act.wait_ge(sem("exponents_ready"), after(act, "exponents_ready"))
                        fn(ysb[:, g, :], ysb[:, g, :], ACT.Exp).then_inc(signal("decays_exp"), 1)
                        act.wait_ge(sem("decays_exp"), told["decays_exp"])
                    for g in range(2):
                        for hh in range(2):
                            h = 4 * r + 2 * g + hh
                            act.wait_ge(sem("sample_exponents"), after(act, "sample_exponents"))
                            fn(ms[:, 1, 0, :], ms[:, 1, 0, :], ACT.Exp).then_inc(signal("sample_decays"), 1)
                            act.wait_ge(sem("sample_decays"), told["sample_decays"])
                            act.wait_ge(filled["scalar"], take())
                            fn(tms[:, 0:2, :], psb()[0:NS, 0:256].rearrange("s (q f) -> s q f", q=2), ACT.Copy).then_inc(drained["scalar"], 1)
                            act.wait_ge(drained["scalar"], n_taken["n"])
                            act.wait_ge(filled["scalar"], take())
                            fn(S[5][:, h, NPR:T], psb()[:, 0:NS], ACT.Copy).then_inc(drained["scalar"], 1)
                            act.wait_ge(drained["scalar"], n_taken["n"])
                            sample_out(OUT["sample_gdn_S"], "gdn", h)
                    for b in range(2):
                        for g in range(2):
                            act.wait_ge(filled["scalar"], take())
                            for hh in range(2):
                                h = 4 * r + 2 * g + hh
                                ins = fn(nu[:, g, hh * P:(hh + 1) * P], psb()[:, hh * P:(hh + 1) * P], ACT.Copy,
                                         scale=tb[:, b, h:h + 1])
                            ins.then_inc(drained["scalar"], 1)
                            act.wait_ge(drained["scalar"], n_taken["n"])
                        for g in range(2):
                            act.wait_ge(filled["scalar"], take())
                            fn(S[5][:, 4 * r + 2 * g:4 * r + 2 * g + 2, b * P:(b + 1) * P],
                                     psb()[:, 0:256].rearrange("p (h t) -> p h t", h=2), ACT.Copy).then_inc(drained["scalar"], 1)
                            act.wait_ge(drained["scalar"], n_taken["n"])
                    for g in range(2):
                        act.wait_ge(drained["vector"], mark["gstate", r, 1, g] + 1)
                        for hh in range(2):
                            act.dma_start(OUT["prompt_gdn_S"][0, 0, 4 * r + 2 * g + hh],
                                          (sp, spo)[hh][:, g, :]).then_inc(sem("prompt_state_out"), 16)
                            state["pout"] += 16
                finish_heads(plan.index(("gwo", 0)))

            def sample_out(out, kind, h):
                act.wait_ge(drained["vector"], mark["sraw", kind, h] + 1)
                act.dma_start(out[0, :, h].rearrange("b k v -> k b v"),
                              sout[:, :].rearrange("p (b v) -> p b v", b=NB)).then_inc(sem("sample_state_out"), 16)
                state["out"] += 16

            def finish_heads(n0):
                squares(S[5])
                first_hi(n0)
                head_rstd(H, 1.0 / P, 0)
                split_out_projection(n0)
                rms()

            def hgrn():
                n0 = plan.index(("hin", 0))
                pre_norm(n0)
                for q, (dst, f) in enumerate(((S[0], ACT.Silu), (S[1], ACT.Sigmoid), (S[4], ACT.Copy), (S[8], ACT.Silu))):
                    for c in range(KC):
                        evac(dst[:, c, :], f)
                        slab = q * 4 + c // 2 + 2
                        if c % 2 and slab < 16:
                            split_hi(n0 + slab)
                        if q == 2 and c == KC - 1:
                            act.wait_ge(sem("f_ready"), after(act, "f_ready"))
                            fn(S[1], S[1], ACT.Ln).then_inc(signal("log_f_ready"), 1)
                            act.wait_ge(sem("log_f_ready"), told["log_f_ready"])
                        if q == 3 and c == 3:
                            act.wait_ge(sem("cumulated"), after(act, "cumulated"))
                            fn(S[5], S[3], ACT.Exp).then_inc(signal("exp_cumulated"), 1)
                            act.wait_ge(sem("exp_cumulated"), told["exp_cumulated"])
                            act.wait_ge(sem("to_end_ready"), after(act, "to_end_ready"))
                            fn(S[6], S[6], ACT.Exp).then_inc(signal("exp_to_end"), 1)
                            act.wait_ge(sem("exp_to_end"), told["exp_to_end"])
                for l in range(1, LEVELS + 1):
                    act.wait_ge(sem("distance_ready"), after(act, "distance_ready"))
                    e = S[7] if l <= 2 else S[7][:, :, 0:NPR]
                    fn(e, e, ACT.Abs).then_inc(signal("scalar_chain"), 1)
                    act.wait_ge(sem("scalar_chain"), told["scalar_chain"])
                    fn(e, e, ACT.Exp, scale=-1.0).then_inc(signal("distance_exp"), 1)
                    act.wait_ge(sem("distance_exp"), told["distance_exp"])
                hear_conv_out()

                def token_major(h):
                    act.wait_ge(filled["scalar"], take())
                    fn(tm[:, h % 2, 0:512], psb(), ACT.Copy).then_inc(drained["scalar"], 1)
                    act.wait_ge(drained["scalar"], n_taken["n"])
                    act.wait_ge(filled["scalar"], take())
                    fn((tms, us)[h % 2][:, 0:2, :], psb()[0:NS, 0:256].rearrange("s (q f) -> s q f", q=2), ACT.Copy).then_inc(drained["scalar"], 1)
                    act.wait_ge(drained["scalar"], n_taken["n"])

                token_major(0)
                for h in range(8):
                    g = h % 2
                    for b in range(2):
                        act.wait_ge(filled["scalar"], take())
                        fn(S[2][:, h, b * P:(b + 1) * P], psb()[:, 0:P], ACT.Copy).then_inc(drained["scalar"], 1)
                        act.wait_ge(drained["scalar"], n_taken["n"])
                        if b == 0 and h < 7:
                            token_major(h + 1)
                        if b == 0 and h:
                            sample_out(OUT["sample_hgrn_S"], "hgrn", h - 1)
                    act.wait_ge(filled["scalar"], take())
                    fn(S[2][:, h, NPR:T], psb()[:, 0:NS], ACT.Copy).then_inc(drained["scalar"], 1)
                    act.wait_ge(drained["scalar"], n_taken["n"])
                    act.wait_ge(drained["vector"], mark["hstate", h] + 1)
                    act.dma_start(OUT["prompt_hgrn_S"][0, 0, h], sp[:, g, :]).then_inc(sem("prompt_state_out"), 16)
                    state["pout"] += 16
                sample_out(OUT["sample_hgrn_S"], "hgrn", 7)
                squares(S[2])
                first_hi(plan.index(("hwo", 0)))
                head_rstd(H, 1.0 / P, 0)
                split_out_projection(plan.index(("hwo", 0)))
                rms()

            stage = flat("A2")

            def rows_in(n, r0, src):
                act.dma_start(stage[r0:r0 + src.shape[0], n * P:(n + 1) * P], src).then_inc(sem("params_landed"), 16)

            def vec(name):
                return A[name].rearrange("j (c f) -> (j c) f", f=P)

            for q, name in enumerate(("norm_mix_pre", "norm_mix_post", "norm_ffn_pre", "norm_ffn_post")):
                rows_in(0, 32 * q, vec(name))
            rows_in(1, 0, A["rwkv_mix"].rearrange("j s (c f) -> (j s c) f", f=P))
            for q, name in enumerate(("rwkv_w0", "rwkv_a0", "rwkv_k_k", "rwkv_k_a")):
                rows_in(2, 16 * q, vec(name))
            rows_in(2, 64, A["rwkv_r_k"].rearrange("j (c h) f -> (j c) (h f)", h=2))
            rows_in(2, 80, vec("rwkv_lnx_w"))
            rows_in(2, 96, vec("rwkv_lnx_b"))
            rows_in(2, 112, vec("rwkv_v0"))
            rows_in(3, 0, vec("hgrn_lb"))
            rows_in(3, 32, A["hgrn_norm_w"])
            rows_in(3, 33, A["gdn_norm_w"])
            rows_in(4, 0, A["gdn_conv_w"].rearrange("j w (c f) -> (j w c) f", f=P))
            taps = A["ffn_conv_w"].rearrange("i w (c f) -> (i w c) f", f=P)
            for q in range(6):
                rows_in(5 + q, 0, taps[q * 88:(q + 1) * 88])
            rows_in(11, 0, A["state_rwkv_shift"].rearrange("j b (c f) -> (j b c) f", f=P))
            for q, name in enumerate(("gdn_a_log", "gdn_dt_bias")):
                act.dma_start(gpar[:, q:q + 1], A[name].rearrange("j (h o) -> (j h) o", o=1)).then_inc(
                    sem("gate_params_landed"), 16)
            act.wait_ge(sem("constants_ready"), after(act, "constants_ready"))
            for n, rows in enumerate(PARAM_ROWS):
                act.wait_ge(filled["scalar"], take())
                fn(pv[:, n, 0:rows], psb()[:, 0:rows], ACT.Copy).then_inc(drained["scalar"], 1)
                act.wait_ge(drained["scalar"], n_taken["n"])
            act.wait_ge(sem("gate_params_landed"), after_dma(act, "gate_params_landed", 2))
            fn(gpar[:, 2:3], gpar[:, 0:1], ACT.Exp).then_inc(signal("scalar_chain"), 1)
            act.wait_ge(sem("scalar_chain"), told["scalar_chain"])
            fn(gpar[:, 2:3], gpar[:, 2:3], ACT.Copy, scale=-1.0).then_inc(signal("scalar_chain"), 1)
            act.wait_ge(sem("scalar_chain"), told["scalar_chain"])
            act.wait_ge(sem("lb_shifted"), after(act, "lb_shifted"))
            fn(lb[:, 0:4, :], lb[:, 0:4, :], ACT.Exp).then_inc(signal("lb_exp"), 1)
            act.wait_ge(sem("lb_exp"), told["lb_exp"])
            for blk, n in enumerate((P, P, NS)):
                for q in range(2):
                    act.wait_ge(filled["scalar"], take())
                    fn(X[:, 4 * q:4 * q + 4, blk * P:blk * P + n],
                             psb().rearrange("p (i t) -> p i t", i=4)[:, :, 0:n], ACT.Copy).then_inc(drained["scalar"], 1)
                    act.wait_ge(drained["scalar"], n_taken["n"])
            squares(X)
            first = [True]
            real_pre = pre_norm

            def pre_norm(first_slab):
                if first[0]:
                    first[0] = False
                    split_hi(0)
                    split_hi(1)
                    rms()
                else:
                    real_pre(first_slab)

            rwkv(0)
            ffn(0)
            gdn()
            ffn(1)
            hgrn()
            ffn(2)
            rwkv(1)
            ffn(3)
            y = tm[:, :, :]
            hear_conv_out()
            for blk, n in enumerate((P, P, NS)):
                g = blk % 2
                if blk == 2:
                    act.wait_ge(sem("y_out"), 32)
                for q in range(2):
                    act.wait_ge(filled["scalar"], take())
                    fn(tm[0:n, g, q * 512:(q + 1) * 512], psb()[0:n, :], ACT.Copy).then_inc(drained["scalar"], 1)
                    act.wait_ge(drained["scalar"], n_taken["n"])
                dst = OUT["y_prompt"][0, blk * P:blk * P + n] if blk < 2 else OUT["y_sample"].rearrange("b t f -> (b t) f")
                act.dma_start(dst, tm[0:n, g, :]).then_inc(sem("y_out"), 16)
            act.wait_ge(sem("y_out"), 48)
            hear_state_out()
            hear_prompt_out()

        @block.vector
        def _(dve):
            V = nc.vector
            n_taken = {"n": 0}
            state = {"out": 0}

            def take():
                n_taken["n"] += 1
                return n_taken["n"]

            def psb():
                return bk[vec_bank[n_taken["n"] - 1]]

            def stt(out, a, s, b, o0=ALU.mult, o1=ALU.mult):
                return V.scalar_tensor_tensor(out=out, in0=a, scalar=s, in1=b, op0=o0, op1=o1)

            def tt(out, a, b, op=ALU.mult):
                return V.tensor_tensor(out, a, b, op)

            def ts(out, a, s1, s2=None, o0=ALU.mult, o1=None):
                if s2 is None:
                    return V.tensor_scalar(out, a, s1, None, o0)
                return V.tensor_scalar(out, a, s1, s2, o0, o1)

            def bc(ap, shape):
                return ap.to_broadcast(list(shape))

            def pre_norm(kind, i, name):
                dve.wait_ge(sem("rstd_ready"), after(dve, "rstd_ready"))
                for c in range(KC):
                    ins = stt(H[:, c, :], X[:, c, :], pcol(kind, i, c), rstd[:, :])
                    if name:
                        ins.then_inc(signal(name), 1)
                if not name:
                    name = "h_whole"
                    ins.then_inc(signal(name), 1)
                dve.wait_ge(sem(name), told[name])

            def split_tiles(make, full, hi, lo, name):
                for step in range(KC + 2):
                    if step < KC:
                        make(step).then_inc(signal("tile_made"), 1)
                    if 1 <= step <= KC:
                        dve.wait_ge(sem("tile_made"), after(dve, "tile_made"))
                        V.tensor_copy(act3r(hi)[:, step - 1, :], full[:, step - 1, :]).then_inc(signal("tile_hi"), 1)
                    if step >= 2:
                        dve.wait_ge(sem("tile_hi"), after(dve, "tile_hi"))
                        tt(act3r(lo)[:, step - 2, :], full[:, step - 2, :], act3r(hi)[:, step - 2, :],
                           ALU.subtract).then_inc(signal(name), 1)

            def split_lo(n):
                dve.wait_ge(sem("hi_ready"), after(dve, "hi_ready"))
                raw = ring[:, n % RING, 0:slab_size(n)]
                tt(w_lo[:, n % RING, 0:slab_size(n)], raw, w_hi[:, hi_slot(n), 0:slab_size(n)],
                   ALU.subtract).then_inc(signal("lo_ready"), 1)

            def post_norm(kind, i, out=S[3], scratch=SQ):
                dve.wait_ge(sem("rstd_ready"), after(dve, "rstd_ready"))
                for c in range(KC):
                    stt(scratch[:, c, :], out[:, c, :], pcol(kind, i, c), rstd[:, :]).then_inc(signal("vector_chain"), 1)
                    dve.wait_ge(sem("vector_chain"), told["vector_chain"])
                    tt(X[:, c, :], X[:, c, :], scratch[:, c, :], ALU.add).then_inc(signal("x_ready"), 1)
                dve.wait_ge(sem("x_ready"), told["x_ready"])

            def conv(n_in, n_out, width, coef, name):
                lead = width - 1
                n = span(lead) - lead
                e, o = buf(n_in, lead), buf(n_out, lead)
                ts(o[:, 0:n], e[:, 0:n], coef(0)).then_inc(signal("vector_chain"), 1)
                dve.wait_ge(sem("vector_chain"), told["vector_chain"])
                for j in range(1, width):
                    ins = stt(o[:, 0:n], e[:, j:j + n], coef(j), o[:, 0:n], ALU.mult, ALU.add)
                    if j < width - 1:
                        ins.then_inc(signal("vector_chain"), 1)
                        dve.wait_ge(sem("vector_chain"), told["vector_chain"])
                ins.then_inc(signal(name), 1)
                dve.wait_ge(sem(name), told[name])

            def ffn(i):
                n0 = plan.index(("up", i, 0, 0))
                split_lo(n0)
                split_lo(n0 + 1)
                pre_norm("ffn_pre", i, "h_to_split")
                for c in range(KC):
                    dve.wait_ge(sem("x_hi"), after(dve, "x_hi"))
                    tt(act3r("H")[:, c, :], H[:, c, :], act3r("A4")[:, c, :], ALU.subtract).then_inc(signal("x_split"), 1)
                lead = FW - 1
                y = flat("A0", 3)[:, 0:FC * T].rearrange("p (c t) -> p c t", c=FC)

                def product(p):
                    for q in range(2):
                        dve.wait_ge(sem("silu_ready"), after(dve, "silu_ready"))
                        a, g = buf(4 + (p % 2) * 4 + q, lead), buf(4 + (p % 2) * 4 + 2 + q, lead)
                        d = y[:, 2 * p + q, :]
                        tt(d[:, 0:NPR], a[:, 0:NPR], g[:, 0:NPR])

                        def seqs(ap):
                            return ap[:, lead + NPR:span(lead)].rearrange("p (b t) -> p b t", b=NB)[:, :, 0:NT]

                        tt(d[:, NPR:T].rearrange("p (b t) -> p b t", b=NB), seqs(a), seqs(g)).then_inc(signal("y_made"), 1)
                        dve.wait_ge(sem("y_made"), told["y_made"])

                for p in range(FPAIR):
                    for half in range(2):
                        if half and p:
                            product(p - 1)
                        for q in range(2):
                            dve.wait_ge(drained["scalar"], mark[("up", i, p, half), q] + 1)
                            dve.wait_ge(sem("hist_in"), after(dve, "hist_in"))
                            conv(half * 2 + q, 4 + (p % 2) * 4 + half * 2 + q, FW,
                                 lambda t: fconv(i, t, half * FC + 2 * p + q), ("value_conv", "gate_conv")[half])
                        split_lo(n0 + 2 * p + half + 2)
                product(FPAIR - 1)
                for s in range(2, 12):
                    split_lo(n0 + 2 * FPAIR + s)
                post_norm("ffn_post", i, S[4], H)

            def blocks(ap):
                return ap[:, :, 0:NPR].rearrange("p c (b t) -> p c b t", b=2)

            def seqs(ap):
                return ap[:, :, NPR:T].rearrange("p c (b t) -> p c b t", b=NB)

            def invert(between):
                for l in range(LEVELS):
                    for g in range(2):
                        dve.wait_ge(filled["vector"], take())
                        y = psb().rearrange("p (m t) -> p m t", m=4)
                        mask = low[:, l:l + 1, :].to_broadcast([P, 4, P])
                        if l == 0:
                            tt(T2[:, g, :, 0, :], y, mask).then_inc(signal("vector_chain"), 1)
                            dve.wait_ge(sem("vector_chain"), told["vector_chain"])
                            tt(T2[:, g, :, 0, :], ident[:, None, :].to_broadcast([P, 4, P]), T2[:, g, :, 0, :],
                               ALU.subtract).then_inc(drained["vector"], 1)
                        else:
                            tt(ysb[:, g, :].rearrange("p (m t) -> p m t", m=4), y, mask).then_inc(drained["vector"], 1)
                        dve.wait_ge(drained["vector"], n_taken["n"])
                        next(between, None)
                    if l == 0:
                        continue
                    for g in range(2):
                        dve.wait_ge(filled["vector"], take())
                        first = 0 if l < LEVELS - 1 else 1
                        t = T2[:, g, :, first:2, :]
                        new = wide[1 + g][:, :].rearrange("p (m q t) -> p m q t", m=4, q=2)[:, :, first:2, :]
                        tt(t, t, new, ALU.subtract).then_inc(drained["vector"], 1)
                        dve.wait_ge(drained["vector"], n_taken["n"])
                        next(between, None)
                for _ in between:
                    pass

            def start_inverse(g):
                tt(T2[:, g, :, 1, :], MX[:, g, :, 0, :], upp[:, 0:1, :].to_broadcast([P, 4, P])).then_inc(signal("vector_chain"), 1)
                dve.wait_ge(sem("vector_chain"), told["vector_chain"])
                tt(T2[:, g, :, 1, :], ident[:, None, :].to_broadcast([P, 4, P]), T2[:, g, :, 1, :],
                   ALU.subtract).then_inc(signal("vector_chain"), 1)
                dve.wait_ge(sem("vector_chain"), told["vector_chain"])

            def rwkv(j):
                slabs = [plan.index(("rkv", j, q, m)) for q in (2, 1, 0) for m in range(4)]
                split_lo(slabs[0])
                split_lo(slabs[1])
                pre_norm("mix_pre", 3 * j, None)
                M = [S[1], S[2]]
                Dx = S[0]
                tt(Dx[:, :, 1:NPR], H[:, :, 0:NPR - 1], H[:, :, 1:NPR], ALU.subtract)
                ts(Dx[:, :, 0:1], H[:, :, 0:1], -1.0)
                tt(seqs(Dx)[:, :, :, 1:NT], seqs(H)[:, :, :, 0:NT - 1], seqs(H)[:, :, :, 1:NT], ALU.subtract)
                tt(seqs(Dx)[:, :, :, 0], shiftT[:, j].rearrange("p b c -> p c b"), seqs(H)[:, :, :, 0], ALU.subtract).then_inc(signal("vector_chain"), 1)
                dve.wait_ge(sem("vector_chain"), told["vector_chain"])
                for i, s in enumerate(MIX_ORDER):
                    if i >= 2:
                        dve.wait_ge(filled["scalar"], mark["mix_used", j, i - 2] + 1)
                    def mixture(c):
                        return stt(M[i % 2][:, c, :], Dx[:, c, :], pcol("mix", j * 6 + s, c), H[:, c, :], ALU.mult, ALU.add)

                    if i < 3:
                        split_tiles(mixture, M[i % 2], ("A6", "A5", "A6")[i], ("A4", "A2", "A1")[i], "mix_split")
                    else:
                        for c in range(KC):
                            mixture(c).then_inc(signal("mix_ready"), 1)
                    for n in ((), (2, 3, 4, 5), (6, 7, 8, 9), (10, 11), (), ())[i]:
                        split_lo(slabs[n])
                    if j and i == 2:
                        dve.wait_ge(drained["scalar"], mark[("v2", j, KC - 1), 0] + 1)
                        dve.wait_ge(sem("v_first_back"), 16)
                        tt(S[7], S[8], S[3], ALU.subtract).then_inc(signal("vector_chain"), 1)
                        dve.wait_ge(sem("vector_chain"), told["vector_chain"])
                        tt(S[7], S[7], SQ).then_inc(signal("vector_chain"), 1)
                        dve.wait_ge(sem("vector_chain"), told["vector_chain"])
                        tt(S[3], S[3], S[7], ALU.add).then_inc(signal("v_mixed"), 1)
                        dve.wait_ge(sem("v_mixed"), told["v_mixed"])
                dve.wait_ge(sem("mix_ready"), told["mix_ready"])
                K, B, KK, Vv, R = S[4], S[1], S[0], S[3], S[5]
                for c in range(KC):
                    dve.wait_ge(drained["scalar"], mark[("k", j), KC - 1] + 1)
                    ins = ts(KK[:, c, :], K[:, c, :], pcol("k_k", j, c))
                    ins.then_inc(signal("kk_raw"), 1)
                dve.wait_ge(drained["scalar"], mark[("w2", j, KC - 1), 0] + 1)
                ts(S[6], S[6], -RW_DECAY).then_inc(signal("vector_chain"), 1)
                dve.wait_ge(sem("vector_chain"), told["vector_chain"])
                if not j:
                    dve.wait_ge(sem("masks_ready"), after(dve, "masks_ready"))
                dve.wait_ge(sem("shift_saved"), after(dve, "shift_saved"))
                for c in range(KC):
                    ins = V.tensor_tensor_scan(H[:, c, :], seg[:, :], S[6][:, c, :], 0.0, ALU.mult, ALU.add)
                ins.then_inc(signal("vector_chain"), 1)
                dve.wait_ge(sem("vector_chain"), told["vector_chain"])
                V.tensor_copy(cen[:, 0], H[:, :, 63:NPR:128]).then_inc(signal("vector_chain"), 1)
                dve.wait_ge(sem("vector_chain"), told["vector_chain"])
                tt(blocks(H), blocks(H), cen[:, 0][:, :, :, None].to_broadcast([P, KC, 2, P]), ALU.subtract).then_inc(signal("vector_chain"), 1)
                dve.wait_ge(sem("vector_chain"), told["vector_chain"])
                dve.wait_ge(drained["scalar"], mark[("a2", j, KC - 1), 0] + 1)
                dve.wait_ge(filled["scalar"], mark["mix_used", j, 5] + 1)
                for c in range(KC):
                    ins = ts(S[2][:, c, :], S[7][:, c, :], pcol("k_a", j, c), omka[:, j, c:c + 1], ALU.mult, ALU.add)
                ins.then_inc(signal("vector_chain"), 1)
                dve.wait_ge(sem("vector_chain"), told["vector_chain"])
                tt(K, K, S[2]).then_inc(signal("vector_chain"), 1)
                dve.wait_ge(sem("vector_chain"), told["vector_chain"])
                dve.wait_ge(sem("rk_ready"), after(dve, "rk_ready"))
                tt(KK, KK, S[1]).then_inc(signal("vector_chain"), 1)
                dve.wait_ge(sem("vector_chain"), told["vector_chain"])
                tt(B, KK, S[7]).then_inc(signal("vector_chain"), 1)
                dve.wait_ge(sem("vector_chain"), told["vector_chain"])
                tt(S[2], H, S[6], ALU.subtract).then_inc(signal("ge_ready"), 1)
                for c in range(KC):
                    stt(SQ[:, c, :], R[:, c, :], pcol("r_k", j, c), K[:, c, :]).then_inc(signal("bonus_product"), 1)
                dve.wait_ge(sem("e_excl"), after(dve, "e_excl"))
                tt(ARp[:, :, :, 0, :], blocks(KK), blocks(S[2]))
                tt(ARs[:, :, 0, :], KK[:, :, NPR:T], S[2][:, :, NPR:T]).then_inc(signal("a_done"), 1)
                dve.wait_ge(sem("a_done"), told["a_done"])
                for c in range(KC):
                    dve.wait_ge(filled["vector"], take())
                    tt(S[2][:, c, :], psb()[:, 0:T], Vv[:, c, :]).then_inc(drained["vector"], 1)
                    dve.wait_ge(drained["vector"], n_taken["n"])
                dve.wait_ge(sem("e_incl"), after(dve, "e_incl"))
                tt(ARp[:, :, :, 1, :], blocks(R), blocks(S[0]))
                tt(ARs[:, :, 1, :], R[:, :, NPR:T], S[0][:, :, NPR:T])
                V.tensor_copy(cen[:, 2], S[0][:, :, 127:NPR:128])
                V.tensor_copy(els[:, :, :], seqs(S[0])[:, :, :, NT - 1]).then_inc(signal("vector_chain"), 1)
                dve.wait_ge(sem("vector_chain"), told["vector_chain"])
                dve.wait_ge(sem("e_neg"), after(dve, "e_neg"))
                tt(K, K, H)
                if j:
                    dve.wait_ge(sem("prompt_state_out"), 16 * 32)
                V.memset(sp[:, :, :], 0.0)
                V.memset(ams[:, :, :, :], 0.0)
                V.memset(rms_[:, :, :], 0.0)
                tt(B, B, H).then_inc(signal("operands_ready"), 1)
                dve.wait_ge(sem("operands_ready"), told["operands_ready"])
                for r in range(4):
                    for g in range(2):
                        for m in range(4):
                            dve.wait_ge(filled["vector"], take())
                            tt(MX[:, g, m].rearrange("p q t -> p (q t)"), psb(),
                                     mask4[:, :, :].rearrange("p q t -> p (q t)")).then_inc(drained["vector"], 1)
                            dve.wait_ge(drained["vector"], n_taken["n"])
                        start_inverse(g)
                    invert(samples(rwkv_sample, [(j, 2 * r), (j, 2 * r + 1)]))
                    for b in range(2):
                        for g in range(2):
                            dve.wait_ge(filled["vector"], take())
                            V.tensor_copy(rs[:, g, 0:P], psb()[:, 0:P]).then_inc(drained["vector"], 1)
                            dve.wait_ge(drained["vector"], n_taken["n"])
                        for g in range(2):
                            c = 2 * r + g
                            dve.wait_ge(filled["vector"], take())
                            if b:
                                ts(sp[:, g, :], sp[:, g, :], cen[:, 2, c, 1:2]).then_inc(signal("vector_chain"), 1)
                                dve.wait_ge(sem("vector_chain"), told["vector_chain"])
                            for hh in range(2):
                                rows = slice(64 * hh, 64 * hh + 64)
                                src = psb()[rows, hh * 64:hh * 64 + 64]
                                if b:
                                    ins = stt(sp[rows, g, rows], src, cen[rows, 2, c, 1:2], sp[rows, g, rows],
                                              ALU.mult, ALU.add)
                                else:
                                    ins = ts(sp[rows, g, rows], src, cen[rows, 2, c, 0:1], cen[rows, 1, c, 1:2],
                                             ALU.mult, ALU.mult)
                            ins.then_inc(drained["vector"], 1)
                            dve.wait_ge(drained["vector"], n_taken["n"])
                for c in range(KC):
                    dve.wait_ge(filled["vector"], take())
                    stt(S[5][:, c, :], psb()[:, 0:T], -1.0 / 64, S[5][:, c, :], ALU.mult, ALU.add).then_inc(drained["vector"], 1)
                    dve.wait_ge(drained["vector"], n_taken["n"])
                split_lo(plan.index(("rwo", j, 0)))
                split_lo(plan.index(("rwo", j, 1)))
                dve.wait_ge(sem("rk_ready"), after(dve, "rk_ready"))
                tt(S[5], S[5], H).then_inc(signal("vector_chain"), 1)
                dve.wait_ge(sem("vector_chain"), told["vector_chain"])
                for c in range(KC):
                    ins = ts(S[5][:, c, :], S[5][:, c, :], pcol("lnx_w", j, c), pcol("lnx_b", j, c), ALU.mult, ALU.add)
                ins.then_inc(signal("vector_chain"), 1)
                dve.wait_ge(sem("vector_chain"), told["vector_chain"])
                tt(S[5], S[5], S[2], ALU.add).then_inc(signal("vector_chain"), 1)
                dve.wait_ge(sem("vector_chain"), told["vector_chain"])
                gated_out(S[5], plan.index(("rwo", j, 0)))
                post_norm("mix_post", 3 * j)

            def spread_rows(dst, src, n):
                return tt(dst.rearrange("s (b v) -> s b v", b=NB), src[:, None, :].to_broadcast([NS, NB, n]),
                          rmask[:, :, None].to_broadcast([NS, NB, n]))

            def rwkv_sample(j, c):
                for hh in range(2):
                    rows = slice(64 * hh, 64 * hh + 64)
                    V.tensor_copy(rms_[rows, hh, :], ARs[rows, c, 1, :])
                    ins = tt(ams[rows, hh], ARs[rows, c, 0, None, :].to_broadcast([64, NB, NS]), bmask[rows])
                ins.then_inc(signal("spread_ready"), 1)
                dve.wait_ge(sem("spread_ready"), told["spread_ready"])
                yield
                for hh in range(2):
                    dve.wait_ge(filled["vector"], take())
                    tt(ms[:, hh].rearrange("s q t -> s (q t)"), psb()[0:NS, 0:128],
                             samp4[:, :, :].rearrange("s q t -> s (q t)")).then_inc(drained["vector"], 1)
                    dve.wait_ge(drained["vector"], n_taken["n"])
                yield
                dve.wait_ge(filled["vector"], take())
                V.tensor_copy(us[:, 0, :], psb()[0:NS, 0:P]).then_inc(drained["vector"], 1)
                dve.wait_ge(drained["vector"], n_taken["n"])
                yield
                yield from nilpotent()
                dve.wait_ge(drained["scalar"], mark["tms", "rwkv", j, c] + 1)
                for hh in range(2):
                    rows = slice(64 * hh, 64 * hh + 64)
                    spread_rows(vms[:, 0, :], tms[:, 0, hh * 64:hh * 64 + 64], 64)
                    spread_rows(vms[:, 1, :], us[:, 3, hh * 64:hh * 64 + 64], 64).then_inc(signal("values_spread"), 1)
                    dve.wait_ge(sem("values_spread"), told["values_spread"])
                    if hh == 0:
                        yield
                    yield
                    dve.wait_ge(filled["vector"], take())
                    tt(sst[rows, 1, :], psb()[rows, :], sst[rows, 0, :], ALU.add).then_inc(drained["vector"], 1)
                    dve.wait_ge(drained["vector"], n_taken["n"])
                    s3 = sst[rows, 1, :].rearrange("p (b v) -> p b v", b=NB)
                    ins = tt(s3, s3, els[rows, c, :, None].to_broadcast([64, NB, 64]))
                    if hh:
                        ins.then_inc(signal("sample_state_new"), 1)
                        dve.wait_ge(sem("sample_state_new"), told["sample_state_new"])
                    else:
                        ins.then_inc(signal("vector_chain"), 1)
                        dve.wait_ge(sem("vector_chain"), told["vector_chain"])
                yield

            def nilpotent():
                dve.wait_ge(filled["vector"], take())
                V.tensor_copy(us[:, 1, :], psb()[0:NS, 0:P]).then_inc(drained["vector"], 1)
                dve.wait_ge(drained["vector"], n_taken["n"])
                yield
                dve.wait_ge(filled["vector"], take())
                tt(us[:, 2, :], psb()[0:NS, 0:P], us[:, 0, :], ALU.add).then_inc(drained["vector"], 1)
                dve.wait_ge(drained["vector"], n_taken["n"])
                yield
                dve.wait_ge(filled["vector"], take())
                tt(us[:, 3, :], psb()[0:NS, 0:P], us[:, 2, :], ALU.subtract).then_inc(drained["vector"], 1)
                dve.wait_ge(drained["vector"], n_taken["n"])

            def gdn():
                n0 = plan.index(("gin", 0))
                split_lo(n0)
                split_lo(n0 + 1)
                dve.wait_ge(sem("rstd_ready"), after(dve, "rstd_ready"))
                split_tiles(lambda c: stt(H[:, c, :], X[:, c, :], pcol("mix_pre", 1, c), rstd[:, :]), H, "A3", "A0", "h_split")
                for n in range(GT):
                    dve.wait_ge(drained["scalar"], mark["gin", n] + 1)
                    dve.wait_ge(sem("hist_in"), after(dve, "hist_in"))
                    if n >= 4:
                        dve.wait_ge(sem("qkv_ready"), after(dve, "qkv_ready"))
                    conv(n % 4, 4 + n % 4, GW, lambda t: gconv(t, n), "gconv")
                    if n % 2:
                        split_lo(n0 + n // 2 + 2)
                split_lo(n0 + 14)
                split_lo(n0 + 15)
                dve.wait_ge(sem("qkv_ready"), after(dve, "qkv_ready", 4))
                dve.wait_ge(sem("softplus_ready"), after(dve, "softplus_ready"))
                stt(g8[:, 1, :], g8[:, 1, :], 0.0, g8[:, 2, :], ALU.max, ALU.add).then_inc(signal("vector_chain"), 1)
                dve.wait_ge(sem("vector_chain"), told["vector_chain"])
                ts(g8[:, 1, :], g8[:, 1, :], gpar[:, 2:3]).then_inc(signal("vector_chain"), 1)
                dve.wait_ge(sem("vector_chain"), told["vector_chain"])
                V.tensor_tensor_scan(g8[:, 2, :], seg[0:8, :], g8[:, 1, :], 0.0, ALU.mult, ALU.add).then_inc(signal("decay_ready"), 1)
                dve.wait_ge(sem("decay_ready"), told["decay_ready"])
                Q, K, Vv, QG, EG, GR = S[1], S[4], S[2], S[7], S[3], S[6]
                dve.wait_ge(sem("rk_ready"), after(dve, "rk_ready"))
                stt(Q, Q, float(P) ** -0.5, S[3]).then_inc(signal("vector_chain"), 1)
                dve.wait_ge(sem("vector_chain"), told["vector_chain"])
                dve.wait_ge(sem("rk_ready"), after(dve, "rk_ready"))
                tt(K, K, SQ).then_inc(signal("qk_done"), 1)
                dve.wait_ge(sem("qk_done"), told["qk_done"])
                dve.wait_ge(sem("eg_ready"), after(dve, "eg_ready"))
                tt(QG, Q, EG).then_inc(signal("operands_ready"), 1)
                dve.wait_ge(sem("operands_ready"), told["operands_ready"])
                for r in range(2):
                    for g in range(2):
                        for m in range(4):
                            hh, b = divmod(m, 2)
                            h = 4 * r + 2 * g + hh
                            ins = ts(ysb[:, g, m * P:(m + 1) * P], GR[:, h, b * P:(b + 1) * P], tb[:, b, 8 + h:9 + h], 0.0,
                                     ALU.subtract, ALU.min)
                        ins.then_inc(signal("exponents_ready"), 1)
                        dve.wait_ge(sem("exponents_ready"), told["exponents_ready"])
                    for g in range(2):
                        dve.wait_ge(sem("decays_exp"), after(dve, "decays_exp"))
                        e = ysb[:, g, :].rearrange("p (m t) -> p m t", m=4)
                        V.tensor_copy(ed[:, g, :], e[:, :, P - 1])
                        for q in range(2):
                            ins = tt(MX[:, g, :, 2 + q, :], e, mask4[:, q:q + 1, :].to_broadcast([P, 4, P]))
                        ins.then_inc(signal("vector_chain"), 1)
                        dve.wait_ge(sem("vector_chain"), told["vector_chain"])
                        for m in range(4):
                            hh, b = divmod(m, 2)
                            h = 4 * r + 2 * g + hh
                            dve.wait_ge(filled["vector"], take())
                            stt(MX[:, g, m, 0, :], psb()[:, 0:P], tb[:, b, h:h + 1], MX[:, g, m, 2, :])
                            tt(MX[:, g, m, 1, :], psb()[:, P:2 * P], MX[:, g, m, 3, :]).then_inc(drained["vector"], 1)
                            dve.wait_ge(drained["vector"], n_taken["n"])
                        start_inverse(g)
                    invert(samples(gdn_sample, [(4 * r + i,) for i in range(4)]))
                    for b in range(2):
                        if b:
                            for g in range(2):
                                tg = tm[:, g, :].rearrange("p (h b q f) -> p h b q f", h=2, b=2, q=2)
                                dve.wait_ge(drained["scalar"], mark["gtm", r, g] + 1)
                                dve.wait_ge(filled["vector"], take())
                                for hh in range(2):
                                    h = 4 * r + 2 * g + hh
                                    ins = stt(rs[:, g, hh * P:(hh + 1) * P], psb()[:, hh * P:(hh + 1) * P],
                                              neg[:, 1, h:h + 1], tg[:, hh, 1, 0, :], ALU.mult, ALU.add)
                                ins.then_inc(drained["vector"], 1)
                                dve.wait_ge(drained["vector"], n_taken["n"])
                        for g in range(2):
                            dve.wait_ge(drained["scalar"], mark["z", r, b, g] + 1)
                            for hh in range(2):
                                ins = ts(xd[:, g, hh * P:(hh + 1) * P], nu[:, g, hh * P:(hh + 1) * P],
                                         ed[:, g, 2 * hh + b:2 * hh + b + 1])
                            ins.then_inc(signal("xd_ready"), 1)
                            dve.wait_ge(sem("xd_ready"), told["xd_ready"])
                        for g in range(2):
                            dve.wait_ge(filled["vector"], take())
                            if b == 0 and r:
                                dve.wait_ge(sem("prompt_state_out"), 16 * 16 + 64)
                            if b == 0 and not r:
                                dve.wait_ge(sem("prompt_state_out"), 16 * 16)
                            for hh in range(2):
                                h = 4 * r + 2 * g + hh
                                src, st = psb()[:, hh * P:(hh + 1) * P], (sp, spo)[hh][:, g, :]
                                if b:
                                    ins = stt(st, st, EG[:, h, NPR - 1:NPR], src, ALU.mult, ALU.add)
                                else:
                                    ins = V.tensor_copy(st, src)
                            ins.then_inc(drained["vector"], 1)
                            dve.wait_ge(drained["vector"], n_taken["n"])
                finish_heads(S[5], pv[:, 3, 33:34], 1, plan.index(("gwo", 0)))

            def gated_out(o, n0):
                def product(c):
                    return tt(S[5][:, c, :], o[:, c, :], S[8][:, c, :])

                split_tiles(product, S[5], "A1", "A5", "mixer_out")
                split_lo(n0 + 2)
                split_lo(n0 + 3)

            def finish_heads(o, w, i, n0):
                split_lo(n0)
                split_lo(n0 + 1)
                dve.wait_ge(sem("rk_ready"), after(dve, "rk_ready"))
                for c in range(KC):
                    ins = stt(o[:, c, :], o[:, c, :], w, H[:, c, :])
                ins.then_inc(signal("vector_chain"), 1)
                dve.wait_ge(sem("vector_chain"), told["vector_chain"])
                gated_out(o, n0)
                post_norm("mix_post", i)

            def state_stored():
                dve.wait_ge(sem("sample_state_out"), state["out"])

            def sample_update(h, decay):
                s3 = head_state(h).rearrange("p (b v) -> p b v", b=NB)
                o3 = sout[:, :].rearrange("p (b v) -> p b v", b=NB)
                dve.wait_ge(filled["vector"], take())
                state_stored()
                tt(o3, s3, decay.to_broadcast([P, NB, P])).then_inc(signal("vector_chain"), 1)
                dve.wait_ge(sem("vector_chain"), told["vector_chain"])
                for q in range(2):
                    if q:
                        dve.wait_ge(filled["vector"], take())
                    o = sout[:, q * 512:(q + 1) * 512]
                    tt(o, o, psb(), ALU.add).then_inc(drained["vector"], 1)
                    dve.wait_ge(drained["vector"], n_taken["n"])
                state["out"] += 16

            def gdn_sample(h):
                Q, K, Vv, QG, EG, GR = S[1], S[4], S[2], S[7], S[3], S[6]
                ts(ms[:, 1, 0, :], GR[0:NS, h, NPR:T], tb[0:NS, 2, 8 + h:9 + h], 0.0, ALU.subtract, ALU.min).then_inc(signal("sample_exponents"), 1)
                dve.wait_ge(sem("sample_exponents"), told["sample_exponents"])
                tt(ams[:, 0], K[:, h, None, NPR:T].to_broadcast([P, NB, NS]), bmask[:, :, :]).then_inc(signal("spread_ready"), 1)
                dve.wait_ge(sem("spread_ready"), told["spread_ready"])
                yield
                dve.wait_ge(sem("sample_decays"), after(dve, "sample_decays"))
                tt(ms[:, 1, 2:4, :], ms[:, 1, 0:1, :].to_broadcast([NS, 2, NS]), samp4[:, 0:2, :])
                tt(ms[:, 1, 1, :], ms[:, 1, 0, :], lastm[:, :]).then_inc(signal("vector_chain"), 1)
                dve.wait_ge(sem("vector_chain"), told["vector_chain"])
                V.reduce_sum(ed[0:NS, 2, 0:1], ms[:, 1, 1, :], AX_X).then_inc(signal("vector_chain"), 1)
                dve.wait_ge(sem("vector_chain"), told["vector_chain"])
                dve.wait_ge(filled["vector"], take())
                stt(ms[:, 0, 0, :], psb()[0:NS, 0:NS], tb[0:NS, 2, h:h + 1], ms[:, 1, 2, :])
                tt(ms[:, 0, 1, :], psb()[0:NS, NS:2 * NS], ms[:, 1, 3, :]).then_inc(drained["vector"], 1)
                dve.wait_ge(drained["vector"], n_taken["n"])
                yield
                dve.wait_ge(filled["vector"], take())
                dve.wait_ge(drained["scalar"], mark["tms", "gdn", h] + 1)
                stt(us[:, 0, :], psb()[0:NS, 0:P], neg[0:NS, 2, h:h + 1], tms[:, 0, :], ALU.mult, ALU.add).then_inc(drained["vector"], 1)
                dve.wait_ge(drained["vector"], n_taken["n"])
                yield
                yield from nilpotent()
                ts(us[:, 3, :], us[:, 3, :], tb[0:NS, 2, h:h + 1], -1.0, ALU.mult, ALU.mult).then_inc(signal("x_scaled"), 1)
                dve.wait_ge(sem("x_scaled"), told["x_scaled"])
                ts(us[:, 1, :], us[:, 3, :], ed[0:NS, 2, 0:1]).then_inc(signal("vector_chain"), 1)
                dve.wait_ge(sem("vector_chain"), told["vector_chain"])
                spread_rows(vms[:, :, :].rearrange("s a b -> s (a b)"), us[:, 1, :], P).then_inc(signal("values_spread"), 1)
                dve.wait_ge(sem("values_spread"), told["values_spread"])
                yield
                sample_update(h, EG[:, h, NPR + NT - 1:T:NT][:, :, None])

            def hgrn():
                n0 = plan.index(("hin", 0))
                split_lo(n0)
                split_lo(n0 + 1)
                dve.wait_ge(sem("rstd_ready"), after(dve, "rstd_ready"))
                split_tiles(lambda c: stt(H[:, c, :], X[:, c, :], pcol("mix_pre", 2, c), rstd[:, :]), H, "A7", "H", "h_split")
                for slab in range(2, 12):
                    split_lo(n0 + slab)
                Q, F, K, G, Vv, QG, KD, E = S[0], S[1], S[2], S[3], S[4], S[5], S[6], S[7]
                dve.wait_ge(drained["scalar"], mark["hin", 2 * KC - 1] + 1)
                for c in range(KC):
                    ins = ts(F[:, c, :], F[:, c, :], lb[:, 5, c:c + 1], lb[:, 4, c:c + 1], ALU.mult, ALU.add)
                ins.then_inc(signal("vector_chain"), 1)
                dve.wait_ge(sem("vector_chain"), told["vector_chain"])
                ts(K, F, -1.0, 1.0, ALU.mult, ALU.add).then_inc(signal("f_ready"), 1)
                dve.wait_ge(sem("f_ready"), told["f_ready"])
                split_lo(n0 + 12)
                split_lo(n0 + 13)
                dve.wait_ge(sem("log_f_ready"), after(dve, "log_f_ready"))
                for c in range(KC):
                    ins = V.tensor_tensor_scan(G[:, c, :], seg[:, :], F[:, c, :], 0.0, ALU.mult, ALU.add)
                ins.then_inc(signal("cumulated"), 1)
                dve.wait_ge(sem("cumulated"), told["cumulated"])
                V.memset(flat("A1"), 0.0)
                tt(blocks(KD), blocks(G)[:, :, :, P - 1:P].to_broadcast([P, KC, 2, P]), blocks(G), ALU.subtract)
                tt(seqs(KD), seqs(G)[:, :, :, NT - 1:NT].to_broadcast([P, KC, NB, NT]), seqs(G), ALU.subtract).then_inc(signal("to_end_ready"), 1)
                dve.wait_ge(sem("to_end_ready"), told["to_end_ready"])
                split_lo(n0 + 14)
                split_lo(n0 + 15)
                dve.wait_ge(sem("exp_cumulated"), after(dve, "exp_cumulated"))
                V.tensor_copy(cen[:, 2], QG[:, :, 127:NPR:128])
                V.tensor_copy(els[:, :, :], seqs(QG)[:, :, :, NT - 1]).then_inc(signal("vector_chain"), 1)
                dve.wait_ge(sem("vector_chain"), told["vector_chain"])
                tt(QG, QG, Q).then_inc(signal("vector_chain"), 1)
                dve.wait_ge(sem("vector_chain"), told["vector_chain"])
                dve.wait_ge(sem("exp_to_end"), after(dve, "exp_to_end"))
                dve.wait_ge(drained["scalar"], mark["hin", 4 * KC - 1] + 1)
                tt(KD, KD, K).then_inc(signal("level_operands"), 1)
                dve.wait_ge(sem("level_operands"), told["level_operands"])
                AT = flat("A1")[:, 0:2048].rearrange("p (n i t) -> p n i t", n=4, i=4)
                ATS = flat("A1")[0:NS, 2048:2304].rearrange("p (h t) -> p h t", h=8)

                def distances(l):
                    n = 1 << l
                    if l <= 2:
                        g = G.rearrange("p c t -> p (c t)").rearrange("p (b t) -> p b t", t=n)
                        e = E.rearrange("p c t -> p (c t)").rearrange("p (b t) -> p b t", t=n)
                        ins = tt(e, g, g[:, :, n // 2 - 1:n // 2].to_broadcast([P, KC * T // n, n]), ALU.subtract)
                    else:
                        g = G[:, :, 0:NPR].rearrange("p c (b t) -> p c b t", t=n)
                        e = E[:, :, 0:NPR].rearrange("p c (b t) -> p c b t", t=n)
                        ins = tt(e, g, g[:, :, :, n // 2 - 1:n // 2].to_broadcast([P, KC, NPR // n, n]), ALU.subtract)
                    ins.then_inc(signal("distance_ready"), 1)
                    dve.wait_ge(sem("distance_ready"), told["distance_ready"])

                for l in range(LEVELS + 1):
                    if l < LEVELS:
                        distances(l + 1)
                    m = ident[:, :] if l == 0 else upp[:, l - 1, :]
                    for n in range(4):
                        dve.wait_ge(filled["vector"], take())
                        V.copy_predicated(AT[:, n], m.bitcast(U32)[:, None, :].to_broadcast([P, 4, P]),
                                                psb().rearrange("p (i t) -> p i t", i=4)).then_inc(drained["vector"], 1)
                        dve.wait_ge(drained["vector"], n_taken["n"])
                    if l <= 2:
                        dve.wait_ge(filled["vector"], take())
                        V.copy_predicated(ATS, m[0:NS, 0:NS].bitcast(U32)[:, None, :].to_broadcast([NS, 8, NS]),
                                                psb()[0:NS, 0:256].rearrange("p (i t) -> p i t", i=8)).then_inc(drained["vector"], 1)
                        dve.wait_ge(drained["vector"], n_taken["n"])
                    if l < LEVELS:
                        dve.wait_ge(sem("distance_exp"), after(dve, "distance_exp"))
                        w = T if l + 1 <= 2 else NPR
                        tt(H[:, :, 0:w], Q[:, :, 0:w], E[:, :, 0:w])
                        tt(SQ[:, :, 0:w], K[:, :, 0:w], E[:, :, 0:w]).then_inc(signal("level_operands"), 1)
                        dve.wait_ge(sem("level_operands"), told["level_operands"])
                for h in range(8):
                    g = h % 2
                    for b in range(2):
                        if b:
                            dve.wait_ge(drained["scalar"], mark["tms", "hgrn", h] + 1)
                            spread_rows(vms[:, :, :].rearrange("s a b -> s (a b)"), (tms, us)[g][:, 0, :],
                                        P).then_inc(signal("values_spread"), 1)
                            dve.wait_ge(sem("values_spread"), told["values_spread"])
                        dve.wait_ge(filled["vector"], take())
                        if b:
                            ins = stt(sp[:, g, :], sp[:, g, :], cen[:, 2, h, 1:2], psb()[:, 0:P], ALU.mult, ALU.add)
                        else:
                            dve.wait_ge(sem("prompt_state_out"), 16 * 16 + 16 * 8 + 16 * max(h - 1, 0))
                            ins = V.tensor_copy(sp[:, g, :], psb()[:, 0:P])
                        ins.then_inc(drained["vector"], 1)
                        dve.wait_ge(drained["vector"], n_taken["n"])
                    sample_update(h, els[:, h, :, None])
                finish_heads(S[2], pv[:, 3, 32:33], 2, plan.index(("hwo", 0)))

            dve.wait_ge(drained["scalar"], 3 + 1)
            logits = pv[:, 3, 0:32].rearrange("p (l c) -> p l c", l=4)
            tt(lb[:, 6, :], logits[:, 0, :], logits[:, 1, :], ALU.max).then_inc(signal("vector_chain"), 1)
            dve.wait_ge(sem("vector_chain"), told["vector_chain"])
            tt(lb[:, 7, :], logits[:, 2, :], logits[:, 3, :], ALU.max).then_inc(signal("vector_chain"), 1)
            dve.wait_ge(sem("vector_chain"), told["vector_chain"])
            tt(lb[:, 6, :], lb[:, 6, :], lb[:, 7, :], ALU.max).then_inc(signal("vector_chain"), 1)
            dve.wait_ge(sem("vector_chain"), told["vector_chain"])
            tt(lb[:, 0:4, :], logits, lb[:, 6:7, :].to_broadcast([P, 4, KC]), ALU.subtract).then_inc(signal("lb_shifted"), 1)
            dve.wait_ge(sem("lb_shifted"), told["lb_shifted"])
            dve.wait_ge(sem("lb_exp"), after(dve, "lb_exp"))
            tt(lb[:, 4, :], lb[:, 1, :], lb[:, 2, :], ALU.add).then_inc(signal("vector_chain"), 1)
            dve.wait_ge(sem("vector_chain"), told["vector_chain"])
            tt(lb[:, 6, :], lb[:, 0, :], lb[:, 3, :], ALU.add).then_inc(signal("vector_chain"), 1)
            dve.wait_ge(sem("vector_chain"), told["vector_chain"])
            tt(lb[:, 6, :], lb[:, 6, :], lb[:, 4, :], ALU.add).then_inc(signal("vector_chain"), 1)
            dve.wait_ge(sem("vector_chain"), told["vector_chain"])
            V.reciprocal(lb[:, 7, :], lb[:, 6, :]).then_inc(signal("vector_chain"), 1)
            dve.wait_ge(sem("vector_chain"), told["vector_chain"])
            tt(lb[:, 4, :], lb[:, 4, :], lb[:, 7, :]).then_inc(signal("vector_chain"), 1)
            dve.wait_ge(sem("vector_chain"), told["vector_chain"])
            ts(lb[:, 5, :], lb[:, 4, :], -1.0, 1.0, ALU.mult, ALU.add).then_inc(signal("vector_chain"), 1)
            dve.wait_ge(sem("vector_chain"), told["vector_chain"])
            for j in range(2):
                ins = ts(omka[:, j, :], pv[:, 2, (3 * 2 + j) * 8:(3 * 2 + j) * 8 + 8], -1.0, 1.0, ALU.mult, ALU.add)
            ins.then_inc(signal("vector_chain"), 1)
            dve.wait_ge(sem("vector_chain"), told["vector_chain"])
            state["out"] = 32 * 9
            rwkv(0)
            ffn(0)
            gdn()
            ffn(1)
            hgrn()
            ffn(2)
            rwkv(1)
            ffn(3)

        @block.gpsimd
        def _(pool):
            G = nc.gpsimd

            def select(dst, pattern, base, mult, op=ALU.is_ge, fill=0.0):
                G.affine_select(out=dst, in_=dst, compare_op=op, fill=fill, base=base, pattern=pattern,
                                     channel_multiplier=mult).then_inc(signal("gpsimd_chain"), 1)
                pool.wait_ge(sem("gpsimd_chain"), told["gpsimd_chain"])

            G.memset(eps[:, 0:1], EPS).then_inc(signal("gpsimd_chain"), 1)
            pool.wait_ge(sem("gpsimd_chain"), told["gpsimd_chain"])
            G.memset(eps[:, 1:2], LNX_EPS).then_inc(signal("constants_ready"), 1)
            pool.wait_ge(sem("constants_ready"), told["constants_ready"])
            G.memset(ident[:, :], 0.0).then_inc(signal("gpsimd_chain"), 1)
            pool.wait_ge(sem("gpsimd_chain"), told["gpsimd_chain"])
            select(ident[:, :], [[-1, P]], 0, 1, ALU.not_equal, 1.0)
            G.memset(ones[:, :], 1.0)
            G.memset(bones[:, :], 0.0).then_inc(signal("gpsimd_chain"), 1)
            pool.wait_ge(sem("gpsimd_chain"), told["gpsimd_chain"])
            G.memset(bones[0:64, 0:64], 1.0)
            G.memset(bones[64:128, 64:128], 1.0).then_inc(signal("basics_ready"), 1)
            pool.wait_ge(sem("basics_ready"), told["basics_ready"])
            G.memset(mask4[:, :, :], 1.0).then_inc(signal("gpsimd_chain"), 1)
            pool.wait_ge(sem("gpsimd_chain"), told["gpsimd_chain"])
            for q in range(4):
                select(mask4[:, q, :], [[1, P]], -1 if q % 2 == 0 else 0, -1)
            G.tensor_copy(same[:, 0, :], ident[:, :]).then_inc(signal("gpsimd_chain"), 1)
            pool.wait_ge(sem("gpsimd_chain"), told["gpsimd_chain"])
            for l in range(1, LEVELS + 1):
                n = 1 << l
                cur, old = same[:, l % 2, :], same[:, (l - 1) % 2, :]
                G.memset(cur, 1.0).then_inc(signal("gpsimd_chain"), 1)
                pool.wait_ge(sem("gpsimd_chain"), told["gpsimd_chain"])
                if l < LEVELS:
                    v = cur.rearrange("p (b r) -> p b r", r=n)
                    select(v, [[-n, P // n], [0, n]], 0, 1)
                    select(v, [[n, P // n], [0, n]], n - 1, -1)
                if l == 2:
                    for q in range(4):
                        G.tensor_tensor(samp4[:, q, :], mask4[0:NS, q, 0:NS], cur[0:NS, 0:NS], ALU.mult).then_inc(signal("gpsimd_chain"), 1)
                        pool.wait_ge(sem("gpsimd_chain"), told["gpsimd_chain"])
                    G.memset(lastm[:, :], 0.0).then_inc(signal("gpsimd_chain"), 1)
                    pool.wait_ge(sem("gpsimd_chain"), told["gpsimd_chain"])
                    G.tensor_copy(lastm[:, NT - 1:NS:NT], cur[0:NS, NT - 1:NS:NT]).then_inc(signal("gpsimd_chain"), 1)
                    pool.wait_ge(sem("gpsimd_chain"), told["gpsimd_chain"])
                G.tensor_tensor(upp[:, l - 1, :], cur, old, ALU.subtract).then_inc(signal("gpsimd_chain"), 1)
                pool.wait_ge(sem("gpsimd_chain"), told["gpsimd_chain"])
                G.tensor_copy(low[:, l - 1, :], upp[:, l - 1, :]).then_inc(signal("gpsimd_chain"), 1)
                pool.wait_ge(sem("gpsimd_chain"), told["gpsimd_chain"])
                G.tensor_tensor(upp[:, l - 1, :], upp[:, l - 1, :], mask4[:, 0, :], ALU.mult).then_inc(signal("gpsimd_chain"), 1)
                pool.wait_ge(sem("gpsimd_chain"), told["gpsimd_chain"])
                G.tensor_tensor(low[:, l - 1, :], low[:, l - 1, :], upp[:, l - 1, :], ALU.subtract).then_inc(signal("gpsimd_chain"), 1)
                pool.wait_ge(sem("gpsimd_chain"), told["gpsimd_chain"])
            G.memset(seg[:, :], 1.0).then_inc(signal("gpsimd_chain"), 1)
            pool.wait_ge(sem("gpsimd_chain"), told["gpsimd_chain"])
            G.memset(seg[:, 0:NPR:P], 0.0).then_inc(signal("gpsimd_chain"), 1)
            pool.wait_ge(sem("gpsimd_chain"), told["gpsimd_chain"])
            G.memset(seg[:, NPR:T:NT], 0.0).then_inc(signal("gpsimd_chain"), 1)
            pool.wait_ge(sem("gpsimd_chain"), told["gpsimd_chain"])
            G.memset(bmask[:, :, :], 1.0).then_inc(signal("gpsimd_chain"), 1)
            pool.wait_ge(sem("gpsimd_chain"), told["gpsimd_chain"])
            select(bmask[:, :, :], [[-NT, NB], [1, NS]], 0, 0)
            select(bmask[:, :, :], [[NT, NB], [-1, NS]], NT - 1, 0)
            G.memset(rmask[:, :], 1.0).then_inc(signal("gpsimd_chain"), 1)
            pool.wait_ge(sem("gpsimd_chain"), told["gpsimd_chain"])
            select(rmask[:, :], [[-NT, NB]], 0, 1)
            select(rmask[:, :], [[NT, NB]], NT - 1, -1)
            G.memset(same[:, 0, 0:1], 1.0).then_inc(signal("masks_ready"), 1)
            pool.wait_ge(sem("masks_ready"), told["masks_ready"])

            def ffn(i):
                lead = FW - 1
                load_hist(A["state_ffn_conv"][i])
                history(lead, 88, i, [(("up", i, p, half), q, half * 2 + q, half * FC + 2 * p + q,
                                       ("value_conv", "gate_conv")[half])
                                      for p in range(FPAIR) for half in range(2) for q in range(2)])

            def load_hist(src):
                sample_free()
                pool.dma_start(sraw[0:src.shape[1] * src.shape[2] // P, :].rearrange("r (b f) -> r b f", b=NB),
                               src.rearrange("b w (c f) -> (w c) b f", f=P)).then_inc(sem("hist_landed"), 16)

            last_use = [None]

            def sample_free():
                if last_use[0]:
                    e, k = last_use[0]
                    pool.wait_ge(filled["scalar"] if e == "turned" else drained["vector"], k + 1)

            def hidden_lo(p):
                for kt in (2 * p, 2 * p + 1):
                    pool.wait_ge(sem("y_hi"), after(pool, "y_hi"))
                    G.tensor_tensor(y_lo(kt), flat("A0", 3)[:, kt * T:(kt + 1) * T], y_hi(kt),
                                    ALU.subtract).then_inc(signal("y_ready"), 1)

            def history(lead, rows, layer, tiles):
                pool.wait_ge(drained["scalar"], mark["hist", layer] + 1)
                last_use[0] = ("turned", mark["hist", layer])
                for n in range(4):
                    ins = G.memset(buf(n, lead)[:, 0:lead], 0.0)
                ins.then_inc(signal("gpsimd_chain"), 1)
                pool.wait_ge(sem("gpsimd_chain"), told["gpsimd_chain"])
                hv = hist[:, :, 0:rows].rearrange("p b (w c) -> p b w c", w=lead)
                lv = last[:, :, 0:rows].rearrange("p b (w c) -> p b w c", w=lead)

                def put(i):
                    _, _, e, c, used = tiles[i]
                    if i >= 4:
                        pool.wait_ge(sem(used), after(pool, used))
                    s = buf(e, lead)[:, lead + NPR:span(lead)].rearrange("p (b t) -> p b t", b=NB)
                    G.tensor_copy(s[:, :, 0:lead], hv[:, :, :, c]).then_inc(signal("hist_in"), 1)
                    pool.wait_ge(sem("hist_in"), told["hist_in"])

                def save(i):
                    key, q, e, c, used = tiles[i]
                    k = mark[key, q] if q is not None else mark[key]
                    pool.wait_ge(drained["scalar"], k + 1)
                    ext = buf(e, lead)
                    s = ext[:, lead + NPR:span(lead)].rearrange("p (b t) -> p b t", b=NB)
                    G.tensor_copy(lv[:, 0, :, c], ext[:, NPR:NPR + lead])
                    G.tensor_copy(lv[:, 1:NB + 1, :, c], s[:, :, NT:NT + lead]).then_inc(signal("saved"), 1)
                    pool.wait_ge(sem("saved"), told["saved"])

                for i in range(4):
                    put(i)
                for i in range(len(tiles)):
                    save(i)
                    if i + 4 < len(tiles):
                        put(i + 4)
                    if layer != "gdn" and i % 4 == 3 and i >= 8:
                        hidden_lo(i // 4 - 2)
                for i in range(len(tiles) - 4, len(tiles)):
                    pool.wait_ge(sem(tiles[i][4]), after(pool, tiles[i][4]))
                G.memset(same[:, 0, 0:1], 0.0).then_inc(signal("last_saved"), 1)
                if layer != "gdn":
                    hidden_lo(FPAIR - 2)
                    hidden_lo(FPAIR - 1)
                pool.wait_ge(sem("last_saved"), told["last_saved"])

            def rwkv(j):
                pool.wait_ge(sem("h_whole"), after(pool, "h_whole"))
                G.tensor_copy(spo_flat[:, 0:8], H[:, :, NPR - 1])
                G.tensor_copy(spo_flat[:, 8:72].rearrange("p (b c) -> p c b", b=NB),
                                         H[:, :, NPR + NT - 1:T:NT]).then_inc(signal("shift_saved"), 1)
                pool.wait_ge(sem("shift_saved"), told["shift_saved"])
                for c in range(KC):
                    sample_free()
                    dst = sraw[0:64, :].rearrange("v (b h k) -> v b h k", b=NB, h=2)
                    for hh in range(2):
                        pool.dma_start(dst[:, :, hh, :], A["state_rwkv_wkv"][j, :, 2 * c + hh].rearrange(
                            "b v k -> v b k")).then_inc(sem("sample_state_in"), 16)
                    last_use[0] = ("turned", mark["sraw", "rwkv", j, c])

            spo_flat = spo[:, :, :].rearrange("p a b -> p (a b)")

            def heads(src, kind, last_slab):
                for h in range(8):
                    if h == 0:
                        sample_free()
                    elif h == 1:
                        pool.wait_ge(*release[last_slab])
                    else:
                        pool.wait_ge(drained["vector"], mark["sraw", kind, h - 2] + 1)
                    pool.dma_start(head_state(h).rearrange("p (b v) -> p b v", b=NB),
                                   src[0, :, h].rearrange("b k v -> k b v")).then_inc(sem(f"head_state_in{h % 2}"), 16)
                last_use[0] = ("updated", mark["sraw", kind, 7])

            rwkv(0)
            ffn(0)
            load_hist(A["state_gdn_conv"][0])
            history(GW - 1, 72, "gdn", [(("gin", n), None, n % 4, n, "gconv") for n in range(GT)])
            heads(A["state_gdn_S"], "gdn", plan.index(("gin", 15)))
            ffn(1)
            heads(A["state_hgrn_S"], "hgrn", plan.index(("hin", 15)))
            ffn(2)
            rwkv(1)
            ffn(3)

        @block.sync
        def _(sync):
            sync.dma_start(flat("A0", 2)[:, 0:2048].rearrange("p (b f) -> p b f", b=2),
                           A["x_prompt"][0].rearrange("(b p) f -> p b f", p=P)).then_inc(sem("x_landed"), 16)
            sync.dma_start(flat("A0", 2)[0:NS, 2048:3072],
                           A["x_sample"].rearrange("b t f -> (b t) f")).then_inc(sem("x_landed"), 16)
            for n, key in enumerate(plan):
                if n >= RING:
                    s, v = release[n - RING]
                    sync.wait_ge(s, v)
                for dst, src in slab_parts(key, ring[:, n % RING, :]):
                    sync.dma_start(dst, src).then_inc(landed[n % RING], 16)


_INS = ['x_prompt', 'x_sample', 'state_rwkv_shift', 'state_rwkv_wkv', 'state_gdn_conv', 'state_gdn_S',
        'state_hgrn_S', 'state_ffn_conv', 'norm_mix_pre', 'norm_mix_post', 'norm_ffn_pre', 'norm_ffn_post',
        'rwkv_mix', 'rwkv_w_rkv', 'rwkv_w0', 'rwkv_w1', 'rwkv_w2', 'rwkv_a0', 'rwkv_a1', 'rwkv_a2',
        'rwkv_v0', 'rwkv_v1', 'rwkv_v2', 'rwkv_g1', 'rwkv_g2', 'rwkv_k_k', 'rwkv_k_a', 'rwkv_r_k',
        'rwkv_lnx_w', 'rwkv_lnx_b', 'rwkv_w_o', 'gdn_w_in', 'gdn_conv_w', 'gdn_a_log', 'gdn_dt_bias',
        'gdn_norm_w', 'gdn_w_o', 'hgrn_w_in', 'hgrn_lb', 'hgrn_norm_w', 'hgrn_w_o',
        'ffn_w_up', 'ffn_conv_w', 'ffn_w_down']
_OUTS = [('y_prompt', (1, 256, 1024)), ('y_sample', (8, 4, 1024)),
         ('prompt_shift', (2, 1, 1024)), ('sample_shift', (2, 8, 1024)),
         ('prompt_wkv', (2, 1, 16, 64, 64)), ('sample_wkv', (2, 8, 16, 64, 64)),
         ('prompt_gdn_conv', (1, 1, 3, 3072)), ('sample_gdn_conv', (1, 8, 3, 3072)),
         ('prompt_gdn_S', (1, 1, 8, 128, 128)), ('sample_gdn_S', (1, 8, 8, 128, 128)),
         ('prompt_hgrn_S', (1, 1, 8, 128, 128)), ('sample_hgrn_S', (1, 8, 8, 128, 128)),
         ('prompt_ffn_conv', (4, 1, 2, 5632)), ('sample_ffn_conv', (4, 8, 2, 5632))]


def kernel(**inputs):
    import numpy as _np
    import concourse.bacc as _bacc
    from concourse.bass_utils import run_bass_kernel_spmd as _run

    nc = _bacc.Bacc("TRN2", target_bir_lowering=False, num_devices=1)
    arrays, ins, outs = {}, {}, {}
    for name in _INS:
        a = _np.ascontiguousarray(inputs[name])
        arrays[f"in_{name}"] = a
        ins[name] = nc.dram_tensor(f"in_{name}", a.shape, mybir.dt.from_np(a.dtype), kind="ExternalInput").ap()
    for name, shape in _OUTS:
        outs[name] = nc.dram_tensor(f"out_{name}", shape, F32, kind="ExternalOutput").ap()
    ins["v_first"] = nc.dram_tensor("v_first", (D, T), F32, kind="Internal").ap()
    build(nc, ins, outs)
    r = _run(nc, [arrays], core_ids=[0])
    return tuple(r.results[0][f"out_{name}"] for name, _ in _OUTS)
```
